# Optimizing a Trainium2 kernel written in Bass

```python
import math
import jax, jax.numpy as jnp
from jax import lax
import numpy as np
import jax
import jax.numpy as jnp

D_MODEL = 1024
BATCH = 1
SEQ = 256
DEPTH = 1

RET_WIDTH = D_MODEL
RET_HEADS = 8
RET_HEAD_DIM = RET_WIDTH // RET_HEADS
RET_CHUNK = 128
ROPE_BASE = 10000.0
LRU_WIDTH = D_MODEL
LRU_BLOCKS = 8
LRU_BLOCK_DIM = LRU_WIDTH // LRU_BLOCKS
LRU_C = 8.0
CONV_WIDTH = 4
MIX_WIDTH = RET_WIDTH + LRU_WIDTH
IN_SPLITS = (RET_WIDTH, 2 * RET_WIDTH, 3 * RET_WIDTH, 4 * RET_WIDTH, 4 * RET_WIDTH + LRU_WIDTH)
IN_WIDTH = 4 * RET_WIDTH + 2 * LRU_WIDTH
NORM_EPS = 1e-6


def rms_norm(x, g):
    x32 = x.astype(jnp.float32)
    y = x32 * lax.rsqrt(jnp.mean(x32 * x32, axis=-1, keepdims=True) + NORM_EPS)
    return (y * g.astype(jnp.float32)).astype(x.dtype)

def rotary(x):
    T, d = x.shape[1], x.shape[-1]
    inv_freq = ROPE_BASE ** (-jnp.arange(0, d, 2, dtype=jnp.float32) / d)
    ang = jnp.arange(T, dtype=jnp.float32)[:, None] * inv_freq[None, :]
    cos = jnp.cos(ang)[None, :, None, :]
    sin = jnp.sin(ang)[None, :, None, :]
    x1, x2 = x[..., : d // 2], x[..., d // 2:]
    return jnp.concatenate([x1 * cos - x2 * sin, x1 * sin + x2 * cos], axis=-1)

def chunkwise_retention(q, k, v):
    B, T, H, d = q.shape
    C = RET_CHUNK
    nc = T // C
    log_g = jnp.log1p(-jnp.exp2(-5.0 - jnp.arange(H, dtype=jnp.float32)))
    idx = jnp.arange(C, dtype=jnp.float32)
    rel = idx[:, None] - idx[None, :]
    decay_mat = jnp.where(rel[None] >= 0,
                          jnp.exp(jnp.maximum(rel, 0.0)[None] * log_g[:, None, None]), 0.0)
    zeta = jnp.exp((C - 1 - idx)[None, :] * log_g[:, None])
    xi = jnp.exp((idx + 1)[None, :] * log_g[:, None])
    chunk_decay = jnp.exp(C * log_g)

    qc = q.reshape(B, nc, C, H, d)
    kc = k.reshape(B, nc, C, H, d)
    vc = v.reshape(B, nc, C, H, d)

    scores = jnp.einsum('bnqhd,bnkhd->bnhqk', qc, kc) * decay_mat[None, None]
    intra = jnp.einsum('bnhqk,bnkhe->bnqhe', scores, vc)

    kv = jnp.einsum('bnkhd,hk,bnkhe->nbhde', kc, zeta, vc)

    def step(state, kv_n):
        new_state = chunk_decay[None, :, None, None] * state + kv_n
        return new_state, state

    _, prev_states = lax.scan(step, jnp.zeros((B, H, d, d), jnp.float32), kv)
    prev_states = jnp.moveaxis(prev_states, 0, 1)
    cross = jnp.einsum('bnqhd,bnhde->bnqhe', qc, prev_states) * xi.T[None, None, :, :, None]
    return (intra + cross).reshape(B, T, H, d)

def group_norm_heads(o):
    mu = jnp.mean(o, axis=-1, keepdims=True)
    var = jnp.mean(jnp.square(o - mu), axis=-1, keepdims=True)
    return (o - mu) * lax.rsqrt(var + NORM_EPS)

def causal_depthwise_conv(x, w, b):
    T = x.shape[1]
    xp = jnp.pad(x, ((0, 0), (CONV_WIDTH - 1, 0), (0, 0)))
    out = b[None, None, :]
    for j in range(CONV_WIDTH):
        out = out + xp[:, j:j + T, :] * w[j][None, None, :]
    return out

def block_diag_linear(x, w, b):
    B, T, _ = x.shape
    xb = x.reshape(B, T, LRU_BLOCKS, LRU_BLOCK_DIM)
    y = jnp.einsum('btni,nio->btno', xb, w) + b[None, None]
    return y.reshape(B, T, LRU_WIDTH)

def rg_lru(x, gate_a_w, gate_a_b, gate_x_w, gate_x_b, lru_lambda):
    r = jax.nn.sigmoid(block_diag_linear(x, gate_a_w, gate_a_b))
    i = jax.nn.sigmoid(block_diag_linear(x, gate_x_w, gate_x_b))
    log_a = -LRU_C * r * jax.nn.softplus(-lru_lambda)[None, None, :]
    a = jnp.exp(log_a)
    mult = jnp.sqrt(jnp.maximum(1.0 - jnp.exp(2.0 * log_a), 0.0))
    b = mult * (i * x)

    def combine(left, right):
        a_l, b_l = left
        a_r, b_r = right
        return a_l * a_r, a_r * b_l + b_r

    _, h = lax.associative_scan(combine, (a, b), axis=1)
    return h

def first_inputs(seed: int = 0) -> dict:
    key = jax.random.key(seed)
    ks = jax.random.split(key, 14)
    f32 = jnp.float32
    x = jax.random.normal(ks[0], (BATCH, SEQ, D_MODEL), f32)
    norm_in_g = 1.0 + 0.05 * jax.random.normal(ks[1], (D_MODEL,), f32)
    w_in = jax.random.normal(ks[2], (D_MODEL, IN_WIDTH), f32) * D_MODEL ** -0.5
    conv_w = jax.random.normal(ks[3], (CONV_WIDTH, LRU_WIDTH), f32) * CONV_WIDTH ** -0.5
    conv_b = 0.01 * jax.random.normal(ks[4], (LRU_WIDTH,), f32)
    gate_a_w = jax.random.normal(ks[5], (LRU_BLOCKS, LRU_BLOCK_DIM, LRU_BLOCK_DIM), f32) * LRU_BLOCK_DIM ** -0.5
    gate_a_b = 0.01 * jax.random.normal(ks[6], (LRU_BLOCKS, LRU_BLOCK_DIM), f32)
    gate_x_w = jax.random.normal(ks[7], (LRU_BLOCKS, LRU_BLOCK_DIM, LRU_BLOCK_DIM), f32) * LRU_BLOCK_DIM ** -0.5
    gate_x_b = 0.01 * jax.random.normal(ks[8], (LRU_BLOCKS, LRU_BLOCK_DIM), f32)
    a_c = jax.random.uniform(ks[9], (LRU_WIDTH,), f32, minval=0.9, maxval=0.999)
    a0 = a_c ** (1.0 / LRU_C)
    lru_lambda = jnp.log(a0) - jnp.log1p(-a0)
    w_out = jax.random.normal(ks[10], (MIX_WIDTH, D_MODEL), f32) * MIX_WIDTH ** -0.5
    norm_out_g = 1.0 + 0.05 * jax.random.normal(ks[11], (D_MODEL,), f32)
    return {"x": x, "norm_in_g": norm_in_g, "w_in": w_in, "conv_w": conv_w, "conv_b": conv_b,
            "gate_a_w": gate_a_w, "gate_a_b": gate_a_b, "gate_x_w": gate_x_w, "gate_x_b": gate_x_b,
            "lru_lambda": lru_lambda, "w_out": w_out, "norm_out_g": norm_out_g}

def first_block(x, norm_in_g, w_in, conv_w, conv_b, gate_a_w, gate_a_b, gate_x_w, gate_x_b,
              lru_lambda, w_out, norm_out_g):
    B, T, _ = x.shape
    f32 = jnp.float32
    h = x
    for _layer in range(DEPTH):
        xn = rms_norm(h, norm_in_g)
        proj = jnp.einsum('btd,de->bte', xn, w_in).astype(f32)
        q, k, v, g_ret, x_lru, g_lru = jnp.split(proj, IN_SPLITS, axis=-1)

        q = rotary(q.reshape(B, T, RET_HEADS, RET_HEAD_DIM))
        k = rotary(k.reshape(B, T, RET_HEADS, RET_HEAD_DIM)) * RET_HEAD_DIM ** -0.5
        v = v.reshape(B, T, RET_HEADS, RET_HEAD_DIM)
        o_ret = group_norm_heads(chunkwise_retention(q, k, v)).reshape(B, T, RET_WIDTH)
        y_ret = o_ret * jax.nn.silu(g_ret)

        xc = causal_depthwise_conv(x_lru, conv_w.astype(f32), conv_b.astype(f32))
        o_lru = rg_lru(xc, gate_a_w.astype(f32), gate_a_b.astype(f32), gate_x_w.astype(f32),
                       gate_x_b.astype(f32), lru_lambda.astype(f32))
        y_lru = o_lru * jax.nn.silu(g_lru)

        mixed = jnp.concatenate([y_ret, y_lru], axis=-1).astype(x.dtype)
        h = h + jnp.einsum('bte,ed->btd', mixed, w_out)
    return rms_norm(h, norm_out_g)


DEPTH_2 = 2

CTX_LEN = 256
GRID_W = 64
N_BRANCH = 3
BRANCH_W = D_MODEL // 2
HEAD_DIM = 64
ML_HEADS = 4
ML_HEAD_DIM = BRANCH_W // ML_HEADS
ML_CHUNK = 64
GQA_HEADS = BRANCH_W // HEAD_DIM
GQA_KV_HEADS = 2
GQA_GROUP = GQA_HEADS // GQA_KV_HEADS
NA_HEADS = BRANCH_W // HEAD_DIM
NA_WIN_R = 8
NA_WIN_C = 16
Q_BLOCK = 128
ROPE_THETA = 10000.0
FFN_DIM = ((8 * D_MODEL // 3 + 127) // 128) * 128
CONV_K = 3
EPS = 1e-6
IN_SIZES = (BRANCH_W, BRANCH_W, BRANCH_W, BRANCH_W, 4 * ML_HEADS,
            GQA_HEADS * HEAD_DIM, GQA_KV_HEADS * HEAD_DIM, GQA_KV_HEADS * HEAD_DIM,
            NA_HEADS * HEAD_DIM, NA_HEADS * HEAD_DIM, NA_HEADS * HEAD_DIM,
            N_BRANCH * D_MODEL)
IN_SPLITS_2 = tuple(sum(IN_SIZES[:i + 1]) for i in range(len(IN_SIZES) - 1))
D_IN = sum(IN_SIZES)


def rms_norm_2(x, g):
    xf = x.astype(jnp.float32)
    y = xf * lax.rsqrt(jnp.mean(xf * xf, axis=-1, keepdims=True) + EPS)
    return (y * g.astype(jnp.float32)).astype(x.dtype)

def modulate(h, shift, scale):
    return h * (1 + scale) + shift

def rope_tables(n_tok, dtype):
    half = HEAD_DIM // 2
    t = jnp.arange(n_tok)
    inv = ROPE_THETA ** (-jnp.arange(0, half, 2, dtype=jnp.float32) / half)
    ang_r = (t // GRID_W).astype(jnp.float32)[:, None] * inv
    ang_c = (t % GRID_W).astype(jnp.float32)[:, None] * inv
    ang = jnp.concatenate([ang_r, ang_r, ang_c, ang_c], axis=-1)
    return jnp.cos(ang).astype(dtype), jnp.sin(ang).astype(dtype)

def apply_rope(x, cos, sin):
    x1, x2, x3, x4 = jnp.split(x, 4, axis=-1)
    rot = jnp.concatenate([-x2, x1, -x4, x3], axis=-1)
    return x * cos[:, None, :] + rot * sin[:, None, :]

def split_heads(z, n_heads):
    B, T, _ = z.shape
    return z.reshape(B, T, n_heads, HEAD_DIM)

def attend(q, k, v):
    s = jnp.einsum('bqkgd,bskd->bkgqs', q, k).astype(jnp.float32) * (HEAD_DIM ** -0.5)
    p = jax.nn.softmax(s, axis=-1).astype(v.dtype)
    return jnp.einsum('bkgqs,bskd->bqkgd', p, v)

def zero_state(B):
    return (jnp.zeros((B, ML_HEADS, ML_HEAD_DIM, ML_HEAD_DIM), jnp.float32),
            jnp.zeros((B, ML_HEADS, ML_HEAD_DIM), jnp.float32),
            jnp.zeros((B, ML_HEADS), jnp.float32))

def mlstm_scan(q, k, v, ig, lf, state):
    B, H, T, d = q.shape
    nc = T // ML_CHUNK

    def to_chunks(a):
        return jnp.moveaxis(a.reshape((B, H, nc, ML_CHUNK) + a.shape[3:]), 2, 0)

    tril = jnp.tril(jnp.ones((ML_CHUNK, ML_CHUNK), dtype=bool))

    def body(carry, xs):
        C, n, m = carry
        qc, kc, vc, igc, lfc = xs
        b = jnp.cumsum(lfc, axis=-1)
        logd = jnp.where(tril, b[..., :, None] - b[..., None, :] + igc[..., None, :], -jnp.inf)
        m_t = jnp.maximum(b + m[..., None], jnp.max(logd, axis=-1))
        dw = jnp.exp(logd - m_t[..., None])
        inter = jnp.exp(b + m[..., None] - m_t)
        s = jnp.einsum('bhtd,bhsd->bhts', qc, kc) * dw
        num = jnp.einsum('bhts,bhse->bhte', s, vc) + inter[..., None] * jnp.einsum('bhtd,bhde->bhte', qc, C)
        den = jnp.sum(s, axis=-1) + inter * jnp.einsum('bhtd,bhd->bht', qc, n)
        h = num / jnp.maximum(jnp.abs(den), jnp.exp(-m_t))[..., None]
        b_last = b[..., -1]
        log_w = b_last[..., None] - b + igc
        m_new = jnp.maximum(b_last + m, jnp.max(log_w, axis=-1))
        w = jnp.exp(log_w - m_new[..., None])
        decay = jnp.exp(b_last + m - m_new)
        C_new = decay[..., None, None] * C + jnp.einsum('bhs,bhsd,bhse->bhde', w, kc, vc)
        n_new = decay[..., None] * n + jnp.einsum('bhs,bhsd->bhd', w, kc)
        return (C_new, n_new, m_new), h

    final, h = lax.scan(body, state, (to_chunks(q), to_chunks(k), to_chunks(v), to_chunks(ig), to_chunks(lf)))
    h = jnp.moveaxis(h, 0, 2).reshape(B, H, T, d)
    return h, final

def mlstm_branch(zq, zk, zv, zo, zgate, gate_bias, g_out, state_f, state_b):
    B, T, _ = zq.shape

    def heads(z):
        return z.reshape(B, T, ML_HEADS, ML_HEAD_DIM).transpose(0, 2, 1, 3)

    q, k, v = heads(zq), heads(zk) * (ML_HEAD_DIM ** -0.5), heads(zv)
    g = (zgate.astype(jnp.float32) + gate_bias.astype(jnp.float32)).reshape(B, T, 4, ML_HEADS).transpose(2, 0, 3, 1)
    i_f, f_f, i_b, f_b = g[0], g[1], g[2], g[3]
    h_f, st_f = mlstm_scan(q, k, v, i_f, jax.nn.log_sigmoid(f_f), state_f)
    rev = lambda a: jnp.flip(a, axis=2)
    h_b, st_b = mlstm_scan(rev(q), rev(k), rev(v), rev(i_b), jax.nn.log_sigmoid(rev(f_b)), state_b)
    h = (h_f + rev(h_b)).transpose(0, 2, 1, 3)
    h = rms_norm_2(h, g_out.reshape(ML_HEADS, ML_HEAD_DIM)).reshape(B, T, BRANCH_W)
    y = h * jax.nn.sigmoid(zo.astype(jnp.float32))
    return y.astype(zq.dtype), st_f, st_b

def gqa_qkv(zq, zk, zv, g_q, g_k):
    B, T, _ = zq.shape
    q = rms_norm_2(zq.reshape(B, T, GQA_HEADS, HEAD_DIM), g_q)
    k = rms_norm_2(zk.reshape(B, T, GQA_KV_HEADS, HEAD_DIM), g_k)
    v = zv.reshape(B, T, GQA_KV_HEADS, HEAD_DIM)
    return q, k, v

def gqa_latent(q, k, v, kc, vc):
    B, T = q.shape[:2]
    k_all = jnp.concatenate([kc, k], axis=1)
    v_all = jnp.concatenate([vc, v], axis=1)
    qb = q.reshape(B, T // Q_BLOCK, Q_BLOCK, GQA_KV_HEADS, GQA_GROUP, HEAD_DIM)
    out = lax.map(lambda qi: attend(qi, k_all, v_all), jnp.moveaxis(qb, 1, 0))
    return jnp.moveaxis(out, 0, 1).reshape(B, T, BRANCH_W)

def na_latent(q, k, v, kc, vc, rpb):
    B, T, H, d = q.shape
    rows = T // GRID_W
    wr = min(NA_WIN_R, rows)
    wc = NA_WIN_C
    qg = q.reshape(B, rows, GRID_W, H, d)
    kg = k.reshape(B, rows, GRID_W, H, d)
    vg = v.reshape(B, rows, GRID_W, H, d)
    cols = jnp.arange(GRID_W)
    c0 = jnp.clip(cols - wc // 2, 0, GRID_W - wc)
    col_idx = c0[:, None] + jnp.arange(wc)[None, :]
    dc = col_idx - cols[:, None] + (NA_WIN_C - 1)
    scale = d ** -0.5

    def row_block(r):
        r0 = jnp.clip(r - wr // 2, 0, rows - wr)
        k_win = lax.dynamic_slice_in_dim(kg, r0, wr, axis=1)[:, :, col_idx]
        v_win = lax.dynamic_slice_in_dim(vg, r0, wr, axis=1)[:, :, col_idx]
        q_row = lax.dynamic_index_in_dim(qg, r, axis=1, keepdims=False)
        dr = r0 + jnp.arange(wr) - r + (NA_WIN_R - 1)
        bias = rpb[:, dr[None, :, None], dc[:, None, :]]
        s_win = jnp.einsum('bqhd,brqjhd->bhqrj', q_row, k_win).astype(jnp.float32) * scale + bias.astype(jnp.float32)
        s_ctx = jnp.einsum('bqhd,bshd->bhqs', q_row, kc).astype(jnp.float32) * scale
        s = jnp.concatenate([s_win.reshape(B, H, GRID_W, wr * wc), s_ctx], axis=-1)
        p = jax.nn.softmax(s, axis=-1).astype(v.dtype)
        p_win = p[..., :wr * wc].reshape(B, H, GRID_W, wr, wc)
        p_ctx = p[..., wr * wc:]
        o = jnp.einsum('bhqrj,brqjhd->bqhd', p_win, v_win) + jnp.einsum('bhqs,bshd->bqhd', p_ctx, vc)
        return o.reshape(B, GRID_W, H * d)

    out = lax.map(row_block, jnp.arange(rows))
    return jnp.moveaxis(out, 0, 1).reshape(B, T, H * d)

def merge_branches(y_ml, y_ga, y_na, zg, w_branch, w_out):
    B, T, _ = zg.shape
    gates = jax.nn.sigmoid(zg.astype(jnp.float32)).astype(zg.dtype).reshape(B, T, N_BRANCH, D_MODEL)
    ys = jnp.stack([y_ml, y_ga, y_na], axis=2)
    proj = jnp.einsum('btnc,ncd->btnd', ys, w_branch)
    return jnp.sum(gates * proj, axis=2) @ w_out

def conv_ffn(h, w_up, conv_w, conv_b, w_down):
    u = h @ w_up
    up = jnp.pad(u, ((0, 0), (1, 1), (0, 0)))
    u = up[:, :-2] * conv_w[0] + up[:, 1:-1] * conv_w[1] + up[:, 2:] * conv_w[2] + conv_b
    a, g = jnp.split(u, 2, axis=-1)
    return (a * jax.nn.silu(g)) @ w_down

def second_inputs(seed: int = 0) -> dict:
    key = jax.random.key(seed)
    ks = jax.random.split(key, 24)
    f32 = jnp.float32

    def nrm(k, shape, s):
        return jax.random.normal(k, shape, f32) * s

    x = nrm(ks[0], (BATCH, SEQ, D_MODEL), 1.0)
    c = nrm(ks[1], (BATCH, D_MODEL), 1.0)
    ctx = nrm(ks[2], (BATCH, CTX_LEN, D_MODEL), 1.0)
    c_ctx = nrm(ks[3], (D_MODEL,), 1.0)
    w_mod = nrm(ks[4], (DEPTH_2, D_MODEL, 6 * D_MODEL), 0.5 * D_MODEL ** -0.5)
    b_mod = nrm(ks[5], (DEPTH_2, 6 * D_MODEL), 0.02)
    g_pre_mix = 1.0 + nrm(ks[6], (DEPTH_2, D_MODEL), 0.05)
    g_post_mix = 1.0 + nrm(ks[7], (DEPTH_2, D_MODEL), 0.05)
    g_pre_ffn = 1.0 + nrm(ks[8], (DEPTH_2, D_MODEL), 0.05)
    g_post_ffn = 1.0 + nrm(ks[9], (DEPTH_2, D_MODEL), 0.05)
    w_in = nrm(ks[10], (DEPTH_2, D_MODEL, D_IN), D_MODEL ** -0.5)
    i_bias = nrm(ks[11], (DEPTH_2, 2, ML_HEADS), 0.1)
    f_bias = jnp.linspace(3.0, 6.0, ML_HEADS, dtype=f32) + nrm(ks[12], (DEPTH_2, 2, ML_HEADS), 0.1)
    b_ml_gates = jnp.stack([i_bias[:, 0], f_bias[:, 0], i_bias[:, 1], f_bias[:, 1]], axis=1).reshape(DEPTH_2, 4 * ML_HEADS)
    g_ml_out = 1.0 + nrm(ks[13], (DEPTH_2, BRANCH_W), 0.05)
    g_q = 1.0 + nrm(ks[14], (DEPTH_2, HEAD_DIM), 0.05)
    g_k = 1.0 + nrm(ks[15], (DEPTH_2, HEAD_DIM), 0.05)
    na_rpb = nrm(ks[16], (DEPTH_2, NA_HEADS, 2 * NA_WIN_R - 1, 2 * NA_WIN_C - 1), 0.1)
    w_branch = nrm(ks[17], (DEPTH_2, N_BRANCH, BRANCH_W, D_MODEL), BRANCH_W ** -0.5)
    w_out = nrm(ks[18], (DEPTH_2, D_MODEL, D_MODEL), D_MODEL ** -0.5)
    w_up = nrm(ks[19], (DEPTH_2, D_MODEL, 2 * FFN_DIM), D_MODEL ** -0.5)
    conv_w = nrm(ks[20], (DEPTH_2, CONV_K, 2 * FFN_DIM), 0.3) + jnp.array([0.0, 1.0, 0.0], f32)[None, :, None]
    conv_b = nrm(ks[21], (DEPTH_2, 2 * FFN_DIM), 0.02)
    w_down = nrm(ks[22], (DEPTH_2, FFN_DIM, D_MODEL), FFN_DIM ** -0.5)
    return {'x': x, 'c': c, 'ctx': ctx, 'c_ctx': c_ctx, 'w_mod': w_mod, 'b_mod': b_mod,
            'g_pre_mix': g_pre_mix, 'g_post_mix': g_post_mix, 'g_pre_ffn': g_pre_ffn, 'g_post_ffn': g_post_ffn,
            'w_in': w_in, 'b_ml_gates': b_ml_gates, 'g_ml_out': g_ml_out, 'g_q': g_q, 'g_k': g_k,
            'na_rpb': na_rpb, 'w_branch': w_branch, 'w_out': w_out, 'w_up': w_up, 'conv_w': conv_w,
            'conv_b': conv_b, 'w_down': w_down}

def second_block(x, c, ctx, c_ctx, w_mod, b_mod, g_pre_mix, g_post_mix, g_pre_ffn, g_post_ffn, w_in, b_ml_gates,
              g_ml_out, g_q, g_k, na_rpb, w_branch, w_out, w_up, conv_w, conv_b, w_down):
    B, T, _ = x.shape
    cos, sin = rope_tables(T, x.dtype)
    xc = ctx
    for l in range(DEPTH_2):
        last = l == DEPTH_2 - 1
        mod = (jax.nn.silu(c) @ w_mod[l] + b_mod[l])[:, None, :]
        mod_c = jax.nn.silu(c_ctx) @ w_mod[l] + b_mod[l]
        sh1, sc1, ga1, sh2, sc2, ga2 = jnp.split(mod, 6, axis=-1)
        csh1, csc1, cga1, csh2, csc2, cga2 = jnp.split(mod_c, 6, axis=-1)

        h = modulate(rms_norm_2(x, g_pre_mix[l]), sh1, sc1)
        hc = modulate(rms_norm_2(xc, g_pre_mix[l]), csh1, csc1)
        (mq, mk, mv, mo, mg, aq, ak, av, nq, nk, nv, zg) = jnp.split(h @ w_in[l], IN_SPLITS_2, axis=-1)
        (cmq, cmk, cmv, cmo, cmg, caq, cak, cav, cnq, cnk, cnv, czg) = jnp.split(hc @ w_in[l], IN_SPLITS_2, axis=-1)

        yc_ml, st_f, st_b = mlstm_branch(cmq, cmk, cmv, cmo, cmg, b_ml_gates[l], g_ml_out[l], zero_state(B), zero_state(B))
        y_ml, _, _ = mlstm_branch(mq, mk, mv, mo, mg, b_ml_gates[l], g_ml_out[l], st_f, st_b)

        qc_a, kc_a, vc_a = gqa_qkv(caq, cak, cav, g_q[l], g_k[l])
        q_a, k_a, v_a = gqa_qkv(aq, ak, av, g_q[l], g_k[l])
        y_ga = gqa_latent(apply_rope(q_a, cos, sin), apply_rope(k_a, cos, sin), v_a, kc_a, vc_a)

        kc_n = split_heads(cnk, NA_HEADS)
        vc_n = split_heads(cnv, NA_HEADS)
        y_na = na_latent(split_heads(nq, NA_HEADS), split_heads(nk, NA_HEADS), split_heads(nv, NA_HEADS), kc_n, vc_n, na_rpb[l])

        o = merge_branches(y_ml, y_ga, y_na, zg, w_branch[l], w_out[l])
        x = x + ga1 * rms_norm_2(o, g_post_mix[l])
        f = conv_ffn(modulate(rms_norm_2(x, g_pre_ffn[l]), sh2, sc2), w_up[l], conv_w[l], conv_b[l], w_down[l])
        x = x + ga2 * rms_norm_2(f, g_post_ffn[l])

        if not last:
            Tc = xc.shape[1]
            yc_ga = attend(qc_a.reshape(B, Tc, GQA_KV_HEADS, GQA_GROUP, HEAD_DIM), kc_a, vc_a).reshape(B, Tc, BRANCH_W)
            yc_na = attend(split_heads(cnq, NA_HEADS)[:, :, :, None, :], kc_n, vc_n).reshape(B, Tc, BRANCH_W)
            oc = merge_branches(yc_ml, yc_ga, yc_na, czg, w_branch[l], w_out[l])
            xc = xc + cga1 * rms_norm_2(oc, g_post_mix[l])
            fc = conv_ffn(modulate(rms_norm_2(xc, g_pre_ffn[l]), csh2, csc2), w_up[l], conv_w[l], conv_b[l], w_down[l])
            xc = xc + cga2 * rms_norm_2(fc, g_post_ffn[l])
    return x


def setup_inputs(seed=0):
    out = dict(first_inputs(seed))
    for name, value in second_inputs(seed + 1).items():
        if name != "x":
            out[name + "_2"] = value
    return out


def reference(
    x, norm_in_g, w_in, conv_w, conv_b, gate_a_w, gate_a_b, gate_x_w, gate_x_b, lru_lambda,
    w_out, norm_out_g, c_2, ctx_2, c_ctx_2, w_mod_2, b_mod_2, g_pre_mix_2, g_post_mix_2,
    g_pre_ffn_2, g_post_ffn_2, w_in_2, b_ml_gates_2, g_ml_out_2, g_q_2, g_k_2, na_rpb_2,
    w_branch_2, w_out_2, w_up_2, conv_w_2, conv_b_2, w_down_2,
):
    x = first_block(
        x, norm_in_g, w_in, conv_w, conv_b, gate_a_w, gate_a_b, gate_x_w, gate_x_b, lru_lambda,
        w_out, norm_out_g,
    )
    return second_block(
        x, c_2, ctx_2, c_ctx_2, w_mod_2, b_mod_2, g_pre_mix_2, g_post_mix_2, g_pre_ffn_2,
        g_post_ffn_2, w_in_2, b_ml_gates_2, g_ml_out_2, g_q_2, g_k_2, na_rpb_2, w_branch_2,
        w_out_2, w_up_2, conv_w_2, conv_b_2, w_down_2,
    )


_drawn_inputs = setup_inputs


def setup_inputs(seed=0):
    import zlib

    import numpy as np

    out = dict(_drawn_inputs(seed))
    spreads = {}
    factors = {'conv_b': 2.829,
     'gate_a_b': 34.225,
     'gate_x_b': 23.445,
     'g_post_ffn_2': 2.762,
     'g_ml_out_2': 3.097,
     'g_q_2': 8.0,
     'g_k_2': 8.0,
     'na_rpb_2': 25.557,
     'conv_b_2': 5.458}
    for name, (base, spread) in spreads.items():
        noise = np.random.default_rng([zlib.crc32(name.encode()), seed]).standard_normal(out[name].shape)
        drawn = base * np.exp(spread * noise) if base else spread * noise
        out[name] = jnp.asarray(drawn.astype(out[name].dtype))
    for name, factor in factors.items():
        out[name] = (out[name] * factor).astype(out[name].dtype)
    return out
```

```python
from contextlib import ExitStack

import numpy as np

import concourse.bass as bass
from concourse import mybir

F32 = mybir.dt.float32
F32R = mybir.dt.float32r
ACT = mybir.ActivationFunctionType
ALU = mybir.AluOpType
AX = mybir.AxisListType

P = 128
D = 1024
KD = D // P
T = 256
NT = T // P
TT = 2 * T
COLS = 512
KP = 2
RING = 4
EPS = 1e-6
HEADS = 8
MH = 4
AH = 8
HD = 64
BW = 512
FF = 2816
FB = FF // P
GRID = 64
WIN = 16
LAYERS = 2
NEG = -1e30
GATE_ROWS = 36

_VEC = [("norm_in_g", 8), ("conv_w", 32), ("conv_b", 8), ("gate_a_b", 8), ("gate_x_b", 8), ("lambda", 8),
        ("c", 8), ("c_ctx", 8)]
for _l in range(LAYERS):
    _VEC += [(f"b_mod{_l}", 48), (f"g_pre_mix{_l}", 8), (f"g_post_mix{_l}", 8), (f"g_pre_ffn{_l}", 8),
             (f"g_post_ffn{_l}", 8), (f"g_ml{_l}", 4), (f"ffn_w{_l}", 3 * 2 * FB), (f"ffn_b{_l}", 2 * FB),
             (f"i_bias{_l}", 1), (f"f_bias{_l}", 1)]
VAT, NV = {}, 0
for _n, _w in _VEC:
    VAT[_n] = NV
    NV += _w

_TAB = [("ident", 128), ("causal", 128), ("anticausal", 128), ("window", 64), ("rope_cos", 2 * HD),
        ("rope_sin", 2 * HD), ("mod_sel", 2)]
TAT, NTAB = {}, 0
for _n, _w in _TAB:
    TAT[_n] = NTAB
    NTAB += _w


def mod_order():
    return range(6 * D // COLS)


def ml_ranges(d, s, first):
    tiles = [t for t in range(first, 4) if ml_allowed(d, s, t)]
    out = []
    for t in tiles:
        if out and out[-1][1] == t * P:
            out[-1] = (out[-1][0], (t + 1) * P)
        else:
            out.append((t * P, (t + 1) * P))
    return out


def ml_allowed(d, s, t):
    if d == 0:
        return t >= s
    return s < 2 <= t or (s // 2 == t // 2 and s >= t)


def stream():
    out = []
    for c in range(12):
        out.append(("w_in", 0, c, KD))
        out.append(("w_mod", 0, c, KD))
    for c in range(2):
        out.append(("w_out", 0, c, 2 * KD))
    for l in range(LAYERS):
        for c in range(9):
            out.append(("w_in_2", l, c, KD))
            if l + 1 < LAYERS:
                out.append(("w_mod", l + 1, c, KD))
        for b in range(3):
            for half in range(2):
                out.append(("w_in_2", l, 9 + 2 * b + half, KD))
                out.append(("w_branch", l, 2 * b + half, BW // P))
                if l + 1 < LAYERS and half == 0:
                    out.append(("w_mod", l + 1, 9 + b, KD))
        for c in range(2):
            out.append(("w_out_2", l, c, KD))
        for c in range(FB // 2):
            out.append(("w_up", l, c, KD))
        for c in range(2):
            out.append(("w_down", l, c, FB))
    return out


NPIECES = sum(k // KP for *_, k in stream())


def build(nc, wst, x_in, ctx_in, vec_in, tab_in, rot_in, decay_in, gatew_in, rowg_in, gout_in, bias_in, out, plan,
          planning):
    es = ExitStack()
    base = (nc.sbuf_base + 31) // 32 * 32
    KB = 1024

    def sb(name, shape, at, dt=F32):
        return nc.alloc_sbuf_tensor_at(name, shape, dt, offset=base + int(at))

    resid = [sb("resid_c", [P, NT, D], 0), sb("resid_x", [P, NT, D], 8 * KB)]
    hT_hi = sb("hT_hi", [P, KD, TT], 16 * KB, F32R)
    hT_lo = sb("hT_lo", [P, KD, TT], 32 * KB, F32R)
    w_raw = sb("w_raw", [P, RING, KP * COLS], 48 * KB)
    w_hi = sb("w_hi", [P, RING, KP, COLS], 64 * KB, F32R)
    w_lo = sb("w_lo", [P, RING, KP, COLS], 80 * KB, F32R)
    R = 96 * KB
    C = 184 * KB
    decay = sb("decay", [P, HEADS, T], 0)
    xT_hi = sb("xT_hi", [P, KD, T], 16 * KB, F32R)
    xT_lo = sb("xT_lo", [P, KD, T], 24 * KB, F32R)
    gatew = sb("gatew", [P, 2, HEADS, P], 32 * KB)
    xc = sb("xc", [P, HEADS, T], 40 * KB)
    mix_hi = sb("mix_hi", [P, 2 * KD, T], R, F32R)
    mix_lo = sb("mix_lo", [P, 2 * KD, T], R + 16 * KB, F32R)
    lru_r = sb("lru_r", [P, HEADS, T], R)
    lru_i = sb("lru_i", [P, HEADS, T], R + 16 * KB)
    qT = sb("qT", [P, HEADS, T], R + 32 * KB)
    kT = sb("kT", [P, HEADS, T], R + 40 * KB)
    v1 = sb("v1", [P, NT, D], R + 48 * KB)
    sg = sb("sg", [P, NT, D], R + 56 * KB)
    xlT = sb("xlT", [P, HEADS, T + 3], R + 64 * KB)
    glT = sb("glT", [P, HEADS, T], R + 73 * KB)
    rot = sb("rot", [P, 2, T], R + 81 * KB)
    rot_tmp = sb("rot_tmp", [P, 2, T], R + 83 * KB)
    sT = sb("sT", [P, 2, 3 * P], R + 85 * KB)
    xn1 = sb("xn1", [P, NT, D], R + 32 * KB)
    xt_tmp = sb("xt_tmp", [P, KD, T], R + 48 * KB)
    onrm = sb("onrm", [P, 2, T], 40 * KB)
    gout_row = sb("gout_row", [P, D], R + 64 * KB)
    S = R
    xn = sb("xn", [P, 2 * NT, D], S)
    o_mix = sb("o_mix", [P, 2 * NT, D], S)
    merged = sb("merged", [P, KD, TT], S)
    aq = sb("aq", [P, 2 * NT, BW], S)
    ak = sb("ak", [P, 2 * NT, P], S + 8 * KB)
    kdup = sb("kdup", [P, 2 * NT, 2 * P], S + 10 * KB)
    ml_w = sb("ml_w", [P, 2, 2 * NT, TT], S)
    yT_hi = sb("yT_hi", [P, 4, TT], R + 16 * KB, F32R)
    yT_lo = sb("yT_lo", [P, 4, TT], R + 24 * KB, F32R)
    mqT = sb("mqT", [P, MH, TT], R + 32 * KB)
    mkT = sb("mkT", [P, MH, TT], R + 40 * KB)
    mv = sb("mv", [P, 2 * NT, MH, P + 1], R + 48 * KB)
    zo = sb("zo", [P, 2 * NT, BW], R + 56.5 * KB)
    nqT = sb("nqT", [P, 4, TT], R + 32 * KB)
    nkT = sb("nkT", [P, 4, TT], R + 40 * KB)
    nv = sb("nv", [P, 2 * NT, BW], R + 48 * KB)
    nbias = sb("nbias", [P, 4, 6, GRID], R + 56.5 * KB)
    av = sb("av", [P, 2 * NT, P], R + 64.5 * KB)
    gqT = sb("gqT", [P, 4, TT], R + 66.5 * KB)
    gkT = sb("gkT", [P, 2, TT], R + 74.5 * KB)
    prob = sb("prob", [P, 2, TT], R + 78.5 * KB)
    probT = sb("probT", [P, 2, TT], R + 82.5 * KB)
    ptmp = sb("ptmp", [P, 4, TT], R + 78.5 * KB)
    fT_hi = sb("fT_hi", [P, FB, TT], R, F32R)
    fT_lo = sb("fT_lo", [P, FB, TT], R + 44 * KB, F32R)
    o_ffn = sb("o_ffn", [P, 2 * NT, D], 16 * KB)
    at = [C]

    def small(name, shape, dt=F32):
        n = 4 * int(np.prod(shape[1:]))
        t = sb(name, shape, at[0], dt)
        at[0] += (n + 31) // 32 * 32
        return t

    vec = small("vec", [P, NV])
    tab = small("tab", [P, NTAB])
    rowg = small("rowg", [P, LAYERS, 2, HD])
    modT = small("modT", [P, LAYERS, 48, 2])
    mrow = small("mrow", [P, 2, COLS])
    mod_c = small("mod_c", [P, KD, 2])
    mod_st = small("mod_st", [P, 4 * KD + P], F32R)
    acol = small("acol", [P, 2 * NT, 2, GATE_ROWS])
    scol = small("scol", [P, KD, 2])
    gcol = small("gcol", [P, KD, 2])
    ones = small("ones", [P, 1])
    zero = small("zero", [P, 1])
    ss = small("ss", [P, 64])
    rs = small("rs", [P, 64])
    att = small("att", [P, 4, 4])
    lam = small("lam", [P, 4, HEADS])
    bnst = small("bnst", [P, 4, 8])
    diag = sb("diag", [P, 2, P], R + 86.5 * KB)
    rows_at = at[0]
    rows = small("rows", [P, 5, TT])
    conv = sb("conv", [P, 4, TT], rows_at)

    ident = tab[:, TAT["ident"]:TAT["ident"] + P]

    def mod_cols_of(j):
        return mod_st[:, 0:4 * KD].rearrange("p (k f) -> p k f", f=4)[:, :, j:j + 2]

    def V(name, i=0, n=1):
        return vec[:, VAT[name] + i:VAT[name] + i + n]

    bank = [es.enter_context(nc.psum_tensor(f"bank{b}", [P, 512], F32)) for b in range(8)]
    bank_filled = [es.enter_context(nc.semaphore(f"bank_filled{b}")) for b in range(8)]
    bank_drained = [es.enter_context(nc.semaphore(f"bank_drained{b}")) for b in range(8)]
    raw_loaded = [es.enter_context(nc.semaphore(f"raw_loaded{s}")) for s in range(RING)]
    hi_ready = es.enter_context(nc.semaphore("hi_ready"))
    lo_ready = es.enter_context(nc.semaphore("lo_ready"))
    piece_used = es.enter_context(nc.semaphore("piece_used"))
    small_loaded = es.enter_context(nc.semaphore("small_loaded"))
    x_loaded = es.enter_context(nc.semaphore("x_loaded"))
    ctx_loaded = es.enter_context(nc.semaphore("ctx_loaded"))
    gout_loaded = es.enter_context(nc.semaphore("gout_loaded"))
    bias_loaded = [es.enter_context(nc.semaphore(f"bias_loaded{s}")) for s in range(4)]
    out_stored = es.enter_context(nc.semaphore("out_stored"))

    class Counter:

        def __init__(self, name):
            self.name, self.sem, self.n = name, es.enter_context(nc.semaphore(name)), 0

        def next(self, key):
            self.n += 1
            plan[(self.name, key)] = (self.name, self.n)
            return self.sem, 1

        def at(self, key):
            assert planning or (self.name, key) in plan, (self.name, key)
            name, n = plan.get((self.name, key), (self.name, 1))
            return by_name[name], n

    acol_ready = Counter("acol_ready")
    ak_raw = Counter("ak_raw")
    ak_ready = Counter("ak_ready")
    aq_ready = Counter("aq_ready")
    bias_used = Counter("bias_used")
    conv_done = Counter("conv_done")
    conv_mid = Counter("conv_mid")
    conv_ready = Counter("conv_ready")
    diag_ready = Counter("diag_ready")
    diag_used = Counter("diag_used")
    exp_done = Counter("exp_done")
    fT_hi_ready = Counter("fT_hi_ready")
    fT_ready = Counter("fT_ready")
    ffn_prod = Counter("ffn_prod")
    ffn_silu = Counter("ffn_silu")
    floor_ready = Counter("floor_ready")
    gate_used = Counter("gate_used")
    h1_ready = Counter("h1_ready")
    hT_hi_ready = Counter("hT_hi_ready")
    hT_ready = Counter("hT_ready")
    hT_tmp_ready = Counter("hT_tmp_ready")
    k_ready = Counter("k_ready")
    lam_ready = Counter("lam_ready")
    lam_scaled = Counter("lam_scaled")
    log_ready = Counter("log_ready")
    lru_a = Counter("lru_a")
    lru_clamped = Counter("lru_clamped")
    lru_e2 = Counter("lru_e2")
    lru_gated = Counter("lru_gated")
    lru_hi = Counter("lru_hi")
    lru_ix = Counter("lru_ix")
    lru_mult = Counter("lru_mult")
    lru_y = Counter("lru_y")
    merged_hi = Counter("merged_hi")
    merged_ready = Counter("merged_ready")
    merged_sum = Counter("merged_sum")
    ml_e = Counter("ml_e")
    ml_exp = Counter("ml_exp")
    ml_root = Counter("ml_root")
    ml_ss = Counter("ml_ss")
    ml_w_ready = Counter("ml_w_ready")
    ml_y = Counter("ml_y")
    mod_c_ready = Counter("mod_c_ready")
    mod_hi_ready = Counter("mod_hi_ready")
    mod_st_ready = Counter("mod_st_ready")
    neg_max = Counter("neg_max")
    post_ms = Counter("post_ms")
    post_root = Counter("post_root")
    post_ss = Counter("post_ss")
    probT_used = Counter("probT_used")
    prob_ready = Counter("prob_ready")
    q_ready = Counter("q_ready")
    qk_root = Counter("qk_root")
    qk_ss = Counter("qk_ss")
    resid_ready = Counter("resid_ready")
    ret_hi = Counter("ret_hi")
    ret_root = Counter("ret_root")
    ret_var = Counter("ret_var")
    ret_y = Counter("ret_y")
    root_ready = Counter("root_ready")
    rows_ready = Counter("rows_ready")
    xT_hi_ready = Counter("xT_hi_ready")
    xT_ready = Counter("xT_ready")
    xn_ready = Counter("xn_ready")
    yT_hi_ready = Counter("yT_hi_ready")
    yT_ready = Counter("yT_ready")
    by_name = {c.name: c.sem for c in (acol_ready, ak_raw, ak_ready, aq_ready, bias_used, conv_done, conv_mid, conv_ready, diag_ready, diag_used, exp_done, fT_hi_ready, fT_ready, ffn_prod, ffn_silu, floor_ready, gate_used, h1_ready, hT_hi_ready, hT_ready, hT_tmp_ready, k_ready, lam_ready, lam_scaled, log_ready, lru_a, lru_clamped, lru_e2, lru_gated, lru_hi, lru_ix, lru_mult, lru_y, merged_hi, merged_ready, merged_sum, ml_e, ml_exp, ml_root, ml_ss, ml_w_ready, ml_y, mod_c_ready, mod_hi_ready, mod_st_ready, neg_max, post_ms, post_root, post_ss, probT_used, prob_ready, q_ready, qk_root, qk_ss, resid_ready, ret_hi, ret_root, ret_var, ret_y, root_ready, rows_ready, xT_hi_ready, xT_ready, xn_ready, yT_hi_ready, yT_ready)}
    by_name.update({f"bank_drained{b}": bank_drained[b] for b in range(8)})
    uses = [0] * 8
    turn = {"rot": 0, "acc": 0}
    pools = {"rot": [0, 1, 2, 3, 4, 5], "acc": [6, 7]}
    fills = [0] * 8
    pieces = [0]

    def take(pe, key, pool="rot"):
        b = pools[pool][turn[pool] % len(pools[pool])]
        turn[pool] += 1
        if uses[b]:
            pe.wait_ge(bank_drained[b], uses[b])
        uses[b] += 1
        plan[("bank", key)] = b, uses[b]
        return bank[b]

    def filled(key):
        b = plan[("bank", key)][0]
        fills[b] += 1
        plan[("filled", key)] = ("bank", b, fills[b], pieces[0])
        return bank_filled[b], 1

    def psum(key):
        return bank[plan.get(("bank", key), (0, 1))[0]]

    def filled_at(key):
        kind, b, n, _ = plan.get(("filled", key), ("bank", 0, 1, 0))
        return bank_filled[b] if kind == "bank" else piece_used, n

    def drained_at(key):
        b, n = plan.get(("bank", key), (0, 1))
        return bank_drained[b], n

    class Steps:

        def __init__(self, name):
            self.chain = Counter(name)
            by_name[name] = self.chain.sem

        def next(self):
            return self.tell(self.chain, self.chain.n)

        def tell(self, counter, key):
            inc = counter.next(key)
            self.at = counter.name, counter.n
            return inc

        def drain(self, key):
            b, n = plan.get(("bank", key), (0, 1))
            self.at = f"bank_drained{b}", n
            return bank_drained[b], 1

        def last(self):
            return by_name[self.at[0]], self.at[1]

        def mark(self, counter, key):
            plan[(counter.name, key)] = self.at

    A, W = Steps("act_chain"), Steps("dve_chain")

    with nc.Block() as block:
        @block.sync
        def _(sp):
            sp.dma_start(vec[:], vec_in).then_inc(small_loaded, 16)
            sp.dma_start(tab[:], tab_in).then_inc(small_loaded, 16)
            sp.dma_start(rowg[:], rowg_in).then_inc(small_loaded, 16)
            sp.dma_start(rot[:], rot_in).then_inc(small_loaded, 16)
            sp.dma_start(gatew[:], gatew_in).then_inc(small_loaded, 16)
            sp.dma_start(decay[:], decay_in).then_inc(small_loaded, 16)
            for s in range(RING):
                sp.dma_start(w_raw[:, s, :], wst[s]).then_inc(raw_loaded[s], 16)
            with sp.Fori(1, NPIECES // RING) as i:
                for s in range(RING):
                    sp.wait_ge(lo_ready, (i - 1) * RING + s + 1)
                    sp.dma_start(w_raw[:, s, :], wst[bass.ds(i * RING + s, 1)].rearrange("a p n -> (a p) n")).then_inc(raw_loaded[s], 16)

        @block.gpsimd
        def _(pool):
            def split_lo(i, s, first):
                pool.wait_ge(hi_ready, i * RING + s + 1)
                if not first:
                    pool.wait_ge(piece_used, (i - 1) * RING + s + 1)
                nc.gpsimd.tensor_tensor(w_lo[:, s].rearrange("p k n -> p (k n)"), w_raw[:, s, :],
                                        w_hi[:, s].rearrange("p k n -> p (k n)").bitcast(F32),
                                        ALU.subtract).then_inc(lo_ready, 1)
            for s in range(RING):
                split_lo(0, s, True)
            with pool.Fori(1, NPIECES // RING) as i:
                for s in range(RING):
                    split_lo(i, s, False)

        @block.tensor
        def _(pe):
            def gemm(banks, tiles, x_hi, x_lo, weights_stationary):
                outs = [(key, take(pe, key), subs) for key, subs in banks]
                for p in range(tiles // KP):
                    s = pieces[0] % RING
                    pe.wait_ge(hi_ready, pieces[0] + 1)
                    pe.wait_ge(lo_ready, pieces[0] + 1)
                    pieces[0] += 1
                    for key, ps, subs in outs:
                        for n, (oc, wc, xcols) in enumerate(subs):
                            for kk in range(KP):
                                k = p * KP + kk
                                for t, (w, x) in enumerate(((w_hi, x_hi), (w_hi, x_lo), (w_lo, x_hi))):
                                    wa, xa = w[:, s, kk, wc], x[:, k, xcols]
                                    st, mv_ = (wa, xa) if weights_stationary else (xa, wa)
                                    mm = pe.matmul(ps[:, oc], st, mv_, start=(k == 0 and t == 0 and n == 0),
                                                   stop=(k == tiles - 1 and t == 2), skip_group_check=True)
                        if p == tiles // KP - 1 and key != outs[-1][0]:
                            mm.then_inc(*filled(key))
                    mm.then_inc(piece_used, 1)
                plan[("filled", outs[-1][0])] = ("piece", 0, pieces[0], pieces[0])

            def blocks_T(key, n, x, xs):
                nt = xs.stop - xs.start
                per = 512 // nt
                return [((key, g), [(slice(j * nt, (j + 1) * nt), slice((g * per + j) * P, (g * per + j + 1) * P), xs)
                                    for j in range(per)]) for g in range(n // per)]

            def gemm_T(key, xs, x_hi, x_lo, n=4, tiles=KD):
                gemm(blocks_T(key, n, None, xs), tiles, x_hi, x_lo, True)

            def gemm_tok(key, tts, x_hi, x_lo, tiles=KD, cols=COLS, at=0):
                per = 512 // cols
                banks = []
                for g in range(len(tts) // per):
                    banks.append(((key, g), [(slice(j * cols, (j + 1) * cols), slice(at, at + cols),
                                              slice(tts[g * per + j] * P, (tts[g * per + j] + 1) * P)) for j in range(per)]))
                gemm(banks, tiles, x_hi, x_lo, False)

            def mod_chunk(l, c):
                key = ("mod", l, c)
                ps = take(pe, key)
                for p in range(KD // KP):
                    s = pieces[0] % RING
                    pe.wait_ge(hi_ready, pieces[0] + 1)
                    pe.wait_ge(lo_ready, pieces[0] + 1)
                    pieces[0] += 1
                    for kk in range(KP):
                        k = p * KP + kk
                        for w in (w_hi, w_lo):
                            mm = pe.matmul(ps[:], mod_st[:, 4 * k:4 * k + P], w[:, s, kk, :],
                                           start=(k == 0 and w is w_hi), stop=(k == KD - 1 and w is w_lo))
                    mm.then_inc(piece_used, 1)
                plan[("filled", key)] = ("piece", 0, pieces[0], pieces[0])

            def mod_turn(l, c):
                pe.wait_ge(*drained_at(("mod", l, c)))
                ps = take(pe, ("modT", l, c))
                for j in range(4):
                    mm = pe.matmul(ps[:, 2 * j:2 * j + 2], mrow[0:4, c % 2, j * P:(j + 1) * P],
                                   tab[0:4, TAT["mod_sel"]:TAT["mod_sel"] + 2], start=True, stop=True)
                mm.then_inc(*filled(("modT", l, c)))

            pe.wait_ge(small_loaded, 96)
            for t in range(NT):
                pe.wait_ge(*xn_ready.at(("b1", t)))
            for g in range(KD // 2):
                ps = take(pe, ("xT", g))
                for j in range(2):
                    for t in range(NT):
                        mm = pe.transpose(ps[:, j * T + t * P:j * T + (t + 1) * P],
                                          xn1[:, t, (2 * g + j) * P:(2 * g + j + 1) * P], ident)
                mm.then_inc(*filled(("xT", g)))
            xs = slice(0, T)
            pe.wait_ge(*xT_ready.at(KD // 2 - 1))
            pe.wait_ge(*mod_st_ready.at(0))

            def gate(n):
                pe.wait_ge(*conv_ready.at(n))
                ps = take(pe, ("gate", n))
                pe.matmul(ps[:, 0:T], gatew[:, 0, n, :], xc[:, n, :], start=True, stop=True)
                mm = pe.matmul(ps[:, T:2 * T], gatew[:, 1, n, :], xc[:, n, :], start=True, stop=True)
                mm.then_inc(*filled(("gate", n)))

            for c in range(12):
                if c < 8:
                    gemm_T(("in", c), xs, xT_hi, xT_lo)
                else:
                    gemm_tok(("in", c), [0, 1], xT_hi, xT_lo)
                mod_chunk(0, c)
                if c:
                    mod_turn(0, c - 1)
                if 4 <= c < 8:
                    gate(2 * (c - 4))
                    gate(2 * (c - 4) + 1)
            mod_turn(0, 11)

            def ret_scores(h):
                pe.wait_ge(*q_ready.at(h // 2))
                pe.wait_ge(*k_ready.at(h // 2))
                ps = take(pe, ("rs", h))
                pe.matmul(ps[:, 0:T], kT[:, h, 0:P], qT[:, h, :], start=True, stop=True)
                mm = pe.matmul(ps[:, T:T + P], kT[:, h, P:T], qT[:, h, P:T], start=True, stop=True)
                mm.then_inc(*filled(("rs", h)))

            def ret_out(h):
                pe.wait_ge(*drained_at(("rs", h)))
                ps = take(pe, ("ro", h))
                e = slice(h * P, (h + 1) * P)
                pe.matmul(ps[:, 0:P], sT[:, h % 2, 0:P], v1[:, 0, e], start=True, stop=True)
                pe.matmul(ps[:, P:T], sT[:, h % 2, P:2 * P], v1[:, 0, e], start=True, stop=False)
                mm = pe.matmul(ps[:, P:T], sT[:, h % 2, 2 * P:3 * P], v1[:, 1, e], start=False, stop=True)
                mm.then_inc(*filled(("ro", h)))

            def ret_turn(h):
                pe.wait_ge(*ret_y.at(h))
                ps = take(pe, ("ry", h))
                for t in range(NT):
                    mm = pe.transpose(ps[:, t * P:(t + 1) * P], onrm[:, h % 2, t * P:(t + 1) * P], ident)
                mm.then_inc(*filled(("ry", h)))

            pe.wait_ge(*drained_at((("in", 9), 1)))
            for h in range(HEADS + 2):
                if h < HEADS:
                    ret_scores(h)
                if 1 <= h <= HEADS:
                    ret_out(h - 1)
                if h >= 2:
                    ret_turn(h - 2)
            pe.wait_ge(*lru_y.at(HEADS - 1))
            pe.wait_ge(*drained_at(("ry", HEADS - 1)))
            for c in range(2):
                gemm_tok(("out", c), [0, 1], mix_hi, mix_lo, tiles=2 * KD)

            def norm_T(l, which, tts):
                for t in tts:
                    pe.wait_ge(*xn_ready.at((l, which, t)))
                for k in range(KD):
                    ps = take(pe, ("nT", l, which, k))
                    for t in tts:
                        mm = pe.transpose(ps[:, t * P:(t + 1) * P], xn[:, t, k * P:(k + 1) * P], ident)
                    mm.then_inc(*filled(("nT", l, which, k)))
                pe.wait_ge(*hT_ready.at((l, which, KD - 1)))

            def spread(l, which, sets):
                for s in sets:
                    for half in range(2):
                        ps = take(pe, ("spread", l, which, s, half))
                        for j in range(4):
                            k = half * 4 + j
                            pe.wait_ge(*diag_ready.at((l, which, s, k)))
                            mm = pe.matmul(ps[:, j * P:(j + 1) * P], ones[:, 0:1].to_broadcast([P, P]),
                                           diag[:, k % 2, :], start=True, stop=True)
                            if j < 3:
                                mm.then_inc(*diag_used.next((l, which, s, k)))
                        mm.then_inc(*filled(("spread", l, which, s, half)))

            for l in range(LAYERS):
                last = l == LAYERS - 1
                every = slice(0, TT)
                tts = list(range(4))
                q_tts = [2, 3] if last else tts
                qs = slice(T, TT) if last else every
                sets = [1] if last else [0, 1]
                q0 = q_tts[0] * P
                norm_T(l, "mix", tts)

                def after(n, l=l, last=last):
                    if not last:
                        mod_chunk(l + 1, n)
                        if n:
                            mod_turn(l + 1, n - 1)

                banks = [((("kv", l), g), [(slice(j * T, (j + 1) * T), slice(0, T),
                                           slice((2 * g + j) * P, (2 * g + j + 1) * P)) for j in range(2)])
                         for g in range(2)]
                outs = [(key, take(pe, key), subs, False) for key, subs in banks]
                gkey = ("gates", l)
                outs.append((gkey, take(pe, gkey), [(every, slice(T, T + P), every)], True))
                for p in range(KD // KP):
                    s = pieces[0] % RING
                    pe.wait_ge(hi_ready, pieces[0] + 1)
                    pe.wait_ge(lo_ready, pieces[0] + 1)
                    pieces[0] += 1
                    for key, ps, subs, stationary in outs:
                        for n, (oc, wc, xcols) in enumerate(subs):
                            for kk in range(KP):
                                k = p * KP + kk
                                for t, (w, x) in enumerate(((w_hi, hT_hi), (w_hi, hT_lo), (w_lo, hT_hi))):
                                    wa, xa = w[:, s, kk, wc], x[:, k, xcols]
                                    st, mv_ = (wa, xa) if stationary else (xa, wa)
                                    mm = pe.matmul(ps[:, oc], st, mv_, start=(k == 0 and t == 0 and n == 0),
                                                   stop=(k == KD - 1 and t == 2), skip_group_check=True)
                        if p == KD // KP - 1 and key != gkey:
                            mm.then_inc(*filled(key))
                    mm.then_inc(piece_used, 1)
                plan[("filled", gkey)] = ("piece", 0, pieces[0], pieces[0])
                after(0)
                gemm_tok(("aq", l), q_tts, hT_hi, hT_lo)
                after(1)
                gemm_T(("mq", l), qs, hT_hi, hT_lo)
                after(2)
                gemm_T(("mk", l), every, hT_hi, hT_lo)
                after(3)
                pe.wait_ge(*rows_ready.at(l))
                ps = take(pe, ("acol", l))
                for t in range(4):
                    for j, r in enumerate((0, 3)):
                        o = (t * 2 + j) * GATE_ROWS
                        mm = pe.transpose(ps[:, o:o + GATE_ROWS], rows[0:GATE_ROWS, r, t * P:(t + 1) * P],
                                          tab[0:GATE_ROWS, TAT["ident"]:TAT["ident"] + GATE_ROWS])
                mm.then_inc(*filled(("acol", l)))
                gemm_tok(("mv", l), tts, hT_hi, hT_lo)
                after(4)
                gemm_tok(("mo", l), q_tts, hT_hi, hT_lo)
                after(5)
                for t in q_tts:
                    pe.wait_ge(*aq_ready.at((l, t)))
                for j in range(4):
                    ps = take(pe, ("gqT", l, j))
                    for t in q_tts:
                        mm = pe.transpose(ps[:, t * P:(t + 1) * P], aq[:, t, j * P:(j + 1) * P], ident)
                    mm.then_inc(*filled(("gqT", l, j)))
                for t in tts:
                    pe.wait_ge(*ak_ready.at((l, t)))
                for j in range(2):
                    ps = take(pe, ("gkT", l, j))
                    for t in tts:
                        mm = pe.transpose(ps[:, t * P:(t + 1) * P], kdup[:, t, j * P:(j + 1) * P], ident)
                    mm.then_inc(*filled(("gkT", l, j)))

                pe.wait_ge(*drained_at((("mv", l), 3)))
                pe.wait_ge(*drained_at(("acol", l)))
                pairs = [(h, d) for h in range(MH) for d in range(2)]

                def ml_scores(i):
                    h, d = pairs[i]
                    ps = take(pe, ("mb", l, h, d))
                    r = 32 * d + h
                    mm = pe.matmul(ps[:, qs], tab[0:GATE_ROWS, TAT["ident"] + r:TAT["ident"] + r + 1].to_broadcast([GATE_ROWS, P]),
                                   rows[0:GATE_ROWS, 4, qs], start=True, stop=True)
                    mm.then_inc(*filled(("mb", l, h, d)))
                    for s in range(4):
                        ps = take(pe, ("ms", l, h, d, s))
                        mm = pe.matmul(ps[:, qs], mkT[:, h, s * P:(s + 1) * P], mqT[:, h, qs], start=True, stop=True)
                        mm.then_inc(*filled(("ms", l, h, d, s)))

                def ml_out(i):
                    h, d = pairs[i]
                    pe.wait_ge(*ml_w_ready.at((l, h, d)))
                    for g in range(len(q_tts) // 2):
                        ps = take(pe, ("mh", l, h, d, g), "acc")
                        for j in range(2):
                            t = q_tts[2 * g + j]
                            keys = [s for s in range(4) if ml_allowed(d, s, t)]
                            for s in keys:
                                mm = pe.matmul(ps[:, j * (P + 1):(j + 1) * (P + 1)], ml_w[:, i % 2, s, t * P:(t + 1) * P],
                                               mv[:, s, h, :], start=(s == keys[0]), stop=(s == keys[-1]))
                        mm.then_inc(*filled(("mh", l, h, d, g)))

                for i in range(len(pairs) + 1):
                    if i < len(pairs):
                        ml_scores(i)
                    if i:
                        ml_out(i - 1)
                pe.wait_ge(*ml_y.at(l))
                for h in range(MH):
                    ps = take(pe, ("my", l, h))
                    for t in q_tts:
                        mm = pe.transpose(ps[:, t * P:(t + 1) * P], ptmp[:, t, h * P:(h + 1) * P], ident)
                    mm.then_inc(*filled(("my", l, h)))

                gemm_T(("nq", l), qs, hT_hi, hT_lo)
                after(6)
                gemm_T(("nk", l), every, hT_hi, hT_lo)
                after(7)
                gemm_tok(("nv", l), tts, hT_hi, hT_lo)
                after(8)

                def merge(b):
                    for half in range(2):
                        gemm_T(("zg", l, b, half), qs, hT_hi, hT_lo)
                        if half == 0:
                            pe.wait_ge(*yT_ready.at((l, b)))
                        gemm_T(("br", l, b, half), qs, yT_hi, yT_lo, tiles=BW // P)
                        if half == 0:
                            after(9 + b)

                def attention(kind, q_, k_, v_):
                    units = [(h, t) for h in range(AH) for t in q_tts]

                    def keys(t):
                        return TT if t >= 2 else T

                    def a_scores(u):
                        h, t = units[u]
                        b0 = (h % 2) * HD
                        ps = take(pe, (kind, "s", l, h, t))
                        kt_ = k_[b0:b0 + HD, h // 4 if kind == "ga" else h // 2, 0:keys(t)]
                        mm = pe.matmul(ps[:, 0:keys(t)], q_[b0:b0 + HD, h // 2, t * P:(t + 1) * P], kt_,
                                       start=True, stop=True)
                        mm.then_inc(*filled((kind, "s", l, h, t)))

                    def a_turn(u):
                        h, t = units[u]
                        pe.wait_ge(*prob_ready.at((kind, l, h, t)))
                        ps = take(pe, (kind, "t", l, h, t))
                        for j in range(keys(t) // P):
                            mm = pe.transpose(ps[:, j * P:(j + 1) * P], prob[:, u % 2, j * P:(j + 1) * P], ident)
                        mm.then_inc(*filled((kind, "t", l, h, t)))

                    def a_out(u):
                        h, t = units[u]
                        pe.wait_ge(*drained_at((kind, "t", l, h, t)))
                        b0 = (h % 2) * HD
                        if h % 2 == 0 and t == q_tts[0]:
                            take(pe, (kind, "o", l, h // 2), "acc")
                        ps = psum((kind, "o", l, h // 2))
                        n = keys(t) // P
                        for j in range(n):
                            vv = v_[:, j, (h // 4) * HD:(h // 4 + 1) * HD] if kind == "ga" else v_[:, j, h * HD:(h + 1) * HD]
                            mm = pe.matmul(ps[b0:b0 + HD, t * P:(t + 1) * P], vv, probT[:, u % 2, j * P:(j + 1) * P],
                                           start=(j == 0), stop=(j == n - 1))
                        if h % 2 == 1 and t == q_tts[-1]:
                            mm.then_inc(*filled((kind, "o", l, h // 2)))
                        else:
                            mm.then_inc(*probT_used.next((kind, l, h, t)))

                    n = len(units)
                    for u in range(n + 2):
                        if u < n:
                            a_scores(u)
                        if 1 <= u <= n:
                            a_turn(u - 1)
                        if u >= 2:
                            a_out(u - 2)

                merge(0)
                pe.wait_ge(*drained_at(("gkT", l, 1)))
                attention("ga", gqT, gkT, av)
                merge(1)
                pe.wait_ge(*drained_at((("nv", l), 3)))
                attention("na", nqT, nkT, nv)
                merge(2)
                if not last:
                    mod_turn(l + 1, 11)
                pe.wait_ge(*merged_ready.at(l))
                for c in range(2):
                    gemm_tok(("wo", l, c), q_tts, hT_hi, hT_lo)
                spread(l, "mix", sets)

                norm_T(l, "ffn", q_tts)
                for c in range(FB // 2):
                    gemm_T(("up", l, c), qs, hT_hi, hT_lo)
                pe.wait_ge(*fT_ready.at((l, FB // 2 - 1)))
                for c in range(2):
                    gemm_tok(("down", l, c), q_tts, fT_hi, fT_lo, tiles=FB)
                spread(l, "ffn", sets)

        hi_done = [0]

        @block.scalar
        def _(act):
            a = nc.scalar

            def split_hi(upto):
                while hi_done[0] < min(upto, NPIECES):
                    p = hi_done[0]
                    act.wait_ge(raw_loaded[p % RING], 16 * (p // RING + 1))
                    if p >= RING:
                        act.wait_ge(piece_used, p - RING + 1)
                    a.activation(w_hi[:, p % RING].rearrange("p k n -> p (k n)"), w_raw[:, p % RING, :],
                                 ACT.Copy).then_inc(hi_ready, 1)
                    hi_done[0] += 1

            def ahead(key):
                split_hi(plan.get(("filled", key), (0, 0, 0, 0))[3] + RING - 1)

            def mod_rows(l, c):
                ahead(("mod", l, c))
                act.wait_ge(*filled_at(("mod", l, c)))
                if c >= 2:
                    act.wait_ge(*filled_at(("modT", l, c - 2)))
                a.activation(mrow[0:4, c % 2, :], psum(("mod", l, c))[0:4, :], ACT.Copy).then_inc(*A.drain(("mod", l, c)))

            act.dma_start(resid[1][:], x_in).then_inc(x_loaded, 16)
            act.wait_ge(x_loaded, 16)
            for t in range(NT):
                a.activation(xn1[:, t, :], resid[1][:, t, :], ACT.Square, accum_out=ss[:, t:t + 1]).then_inc(*A.next())
            act.wait_ge(*A.last())
            a.activation(ss[:, 2:4], ss[:, 0:2], ACT.Copy, scale=1.0 / D, bias=EPS).then_inc(*A.next())
            act.wait_ge(*A.last())
            a.activation(rs[:, 0:2], ss[:, 2:4], ACT.Sqrt).then_inc(*A.tell(root_ready, "b1"))
            act.wait_ge(small_loaded, 96)
            a.activation(mod_c[:, :, 0], V("c", 0, KD), ACT.Silu).then_inc(*A.tell(mod_c_ready, 0))
            a.activation(mod_c[:, :, 1], V("c_ctx", 0, KD), ACT.Silu).then_inc(*A.tell(mod_c_ready, 1))
            act.wait_ge(*A.last())
            a.activation(mod_cols_of(0), mod_c[:], ACT.Copy).then_inc(*A.tell(mod_hi_ready, 0))
            a.activation(lam[:, 0, :], V("lambda", 0, HEADS), ACT.Abs).then_inc(*A.next())
            act.wait_ge(*A.last())
            a.activation(lam[:, 1, :], lam[:, 0, :], ACT.Exp, scale=-1.0).then_inc(*A.next())
            act.wait_ge(*A.last())
            a.activation(lam[:, 2, :], lam[:, 1, :], ACT.Ln, bias=1.0).then_inc(*A.tell(lam_ready, 0))
            for g in range(KD // 2):
                ahead(("xT", g))
                act.wait_ge(*filled_at(("xT", g)))
                ps = psum(("xT", g))
                for j in range(2):
                    k = 2 * g + j
                    a.activation(xt_tmp[:, k, :], ps[:, j * T:(j + 1) * T], ACT.Copy, scale=V("norm_in_g", k))\
                        .then_inc(*(A.drain(("xT", g)) if j else A.next()))
                act.wait_ge(*A.last())
                a.activation(xT_hi[:, 2 * g:2 * g + 2, :], xt_tmp[:, 2 * g:2 * g + 2, :], ACT.Copy)\
                    .then_inc(*A.tell(xT_hi_ready, g))
            for c in range(12):
                for g in range(2):
                    key = (("in", c), g)
                    if c < 2:
                        ahead(key)
                        act.wait_ge(*filled_at(key))
                        b = 4 * c + 2 * g
                        a.activation(xlT[:, b:b + 2, 3:T + 3], psum(key)[:].rearrange("p (b t) -> p b t", b=2), ACT.Copy)\
                            .then_inc(*A.drain(key))
                    elif c < 4:
                        ahead(key)
                        act.wait_ge(*filled_at(key))
                        b = 4 * (c - 2) + 2 * g
                        a.activation(glT[:, b:b + 2, :], psum(key)[:].rearrange("p (b t) -> p b t", b=2), ACT.Silu)\
                            .then_inc(*A.drain(key))
                    elif c >= 8:
                        ahead(key)
                        act.wait_ge(*filled_at(key))
                        dst = v1 if c < 10 else sg
                        a.activation(dst[:, g, (c % 2) * COLS:(c % 2 + 1) * COLS], psum(key)[:],
                                     ACT.Copy if c < 10 else ACT.Silu).then_inc(*A.drain(key))
                mod_rows(0, c)
                if 4 <= c < 8:
                    for n in (2 * (c - 4), 2 * (c - 4) + 1):
                        key = ("gate", n)
                        ahead(key)
                        act.wait_ge(*filled_at(key))
                        a.activation(lru_r[:, n, :], psum(key)[:, 0:T], ACT.Sigmoid, bias=V("gate_a_b", n))\
                            .then_inc(*A.next())
                        a.activation(lru_i[:, n, :], psum(key)[:, T:2 * T], ACT.Sigmoid, bias=V("gate_x_b", n))\
                            .then_inc(*A.drain(key))
            ahead(("modT", 0, 11))
            act.wait_ge(*lam_scaled.at(0))
            for n in range(HEADS):
                act.wait_ge(*lru_ix.at(n))
                act.wait_ge(*A.last())
                a.activation(xc[:, n, :], lru_r[:, n, :], ACT.Exp, scale=lam[:, 1, n:n + 1]).then_inc(*A.tell(lru_e2, n))
            act.wait_ge(*A.last())
            for n in range(HEADS):
                a.activation(lru_r[:, n, :], lru_r[:, n, :], ACT.Exp, scale=lam[:, 0, n:n + 1]).then_inc(*A.tell(lru_a, n))
            act.wait_ge(*lru_clamped.at(0))
            a.activation(xc[:], xc[:], ACT.Sqrt, bias=1.0).then_inc(*A.tell(lru_mult, 0))
            for n in range(HEADS):
                act.wait_ge(*lru_gated.at(n))
                a.activation(mix_hi[:, HEADS + n, :], xc[:, n, :], ACT.Copy).then_inc(*A.tell(lru_hi, n))
            for h in range(HEADS):
                ahead(("ro", h))
                act.wait_ge(*ret_var.at(h))
                a.activation(bnst[:, h % 2, 6:8], bnst[:, 2 + h % 2, 0:2], ACT.Sqrt).then_inc(*A.tell(ret_root, h))
                if h >= 1:
                    ahead(("ry", h - 1))
                    act.wait_ge(*filled_at(("ry", h - 1)))
                    a.activation(mix_hi[:, h - 1, :], psum(("ry", h - 1))[:, 0:T], ACT.Copy)\
                        .then_inc(*A.tell(ret_hi, h - 1))
            ahead(("ry", HEADS - 1))
            act.wait_ge(*filled_at(("ry", HEADS - 1)))
            a.activation(mix_hi[:, HEADS - 1, :], psum(("ry", HEADS - 1))[:, 0:T], ACT.Copy)\
                .then_inc(*A.tell(ret_hi, HEADS - 1))
            act.dma_start(gout_row[:], gout_in).then_inc(gout_loaded, 16)
            act.dma_start(resid[0][:], ctx_in).then_inc(ctx_loaded, 16)
            ahead((("out", 1), 1))
            for t in range(NT):
                act.wait_ge(*h1_ready.at(t))
                a.activation(v1[:, t, :], resid[1][:, t, :], ACT.Square, accum_out=ss[:, t:t + 1]).then_inc(*A.next())
            act.wait_ge(*A.last())
            a.activation(ss[:, 2:4], ss[:, 0:2], ACT.Copy, scale=1.0 / D, bias=EPS).then_inc(*A.next())
            act.wait_ge(*A.last())
            a.activation(rs[:, 0:2], ss[:, 2:4], ACT.Sqrt).then_inc(*A.tell(root_ready, "b1out"))

            def norm(l, which, tts):
                for t in tts:
                    if (l, which) == (0, "mix") and t < 2:
                        act.wait_ge(ctx_loaded, 16)
                    else:
                        act.wait_ge(*resid_ready.at((l, which, t)))
                    a.activation(xn[:, t, :], resid[t // 2][:, t % 2, :], ACT.Square, accum_out=ss[:, t:t + 1])\
                        .then_inc(*A.next())
                act.wait_ge(*A.last())
                lo_, hi_ = tts[0], tts[-1] + 1
                a.activation(ss[:, 4 + lo_:4 + hi_], ss[:, lo_:hi_], ACT.Copy, scale=1.0 / D, bias=EPS).then_inc(*A.next())
                act.wait_ge(*A.last())
                a.activation(rs[:, lo_:hi_], ss[:, 4 + lo_:4 + hi_], ACT.Sqrt).then_inc(*A.tell(root_ready, (l, which)))
                t0 = tts[0] * P
                for k in range(KD):
                    ahead(("nT", l, which, k))
                    act.wait_ge(*hT_tmp_ready.at((l, which, k)))
                    a.activation(hT_hi[:, k, t0:TT], ptmp[:, k % 4, t0:TT], ACT.Copy)\
                        .then_inc(*A.tell(hT_hi_ready, (l, which, k)))

            def post(l, which, tts, o):
                for t in tts:
                    for half in range(2):
                        a.activation(conv[:, half, :], o[:, t, half * COLS:(half + 1) * COLS], ACT.Square,
                                     accum_out=ss[:, 8 + 2 * t + half:9 + 2 * t + half]).then_inc(*A.next())
                    act.wait_ge(*A.last())
                lo_, hi_ = tts[0], tts[-1] + 1
                a.activation(ss[:, 16 + 2 * lo_:16 + 2 * hi_], ss[:, 8 + 2 * lo_:8 + 2 * hi_], ACT.Copy, scale=1.0 / D,
                             bias=EPS / 2).then_inc(*A.tell(post_ss, (l, which)))
                act.wait_ge(*post_ms.at((l, which)))
                a.activation(rs[:, 4 + lo_:4 + hi_], ss[:, 24 + lo_:24 + hi_], ACT.Sqrt)\
                    .then_inc(*A.tell(post_root, (l, which)))

            for l in range(LAYERS):
                last = l == LAYERS - 1
                tts = list(range(4))
                q_tts = [2, 3] if last else tts
                t0 = q_tts[0] * P
                nq = TT - t0
                norm(l, "mix", tts)

                def evac_T(key, dst, n=4, func=ACT.Copy, scale=1.0, nt=None):
                    nt = nt or nq
                    per = 512 // nt
                    for g in range(n // per):
                        ahead((key, g))
                        act.wait_ge(*filled_at((key, g)))
                        a.activation(dst[:, g * per:(g + 1) * per, TT - nt:TT],
                                     psum((key, g))[:].rearrange("p (b t) -> p b t", b=per), func, scale=scale)\
                            .then_inc(*A.drain((key, g)))

                def mod(n, l=l, last=last):
                    if not last:
                        mod_rows(l + 1, n)

                for g in range(2):
                    key = (("kv", l), g)
                    ahead(key)
                    act.wait_ge(*filled_at(key))
                    v_ = psum(key)[:].rearrange("p (t c) -> p t c", t=2)
                    a.activation(ak[:, 2 * g:2 * g + 2, :], v_[:, :, 0:P], ACT.Copy).then_inc(*A.tell(ak_raw, (l, g)))
                    a.activation(av[:, 2 * g:2 * g + 2, :], v_[:, :, P:T], ACT.Copy).then_inc(*A.drain(key))
                key = ("gates", l)
                ahead(key)
                act.wait_ge(*filled_at(key))
                G = GATE_ROWS
                a.activation(rows[0:G, 0, :], psum(key)[0:G, :], ACT.Identity, bias=V(f"i_bias{l}")[0:G])\
                    .then_inc(*A.next())
                a.activation(rows[0:G, 1, :], psum(key)[64:64 + G, :], ACT.Identity, bias=V(f"f_bias{l}")[0:G])\
                    .then_inc(*A.drain(key))
                act.wait_ge(*A.last())
                a.activation(rows[0:G, 2, :], rows[0:G, 1, :], ACT.Abs).then_inc(*A.next())
                act.wait_ge(*A.last())
                a.activation(rows[0:G, 3, :], rows[0:G, 2, :], ACT.Exp, scale=-1.0).then_inc(*A.next())
                act.wait_ge(*A.last())
                a.activation(rows[0:G, 2, :], rows[0:G, 3, :], ACT.Ln, bias=1.0).then_inc(*A.tell(log_ready, l))
                mod(0)
                for g, t in enumerate(q_tts):
                    key = (("aq", l), g)
                    ahead(key)
                    act.wait_ge(*filled_at(key))
                    a.activation(aq[:, t, :], psum(key)[:], ACT.Copy).then_inc(*A.drain(key))
                mod(1)
                evac_T(("mq", l), mqT)
                mod(2)
                act.wait_ge(*qk_ss.at(l))
                a.activation(rs[:, 8:48], ss[:, 8:48], ACT.Sqrt).then_inc(*A.tell(qk_root, l))
                evac_T(("mk", l), mkT, scale=float(P) ** -0.5, nt=TT)
                mod(3)
                for t in tts:
                    key = (("mv", l), t)
                    ahead(key)
                    act.wait_ge(*filled_at(key))
                    a.activation(mv[:, t, :, 0:P], psum(key)[:].rearrange("p (h e) -> p h e", h=MH), ACT.Copy)\
                        .then_inc(*A.drain(key))
                mod(4)
                for g, t in enumerate(q_tts):
                    key = (("mo", l), g)
                    ahead(key)
                    act.wait_ge(*filled_at(key))
                    a.activation(zo[:, t, :], psum(key)[:], ACT.Sigmoid).then_inc(*A.drain(key))
                mod(5)
                for j in range(4):
                    key = ("gqT", l, j)
                    ahead(key)
                    act.wait_ge(*filled_at(key))
                    a.activation(gqT[:, j, t0:TT], psum(key)[:, t0:TT], ACT.Copy).then_inc(*A.drain(key))
                for j in range(2):
                    key = ("gkT", l, j)
                    ahead(key)
                    act.wait_ge(*filled_at(key))
                    a.activation(gkT[:, j, :], psum(key)[:], ACT.Copy).then_inc(*A.drain(key))
                act.wait_ge(*acol_ready.at(l))
                a.activation(acol[:, :, 1, :], acol[:, :, 1, :], ACT.Exp).then_inc(*A.tell(floor_ready, l))
                for i in range(2 * MH):
                    h, d = i // 2, i % 2
                    for s in range(4):
                        rng = ml_ranges(d, s, t0 // P)
                        ahead(("ms", l, h, d, s))
                        act.wait_ge(*ml_e.at((l, h, d, s)))
                        for n, (u0, u1) in enumerate(rng):
                            a.activation(ml_w[:, i % 2, s, u0:u1], ml_w[:, i % 2, s, u0:u1], ACT.Exp)\
                                .then_inc(*(A.tell(ml_exp, (l, h, d, s)) if n == len(rng) - 1 else A.next()))
                act.wait_ge(*ml_ss.at(l))
                a.activation(rs[:, 8:24], ss[:, 8:24], ACT.Sqrt).then_inc(*A.tell(ml_root, l))
                for h in range(MH):
                    key = ("my", l, h)
                    ahead(key)
                    act.wait_ge(*filled_at(key))
                    a.activation(yT_hi[:, h, t0:TT], psum(key)[:, t0:TT], ACT.Copy, scale=V(f"g_ml{l}", h))\
                        .then_inc(*A.tell(yT_hi_ready, (l, 0, h)))
                evac_T(("nq", l), nqT, scale=float(HD) ** -0.5)
                mod(6)
                evac_T(("nk", l), nkT, nt=TT)
                mod(7)
                for t in tts:
                    key = (("nv", l), t)
                    ahead(key)
                    act.wait_ge(*filled_at(key))
                    a.activation(nv[:, t, :], psum(key)[:], ACT.Copy).then_inc(*A.drain(key))
                mod(8)

                def merge(b):
                    per = 512 // nq
                    for half in range(2):
                        for g in range(4 // per):
                            key = (("zg", l, b, half), g)
                            ahead(key)
                            act.wait_ge(*filled_at(key))
                            if half:
                                act.wait_ge(*gate_used.at((l, b, 0, 4 // per - 1)))
                            a.activation(ptmp[:, g * per:(g + 1) * per, t0:TT],
                                         psum(key)[:].rearrange("p (b t) -> p b t", b=per), ACT.Sigmoid)\
                                .then_inc(*A.drain(key))
                        if half == 0:
                            mod(9 + b)

                def attention(kind, b):
                    units = [(h, t) for h in range(AH) for t in q_tts]
                    for u in range(len(units) + 1):
                        if u < len(units):
                            h, t = units[u]
                            nk = TT if t >= 2 else T
                            ahead((kind, "s", l, h, t))
                            if kind == "na" and t == q_tts[0] and 1 <= h <= 4:
                                act.wait_ge(*bias_used.at((l, h - 1)))
                                load_bias(h + 3)
                            act.wait_ge(*neg_max.at((kind, l, h, t)))
                            a.activation(prob[:, u % 2, 0:nk], psum((kind, "s", l, h, t))[:, 0:nk], ACT.Exp,
                                         bias=att[:, u % 4, 0:1], accum_out=att[:, u % 4, 1:2])\
                                .then_inc(*A.drain((kind, "s", l, h, t)))
                            A.mark(exp_done, (kind, l, h, t))
                        if u:
                            h, t = units[u - 1]
                            if u >= 3:
                                hh, tt_ = units[u - 3]
                                if hh % 2 == 1 and tt_ == q_tts[-1]:
                                    act.wait_ge(*filled_at((kind, "o", l, hh // 2)))
                                else:
                                    act.wait_ge(*probT_used.at((kind, l, hh, tt_)))
                            nk = TT if t >= 2 else T
                            ahead((kind, "t", l, h, t))
                            act.wait_ge(*filled_at((kind, "t", l, h, t)))
                            a.activation(probT[:, (u - 1) % 2, 0:nk], psum((kind, "t", l, h, t))[:, 0:nk], ACT.Copy)\
                                .then_inc(*A.drain((kind, "t", l, h, t)))
                        if u >= 3:
                            hh, tt_ = units[u - 3]
                            if hh % 2 == 1 and tt_ == q_tts[-1]:
                                hi_of_pair(kind, b, hh // 2)
                    hi_of_pair(kind, b, AH // 2 - 1)

                def hi_of_pair(kind, b, j):
                    key = (kind, "o", l, j)
                    ahead(key)
                    act.wait_ge(*filled_at(key))
                    a.activation(yT_hi[:, j, t0:TT], psum(key)[:, t0:TT], ACT.Copy)\
                        .then_inc(*A.tell(yT_hi_ready, (l, b, j)))

                def load_bias(h):
                    act.dma_start(nbias[:, h % 4, :, :], bias_in[l, h]).then_inc(bias_loaded[h % 4], 16)

                for h in range(4):
                    load_bias(h)
                merge(0)
                attention("ga", 1)
                merge(1)
                attention("na", 2)
                merge(2)
                for k in range(KD):
                    ahead((("br", l, 2, 1), 4 // (512 // nq) - 1))
                    act.wait_ge(*merged_sum.at((l, k // 4)))
                    a.activation(hT_hi[:, k, t0:TT], merged[:, k, t0:TT], ACT.Copy).then_inc(*A.tell(merged_hi, (l, k)))
                for c in range(2):
                    for g, t in enumerate(q_tts):
                        key = (("wo", l, c), g)
                        ahead(key)
                        act.wait_ge(*filled_at(key))
                        if c == 0 and g == 0:
                            act.wait_ge(*merged_ready.at(l))
                        a.activation(o_mix[:, t, c * COLS:(c + 1) * COLS], psum(key)[:], ACT.Copy).then_inc(*A.drain(key))
                act.wait_ge(*A.last())
                post(l, "mix", q_tts, o_mix)
                norm(l, "ffn", q_tts)
                per = 512 // nq
                for c in range(FB // 2):
                    for g in range(4 // per):
                        key = (("up", l, c), g)
                        ahead(key)
                        act.wait_ge(*filled_at(key))
                        if c and g == 0:
                            act.wait_ge(*fT_ready.at((l, c - 1)))
                        for j in range(per):
                            q = g * per + j
                            blk = 2 * c + q % 2 + (FB if q >= 2 else 0)
                            a.activation(conv[:, q, t0:TT], psum(key)[:, j * nq:(j + 1) * nq], ACT.Identity,
                                         scale=V(f"ffn_w{l}", 2 * FB + blk), bias=V(f"ffn_b{l}", blk))\
                                .then_inc(*(A.tell(conv_mid, (l, c, g)) if j == per - 1 else A.next()))
                    act.wait_ge(*conv_done.at((l, c)))
                    a.activation(conv[:, 2:4, t0:TT], conv[:, 2:4, t0:TT], ACT.Silu).then_inc(*A.tell(ffn_silu, (l, c)))
                    act.wait_ge(*ffn_prod.at((l, c)))
                    a.activation(fT_hi[:, 2 * c:2 * c + 2, t0:TT], conv[:, 0:2, t0:TT], ACT.Copy)\
                        .then_inc(*A.tell(fT_hi_ready, (l, c)))
                for c in range(2):
                    for g, t in enumerate(q_tts):
                        key = (("down", l, c), g)
                        ahead(key)
                        act.wait_ge(*filled_at(key))
                        a.activation(o_ffn[:, t, c * COLS:(c + 1) * COLS], psum(key)[:], ACT.Copy).then_inc(*A.drain(key))
                act.wait_ge(*A.last())
                act.wait_ge(*fT_ready.at((l, FB // 2 - 1)))
                post(l, "ffn", q_tts, o_ffn)
            for t in range(2, 4):
                act.wait_ge(*resid_ready.at((LAYERS, "mix", t)))
            act.dma_start(out, resid[1][:]).then_inc(out_stored, 16)
            act.wait_ge(out_stored, 16)

        @block.vector
        def _(dve):
            v = nc.vector

            v.memset(ones[:], 1.0).then_inc(*W.next())
            v.memset(zero[:], 0.0).then_inc(*W.next())
            v.memset(mod_st[:, 4 * KD:].bitcast(F32), 0.0).then_inc(*W.next())
            v.memset(xlT[:, :, 0:3], 0.0).then_inc(*W.next())
            dve.wait_ge(*root_ready.at("b1"))
            v.reciprocal(rs[:, 2:4], rs[:, 0:2]).then_inc(*W.next())
            dve.wait_ge(*W.last())
            for t in range(NT):
                v.tensor_scalar(xn1[:, t, :], resid[1][:, t, :], rs[:, 2 + t:3 + t], None, ALU.mult)\
                    .then_inc(*W.tell(xn_ready, ("b1", t)))
            dve.wait_ge(*mod_hi_ready.at(0))
            v.tensor_tensor(mod_cols_of(2), mod_c[:], mod_cols_of(0).bitcast(F32), ALU.subtract)\
                .then_inc(*W.tell(mod_st_ready, 0))
            dve.wait_ge(*lam_ready.at(0))
            v.tensor_scalar(lam[:, 3, :], V("lambda", 0, HEADS), -1.0, 0.0, ALU.mult, ALU.max).then_inc(*W.next())
            dve.wait_ge(*W.last())
            v.tensor_tensor(lam[:, 2, :], lam[:, 2, :], lam[:, 3, :], ALU.add).then_inc(*W.next())
            dve.wait_ge(*W.last())
            v.tensor_scalar(lam[:, 0, :], lam[:, 2, :], -8.0, None, ALU.mult).then_inc(*W.next())
            v.tensor_scalar(lam[:, 1, :], lam[:, 2, :], -16.0, None, ALU.mult).then_inc(*W.tell(lam_scaled, 0))
            for g in range(KD // 2):
                dve.wait_ge(*xT_hi_ready.at(g))
                v.tensor_tensor(xT_lo[:, 2 * g:2 * g + 2, :], xt_tmp[:, 2 * g:2 * g + 2, :],
                                xT_hi[:, 2 * g:2 * g + 2, :].bitcast(F32), ALU.subtract).then_inc(*W.tell(xT_ready, g))

            def mod_cols(l, c):
                key = ("modT", l, c)
                dve.wait_ge(*filled_at(key))
                b = V(f"b_mod{l}", 4 * c, 4).unsqueeze(2).to_broadcast([P, 4, 2])
                v.tensor_tensor(modT[:, l, 4 * c:4 * c + 4, :], psum(key)[:, 0:8].rearrange("p (j s) -> p j s", s=2), b,
                                ALU.add).then_inc(*W.drain(key))

            def rotate(key, dst, b, rotated, tk):
                dve.wait_ge(*filled_at(key))
                ps = psum(key)[:].rearrange("p (b t) -> p b t", b=2)
                for half in (slice(0, HD), slice(HD, P)):
                    src = slice(HD, P) if half.start == 0 else slice(0, HD)
                    v.tensor_tensor(rot_tmp[half, :, :], ps[src, :, :], rot[src, 1, :].unsqueeze(1).to_broadcast([HD, 2, T]), ALU.mult)\
                        .then_inc(*W.next())
                v.tensor_tensor(dst[:, b:b + 2, :], ps, rot[:, 0, :].unsqueeze(1).to_broadcast([P, 2, T]), ALU.mult)\
                    .then_inc(*W.drain(key))
                dve.wait_ge(*W.last())
                v.tensor_tensor(dst[:, b:b + 2, :], dst[:, b:b + 2, :], rot_tmp[:], ALU.add).then_inc(*W.tell(rotated, tk))
                dve.wait_ge(*W.last())

            def conv_block(n):
                dve.wait_ge(*drained_at((("in", n // 4), n % 4 // 2)))
                v.tensor_scalar(xc[:, n, :], xlT[:, n, 0:T], V("conv_w", n), V("conv_b", n), ALU.mult, ALU.add)\
                    .then_inc(*W.next())
                for j in range(1, 4):
                    dve.wait_ge(*W.last())
                    v.scalar_tensor_tensor(xc[:, n, :], xlT[:, n, j:j + T], V("conv_w", 8 * j + n), xc[:, n, :],
                                           ALU.mult, ALU.add).then_inc(*(W.tell(conv_ready, n) if j == 3 else W.next()))

            for c in range(12):
                if c in (1, 2):
                    for n in range(4 * (c - 1), 4 * c):
                        conv_block(n)
                if 4 <= c < 8:
                    for g in range(2):
                        i = (c - 4) * 2 + g
                        if c < 6:
                            rotate((("in", c), g), qT, 2 * i, q_ready, i)
                        else:
                            rotate((("in", c), g), kT, 2 * (i - 4), k_ready, i - 4)
                if c:
                    mod_cols(0, c - 1)
                if 4 <= c < 8:
                    for n in (2 * (c - 4), 2 * (c - 4) + 1):
                        dve.wait_ge(*drained_at(("gate", n)))
                        v.tensor_tensor(lru_i[:, n, :], lru_i[:, n, :], xc[:, n, :], ALU.mult).then_inc(*W.tell(lru_ix, n))
            mod_cols(0, 11)
            dve.wait_ge(*lru_e2.at(HEADS - 1))
            v.tensor_scalar(xc[:], xc[:], 1.0, -1.0, ALU.min, ALU.mult).then_inc(*W.tell(lru_clamped, 0))
            dve.wait_ge(*lru_a.at(HEADS - 1))
            dve.wait_ge(*lru_mult.at(0))
            v.tensor_tensor(lru_i[:], lru_i[:], xc[:], ALU.mult).then_inc(*W.next())
            dve.wait_ge(*W.last())
            for n in range(HEADS):
                v.tensor_tensor_scan(xc[:, n, :], lru_r[:, n, :], lru_i[:, n, :], 0.0, ALU.mult, ALU.add)\
                    .then_inc(*W.next())
            dve.wait_ge(*W.last())
            for n in range(HEADS):
                v.tensor_tensor(xc[:, n, :], xc[:, n, :], glT[:, n, :], ALU.mult).then_inc(*W.tell(lru_gated, n))
            for n in range(HEADS):
                dve.wait_ge(*lru_hi.at(n))
                v.tensor_tensor(mix_lo[:, HEADS + n, :], xc[:, n, :], mix_hi[:, HEADS + n, :].bitcast(F32), ALU.subtract)\
                    .then_inc(*W.tell(lru_y, n))

            def ret_decay(h):
                key = ("rs", h)
                dve.wait_ge(*filled_at(key))
                ps = psum(key)
                if h >= 2:
                    dve.wait_ge(*filled_at(("ro", h - 2)))
                v.tensor_tensor(sT[:, h % 2, 0:T], ps[:, 0:T], decay[:, h, :], ALU.mult).then_inc(*W.next())
                v.tensor_tensor(sT[:, h % 2, T:T + P], ps[:, T:T + P], decay[:, h, 0:P], ALU.mult).then_inc(*W.drain(key))

            def ret_stats(h):
                key = ("ro", h)
                dve.wait_ge(*filled_at(key))
                ps = psum(key)
                for t in range(NT):
                    v.bn_stats(bnst[:, t, 0:6], ps[:, t * P:(t + 1) * P]).then_inc(*W.next())
                    dve.wait_ge(*W.last())
                    v.bn_aggr(att[:, 2 * (h % 2) + t, 0:2], bnst[:, t, 0:6]).then_inc(*W.next())
                dve.wait_ge(*W.last())
                return key

            def ret_norm(h):
                key = ret_stats(h)
                ps = psum(key)
                mu = att[:, 2 * (h % 2):2 * (h % 2) + 2, 0]
                v.tensor_scalar(bnst[:, 2 + h % 2, 0:2], att[:, 2 * (h % 2):2 * (h % 2) + 2, 1], EPS, None, ALU.add)\
                    .then_inc(*W.tell(ret_var, h))
                dve.wait_ge(*ret_root.at(h))
                v.reciprocal(bnst[:, 2 + h % 2, 2:4], bnst[:, h % 2, 6:8]).then_inc(*W.next())
                dve.wait_ge(*W.last())
                if h >= 2:
                    dve.wait_ge(*filled_at(("ry", h - 2)))
                for t in range(NT):
                    v.tensor_scalar(onrm[:, h % 2, t * P:(t + 1) * P], ps[:, t * P:(t + 1) * P], mu[:, t:t + 1],
                                    bnst[:, 2 + h % 2, 2 + t:3 + t], ALU.subtract, ALU.mult)\
                        .then_inc(*(W.drain(key) if t == NT - 1 else W.next()))
                dve.wait_ge(*W.last())
                o = onrm[:, h % 2, :].rearrange("p (t c) -> p t c", t=NT)
                v.tensor_tensor(o, o, sg[:, :, h * P:(h + 1) * P], ALU.mult).then_inc(*W.tell(ret_y, h))

            def ret_lo(h):
                dve.wait_ge(*ret_hi.at(h))
                v.tensor_tensor(mix_lo[:, h, :], psum(("ry", h))[:, 0:T], mix_hi[:, h, :].bitcast(F32), ALU.subtract)\
                    .then_inc(*W.drain(("ry", h)))

            for c in (10, 11):
                for g in range(2):
                    dve.wait_ge(*drained_at((("in", c), g)))
            ret_decay(0)
            for h in range(HEADS):
                if h + 1 < HEADS:
                    ret_decay(h + 1)
                ret_norm(h)
                if h >= 1:
                    ret_lo(h - 1)
            ret_lo(HEADS - 1)
            for c in range(2):
                for t in range(NT):
                    key = (("out", c), t)
                    dve.wait_ge(*filled_at(key))
                    r = resid[1][:, t, c * COLS:(c + 1) * COLS]
                    v.tensor_tensor(r, psum(key)[:], r, ALU.add).then_inc(*W.drain(key))
            dve.wait_ge(*W.last())
            for t in range(NT):
                W.mark(h1_ready, t)
            dve.wait_ge(*root_ready.at("b1out"))
            v.reciprocal(rs[:, 2:4], rs[:, 0:2]).then_inc(*W.next())
            dve.wait_ge(*W.last())
            dve.wait_ge(gout_loaded, 16)
            dve.wait_ge(ctx_loaded, 16)
            for t in range(NT):
                v.scalar_tensor_tensor(resid[1][:, t, :], resid[1][:, t, :], rs[:, 2 + t:3 + t], gout_row[:],
                                       ALU.mult, ALU.mult).then_inc(*W.tell(resid_ready, (0, "mix", 2 + t)))

            def norm(l, which, tts):
                o = 0 if which == "mix" else 3
                pre = V(f"g_pre_{which}{l}", 0, KD)
                dve.wait_ge(*W.last())
                v.tensor_scalar(scol[:], modT[:, l, 8 * (o + 1):8 * (o + 2), :], 1.0, None, ALU.add).then_inc(*W.next())
                dve.wait_ge(*W.last())
                v.tensor_tensor(scol[:], scol[:], pre.unsqueeze(2).to_broadcast([P, KD, 2]), ALU.mult).then_inc(*W.next())
                g_post = V(f"g_post_{which}{l}", 0, KD)
                v.tensor_tensor(gcol[:], modT[:, l, 8 * (o + 2):8 * (o + 3), :], g_post.unsqueeze(2).to_broadcast([P, KD, 2]),
                                ALU.mult).then_inc(*W.next())
                dve.wait_ge(*root_ready.at((l, which)))
                lo_, hi_ = tts[0], tts[-1] + 1
                v.reciprocal(ss[:, lo_:hi_], rs[:, lo_:hi_]).then_inc(*W.next())
                dve.wait_ge(*W.last())
                for t in tts:
                    v.tensor_scalar(xn[:, t, :], resid[t // 2][:, t % 2, :], ss[:, t:t + 1], None, ALU.mult)\
                        .then_inc(*W.tell(xn_ready, (l, which, t)))
                t0 = tts[0] * P
                for k in range(KD):
                    key = ("nT", l, which, k)
                    dve.wait_ge(*filled_at(key))
                    if k >= 4:
                        dve.wait_ge(*hT_hi_ready.at((l, which, k - 4)))
                    parts = [(1, T, TT)] if t0 else [(0, 0, T), (1, T, TT)]
                    for n, (s, u0, u1) in enumerate(parts):
                        v.tensor_scalar(ptmp[:, k % 4, u0:u1], psum(key)[:, u0:u1], scol[:, k, 1 - s:2 - s],
                                        modT[:, l, 8 * o + k, 1 - s:2 - s], ALU.mult, ALU.add)\
                            .then_inc(*(W.drain(key) if n == len(parts) - 1 else W.next()))
                    W.mark(hT_tmp_ready, (l, which, k))
                    if k:
                        norm_lo(l, which, k - 1, t0)
                norm_lo(l, which, KD - 1, t0)

            def norm_lo(l, which, k, t0):
                dve.wait_ge(*hT_hi_ready.at((l, which, k)))
                v.tensor_tensor(hT_lo[:, k, t0:TT], ptmp[:, k % 4, t0:TT], hT_hi[:, k, t0:TT].bitcast(F32), ALU.subtract)\
                    .then_inc(*W.tell(hT_ready, (l, which, k)))

            def post(l, which, tts, o, nxt):
                dve.wait_ge(*post_ss.at((l, which)))
                lo_, hi_ = tts[0], tts[-1] + 1
                pr = ss[:, 16 + 2 * lo_:16 + 2 * hi_].rearrange("p (t h) -> p t h", h=2)
                v.tensor_tensor(ss[:, 24 + lo_:24 + hi_], pr[:, :, 0], pr[:, :, 1], ALU.add)\
                    .then_inc(*W.tell(post_ms, (l, which)))
                sets = [1] if lo_ >= 2 else [0, 1]
                n = 0
                first = True
                for s in sets:
                    for k in range(KD):
                        if n >= 2:
                            ps_, pk = (s, k - 2) if k >= 2 else (s - 1, KD - 2 + k)
                            if pk % 4 == 3:
                                dve.wait_ge(*filled_at(("spread", l, which, ps_, pk // 4)))
                            else:
                                dve.wait_ge(*diag_used.at((l, which, ps_, pk)))
                        v.tensor_scalar(diag[:, k % 2, :], ident, gcol[:, k, 1 - s:2 - s], None, ALU.mult)\
                            .then_inc(*W.tell(diag_ready, (l, which, s, k)))
                        n += 1
                    if first:
                        dve.wait_ge(*post_root.at((l, which)))
                        v.reciprocal(rs[:, lo_:hi_], rs[:, 4 + lo_:4 + hi_]).then_inc(*W.next())
                        dve.wait_ge(*W.last())
                        first = False
                    for half in range(2):
                        key = ("spread", l, which, s, half)
                        dve.wait_ge(*filled_at(key))
                        cols = slice(half * COLS, (half + 1) * COLS)
                        for j in range(NT):
                            t = 2 * s + j
                            v.scalar_tensor_tensor(o[:, t, cols], o[:, t, cols], rs[:, t:t + 1], psum(key)[:],
                                                   ALU.mult, ALU.mult)\
                                .then_inc(*(W.drain(key) if j == NT - 1 else W.next()))
                    dve.wait_ge(*W.last())
                    for j in range(NT):
                        t = 2 * s + j
                        v.tensor_tensor(resid[s][:, j, :], resid[s][:, j, :], o[:, t, :], ALU.add)\
                            .then_inc(*W.tell(resid_ready, (*nxt, t)))
                dve.wait_ge(*W.last())

            for l in range(LAYERS):
                last = l == LAYERS - 1
                tts = list(range(4))
                q_tts = [2, 3] if last else tts
                t0 = q_tts[0] * P
                nq = TT - t0
                sets = [1] if last else [0, 1]
                G = GATE_ROWS
                norm(l, "mix", tts)

                def mod(n, l=l, last=last):
                    if not last and n:
                        mod_cols(l + 1, n - 1)

                dve.wait_ge(*log_ready.at(l))
                fwd, bwd = slice(0, MH), slice(32, 32 + MH)
                v.scalar_tensor_tensor(rows[0:G, 2, :], rows[0:G, 1, :], 0.0, rows[0:G, 2, :], ALU.min, ALU.subtract)\
                    .then_inc(*W.next())
                v.memset(rows[0:G, 3, :], 0.0).then_inc(*W.next())
                v.memset(rows[0:G, 4, :], 0.0).then_inc(*W.next())
                dve.wait_ge(*W.last())

                def zeros(p, n):
                    return zero[p, 0:1].to_broadcast([MH, n])

                v.tensor_tensor_scan(rows[fwd, 3, :], rows[fwd, 2, :], zeros(fwd, TT), 0.0, ALU.add, ALU.add)\
                    .then_inc(*W.next())
                v.tensor_tensor_scan(rows[bwd, 3, 0:T][:, ::-1], rows[bwd, 2, 0:T][:, ::-1], zeros(bwd, T), 0.0, ALU.add, ALU.add)\
                    .then_inc(*W.next())
                dve.wait_ge(*W.last())
                v.tensor_tensor_scan(rows[bwd, 3, T:TT][:, ::-1], rows[bwd, 2, T:TT][:, ::-1], zeros(bwd, T),
                                     rows[bwd, 3, 0:1], ALU.add, ALU.add).then_inc(*W.next())
                dve.wait_ge(*W.last())
                v.tensor_tensor(rows[0:G, 0, :], rows[0:G, 0, :], rows[0:G, 3, :], ALU.subtract).then_inc(*W.next())
                dve.wait_ge(*W.last())
                v.tensor_tensor_scan(rows[fwd, 4, :], rows[fwd, 0, :], rows[fwd, 0, :], 0.0, ALU.max, ALU.max)\
                    .then_inc(*W.next())
                v.tensor_tensor_scan(rows[bwd, 4, 0:T][:, ::-1], rows[bwd, 0, 0:T][:, ::-1], rows[bwd, 0, 0:T][:, ::-1], 0.0,
                                     ALU.max, ALU.max).then_inc(*W.next())
                dve.wait_ge(*W.last())
                v.tensor_tensor_scan(rows[bwd, 4, T:TT][:, ::-1], rows[bwd, 0, T:TT][:, ::-1], rows[bwd, 0, T:TT][:, ::-1],
                                     rows[bwd, 4, 0:1], ALU.max, ALU.max).then_inc(*W.next())
                dve.wait_ge(*W.last())
                v.scalar_tensor_tensor(rows[0:G, 3, :], rows[0:G, 3, :], -1.0, rows[0:G, 4, :], ALU.mult, ALU.subtract)\
                    .then_inc(*W.next())
                dve.wait_ge(*W.last())
                v.tensor_scalar(rows[0:G, 4, :], rows[0:G, 4, :], -1.0, None, ALU.mult).then_inc(*W.tell(rows_ready, l))
                mod(0)

                sq = probT[:, 0, :]
                if last:
                    v.memset(ss[:, 8:24], 1.0).then_inc(*W.next())
                for g, t in enumerate(q_tts):
                    dve.wait_ge(*drained_at((("aq", l), g)))
                    dve.wait_ge(*W.last())
                    v.tensor_tensor(sq, aq[:, t, :], aq[:, t, :], ALU.mult).then_inc(*W.next())
                    dve.wait_ge(*W.last())
                    v.tensor_reduce(ss[:, 8 + 8 * t:16 + 8 * t], sq.rearrange("p (h d) -> p h d", h=AH), AX.X, ALU.add)\
                        .then_inc(*W.next())
                mod(1)
                sq = probT[:, 1, :]
                dve.wait_ge(*ak_raw.at((l, 1)))
                v.tensor_tensor(sq, ak[:].rearrange("p t c -> p (t c)"), ak[:].rearrange("p t c -> p (t c)"), ALU.mult)\
                    .then_inc(*W.next())
                dve.wait_ge(*W.last())
                v.tensor_reduce(ss[:, 40:48], sq.rearrange("p (h d) -> p h d", h=AH), AX.X, ALU.add).then_inc(*W.next())
                dve.wait_ge(*W.last())
                v.tensor_scalar(ss[:, 8:48], ss[:, 8:48], 1.0 / HD, EPS, ALU.mult, ALU.add).then_inc(*W.tell(qk_ss, l))
                mod(2)
                dve.wait_ge(*qk_root.at(l))
                v.reciprocal(ss[:, 8:48], rs[:, 8:48]).then_inc(*W.next())
                dve.wait_ge(*W.last())
                v.tensor_scalar(ss[:, 8:40], ss[:, 8:40], float(HD) ** -0.5, None, ALU.mult).then_inc(*W.next())
                dve.wait_ge(*W.last())

                def heads(a_, n, t, col, which):
                    av_ = a_.rearrange("p (h d) -> p h d", h=n)
                    v.tensor_tensor(av_, av_, ss[:, col:col + n].unsqueeze(2).to_broadcast([P, n, HD]), ALU.mult)\
                        .then_inc(*W.next())
                    dve.wait_ge(*W.last())
                    v.tensor_tensor(av_, av_, rowg[:, l, which, :].unsqueeze(1).to_broadcast([P, n, HD]), ALU.mult)\
                        .then_inc(*W.next())
                    dve.wait_ge(*W.last())
                    if t >= 2:
                        c_ = tab[:, TAT["rope_cos"] + (t - 2) * HD:TAT["rope_cos"] + (t - 1) * HD]
                        s_ = tab[:, TAT["rope_sin"] + (t - 2) * HD:TAT["rope_sin"] + (t - 1) * HD]
                        tmp = probT[:, 0, 0:n * HD]
                        q5 = a_.rearrange("p (h a b i) -> p h a b i", h=n, a=2, b=2)
                        t5 = tmp.rearrange("p (h a b i) -> p h a b i", h=n, a=2, b=2)
                        s5 = s_.rearrange("p (a b i) -> p a b i", a=2, b=2)
                        for b in range(2):
                            v.tensor_tensor(t5[:, :, :, b, :], q5[:, :, :, 1 - b, :],
                                            s5[:, :, b, :].unsqueeze(1).to_broadcast([P, n, 2, 16]), ALU.mult)\
                                .then_inc(*W.next())
                        dve.wait_ge(*W.last())
                        v.tensor_tensor(av_, av_, c_.unsqueeze(1).to_broadcast([P, n, HD]), ALU.mult).then_inc(*W.next())
                        dve.wait_ge(*W.last())
                        v.tensor_tensor(a_, a_, tmp, ALU.add).then_inc(*W.next())
                        dve.wait_ge(*W.last())

                for t in q_tts:
                    heads(aq[:, t, :], AH, t, 8 + 8 * t, 0)
                    W.mark(aq_ready, (l, t))
                for t in tts:
                    heads(ak[:, t, :], 2, t, 40 + 2 * t, 1)
                    kd = kdup[:, t, :].rearrange("p (h r d) -> p h r d", h=2, r=2)
                    src = ak[:, t, :].rearrange("p (h d) -> p h d", h=2)
                    v.tensor_copy(kd[:, :, 0, :], src).then_inc(*W.next())
                    v.tensor_copy(kd[:, :, 1, :], src).then_inc(*W.tell(ak_ready, (l, t)))
                mod(3)
                key = ("acol", l)
                dve.wait_ge(*filled_at(key))
                v.tensor_copy(acol[:].rearrange("p t j g -> p (t j g)"), psum(key)[:, 0:8 * G]).then_inc(*W.drain(key))
                W.mark(acol_ready, l)
                v.memset(mv[:, :, :, P:P + 1], 1.0).then_inc(*W.next())
                mod(4)
                mod(5)

                dve.wait_ge(*floor_ready.at(l))
                dve.wait_ge(*drained_at(("gkT", l, 1)))
                pairs = [(h, d) for h in range(MH) for d in range(2)]

                def ml_exponents(i):
                    h, d = pairs[i]
                    mask = tab[:, TAT["causal"]:TAT["causal"] + P] if d == 0 else tab[:, TAT["anticausal"]:TAT["anticausal"] + P]
                    key = ("mb", l, h, d)
                    dve.wait_ge(*filled_at(key))
                    if i >= 2:
                        hh, dd = pairs[i - 2]
                        dve.wait_ge(*filled_at(("mh", l, hh, dd, len(q_tts) // 2 - 1)))
                    for s in range(4):
                        ac = acol[:, s, 0, 32 * d + h:32 * d + h + 1]
                        ops = []
                        for u0, u1 in ml_ranges(d, s, t0 // P):
                            if u0 <= s * P < u1:
                                ops += [(u0, s * P, 0), (s * P, (s + 1) * P, 1), ((s + 1) * P, u1, 0)]
                            else:
                                ops.append((u0, u1, 0))
                        ops = [o for o in ops if o[1] > o[0]]
                        for n, (u0, u1, masked) in enumerate(ops):
                            fin = n == len(ops) - 1
                            src, dst = psum(key)[:, u0:u1], ml_w[:, i % 2, s, u0:u1]
                            ins = (v.scalar_tensor_tensor(dst, src, ac, mask, ALU.add, ALU.min) if masked
                                   else v.tensor_scalar(dst, src, ac, 0.0, ALU.add, ALU.min))
                            ins.then_inc(*(W.drain(key) if fin and s == 3 else W.next()))
                        W.mark(ml_e, (l, h, d, s))

                def ml_weights(i):
                    h, d = pairs[i]
                    for s in range(4):
                        key = ("ms", l, h, d, s)
                        dve.wait_ge(*filled_at(key))
                        dve.wait_ge(*ml_exp.at((l, h, d, s)))
                        rng = ml_ranges(d, s, t0 // P)
                        for n, (u0, u1) in enumerate(rng):
                            w_ = ml_w[:, i % 2, s, u0:u1]
                            v.tensor_tensor(w_, psum(key)[:, u0:u1], w_, ALU.mult)\
                                .then_inc(*(W.drain(key) if n == len(rng) - 1 else W.next()))
                    W.mark(ml_w_ready, (l, h, d))

                def ml_norm(i):
                    h, d = pairs[i]
                    for g in range(len(q_tts) // 2):
                        key = ("mh", l, h, d, g)
                        dve.wait_ge(*filled_at(key))
                        ps = psum(key)[:, 0:2 * (P + 1)].rearrange("p (t e) -> p t e", t=2)
                        ta = q_tts[2 * g]
                        v.tensor_copy(rs[:, 48:50], ps[:, :, P]).then_inc(*W.next())
                        dve.wait_ge(*W.last())
                        v.scalar_tensor_tensor(rs[:, 52:54], rs[:, 48:50], -1.0, rs[:, 48:50], ALU.mult, ALU.max)\
                            .then_inc(*W.next())
                        dve.wait_ge(*W.last())
                        v.tensor_tensor(rs[:, 52:54], rs[:, 52:54], acol[:, ta:ta + 2, 1, 32 * d + h], ALU.max)\
                            .then_inc(*W.next())
                        dve.wait_ge(*W.last())
                        v.reciprocal(rs[:, 50:52], rs[:, 52:54]).then_inc(*W.next())
                        dve.wait_ge(*W.last())
                        for j in range(2):
                            dst = ptmp[:, ta + j, h * P:(h + 1) * P]
                            if d == 0:
                                v.tensor_scalar(dst, ps[:, j, 0:P], rs[:, 50 + j:51 + j], None, ALU.mult)\
                                    .then_inc(*(W.drain(key) if j == 1 else W.next()))
                            else:
                                v.scalar_tensor_tensor(dst, ps[:, j, 0:P], rs[:, 50 + j:51 + j], dst, ALU.mult, ALU.add)\
                                    .then_inc(*(W.drain(key) if j == 1 else W.next()))
                        dve.wait_ge(*W.last())

                for i in range(len(pairs) + 1):
                    if i < len(pairs):
                        ml_exponents(i)
                        ml_weights(i)
                    if i:
                        ml_norm(i - 1)
                if last:
                    v.memset(ss[:, 8:16], 1.0).then_inc(*W.next())
                for t in q_tts:
                    for h in range(MH):
                        y = ptmp[:, t, h * P:(h + 1) * P]
                        v.tensor_tensor(ml_w[:, 0, 0, h * P:(h + 1) * P], y, y, ALU.mult).then_inc(*W.next())
                    dve.wait_ge(*W.last())
                    v.tensor_reduce(ss[:, 8 + 4 * t:12 + 4 * t], ml_w[:, 0, 0, :].rearrange("p (h e) -> p h e", h=MH),
                                    AX.X, ALU.add).then_inc(*W.next())
                    dve.wait_ge(*W.last())
                v.tensor_scalar(ss[:, 8:24], ss[:, 8:24], 1.0 / P, EPS, ALU.mult, ALU.add).then_inc(*W.tell(ml_ss, l))
                dve.wait_ge(*ml_root.at(l))
                v.reciprocal(ss[:, 8:24], rs[:, 8:24]).then_inc(*W.next())
                dve.wait_ge(*W.last())
                for t in q_tts:
                    for h in range(MH):
                        y = ptmp[:, t, h * P:(h + 1) * P]
                        v.scalar_tensor_tensor(y, y, ss[:, 8 + 4 * t + h:9 + 4 * t + h], zo[:, t, h * P:(h + 1) * P],
                                               ALU.mult, ALU.mult).then_inc(*W.next())
                W.mark(ml_y, l)
                for h in range(MH):
                    key = ("my", l, h)
                    dve.wait_ge(*yT_hi_ready.at((l, 0, h)))
                    v.scalar_tensor_tensor(yT_lo[:, h, t0:TT], psum(key)[:, t0:TT], V(f"g_ml{l}", h),
                                           yT_hi[:, h, t0:TT].bitcast(F32), ALU.mult, ALU.subtract).then_inc(*W.drain(key))
                W.mark(yT_ready, (l, 0))
                mod(6)
                mod(7)
                mod(8)

                def merge(b):
                    per = 512 // nq
                    for half in range(2):
                        for g in range(4 // per):
                            key = (("br", l, b, half), g)
                            dve.wait_ge(*filled_at(key))
                            dve.wait_ge(*drained_at((("zg", l, b, half), g)))
                            gate = ptmp[:, g * per:(g + 1) * per, t0:TT]
                            ps = psum(key)[:].rearrange("p (b t) -> p b t", b=per)
                            m = merged[:, 4 * half + g * per:4 * half + (g + 1) * per, t0:TT]
                            if b == 0:
                                v.tensor_tensor(m, ps, gate, ALU.mult).then_inc(*W.drain(key))
                                W.mark(gate_used, (l, b, half, g))
                            else:
                                v.tensor_tensor(gate, ps, gate, ALU.mult).then_inc(*W.drain(key))
                                dve.wait_ge(*W.last())
                                v.tensor_tensor(m, m, gate, ALU.add).then_inc(*W.tell(gate_used, (l, b, half, g)))
                        if half == 0:
                            mod(9 + b)
                        if b == 2:
                            W.mark(merged_sum, (l, half))

                def load_bias(h):
                    s = h % 4
                    dve.wait_ge(bias_loaded[s], 16 * (2 * l + h // 4 + 1))
                    b_ = nbias[:, s, :, :]
                    v.tensor_tensor(b_, b_, tab[:, TAT["window"]:TAT["window"] + GRID].unsqueeze(1).to_broadcast([P, 6, GRID]),
                                    ALU.add).then_inc(*W.next())

                def attention(kind, b):
                    units = [(h, t) for h in range(AH) for t in q_tts]
                    n_ = len(units)
                    if kind == "na":
                        for h in range(AH // 2):
                            load_bias(h)
                        dve.wait_ge(*W.last())

                    def maxes(u):
                        h, t = units[u]
                        nk = TT if t >= 2 else T
                        key = (kind, "s", l, h, t)
                        ps = psum(key)
                        dve.wait_ge(*filled_at(key))
                        if kind == "na" and t >= 2:
                            if h >= 4 and t == 2:
                                load_bias(h)
                                dve.wait_ge(*W.last())
                            j0 = 2 if t == 2 else 0
                            sc = ps[:, T:TT].rearrange("p (r c) -> p r c", c=GRID)
                            v.tensor_tensor(sc, sc, nbias[:, h % 4, j0:j0 + 4, :], ALU.add)\
                                .then_inc(*(W.tell(bias_used, (l, h)) if t == 3 else W.next()))
                            dve.wait_ge(*W.last())
                        v.tensor_reduce(att[:, u % 4, 0:1], ps[:, 0:nk], AX.X, ALU.max, negate=True)\
                            .then_inc(*W.tell(neg_max, (kind, l, h, t)))

                    def normalise(u):
                        h, t = units[u]
                        nk = TT if t >= 2 else T
                        dve.wait_ge(*exp_done.at((kind, l, h, t)))
                        v.reciprocal(att[:, u % 4, 3:4], att[:, u % 4, 1:2]).then_inc(*W.next())
                        dve.wait_ge(*W.last())
                        v.tensor_scalar(prob[:, u % 2, 0:nk], prob[:, u % 2, 0:nk], att[:, u % 4, 3:4], None, ALU.mult)\
                            .then_inc(*W.tell(prob_ready, (kind, l, h, t)))

                    def lo_of_pair(j):
                        key = (kind, "o", l, j)
                        dve.wait_ge(*yT_hi_ready.at((l, b, j)))
                        v.tensor_tensor(yT_lo[:, j, t0:TT], psum(key)[:, t0:TT], yT_hi[:, j, t0:TT].bitcast(F32),
                                        ALU.subtract).then_inc(*W.drain(key))

                    for u in range(n_ + 1):
                        if u < n_:
                            maxes(u)
                        if u:
                            normalise(u - 1)
                        if u >= 4:
                            hh, tt_ = units[u - 4]
                            if hh % 2 == 1 and tt_ == q_tts[-1]:
                                lo_of_pair(hh // 2)
                    lo_of_pair(AH // 2 - 1)
                    W.mark(yT_ready, (l, b))

                merge(0)
                attention("ga", 1)
                merge(1)
                attention("na", 2)
                merge(2)
                for k in range(KD):
                    dve.wait_ge(*merged_hi.at((l, k)))
                    v.tensor_tensor(hT_lo[:, k, t0:TT], merged[:, k, t0:TT], hT_hi[:, k, t0:TT].bitcast(F32), ALU.subtract)\
                        .then_inc(*(W.tell(merged_ready, l) if k == KD - 1 else W.next()))
                if not last:
                    mod_cols(l + 1, 11)
                post(l, "mix", q_tts, o_mix, (l, "ffn"))
                norm(l, "ffn", q_tts)
                per = 512 // nq
                for c in range(FB // 2):
                    for g in range(4 // per):
                        key = (("up", l, c), g)
                        dve.wait_ge(*conv_mid.at((l, c, g)))
                        for tap in (0, 2):
                            if tap == 2:
                                dve.wait_ge(*W.last())
                            for j in range(per):
                                q = g * per + j
                                blk = 2 * c + q % 2 + (FB if q >= 2 else 0)
                                ps = psum(key)[:, j * nq:(j + 1) * nq].rearrange("p (s t) -> p s t", t=T)
                                cv = conv[:, q, t0:TT].rearrange("p (s t) -> p s t", t=T)
                                src, dst = (ps[:, :, 0:T - 1], cv[:, :, 1:T]) if tap == 0 else (ps[:, :, 1:T], cv[:, :, 0:T - 1])
                                v.scalar_tensor_tensor(dst, src, V(f"ffn_w{l}", tap * 2 * FB + blk), dst, ALU.mult, ALU.add)\
                                    .then_inc(*(W.drain(key) if tap == 2 and j == per - 1 else W.next()))
                            W.mark(conv_done, (l, c))
                    dve.wait_ge(*ffn_silu.at((l, c)))
                    v.tensor_tensor(conv[:, 0:2, t0:TT], conv[:, 0:2, t0:TT], conv[:, 2:4, t0:TT], ALU.mult)\
                        .then_inc(*W.tell(ffn_prod, (l, c)))
                    dve.wait_ge(*fT_hi_ready.at((l, c)))
                    v.tensor_tensor(fT_lo[:, 2 * c:2 * c + 2, t0:TT], conv[:, 0:2, t0:TT],
                                    fT_hi[:, 2 * c:2 * c + 2, t0:TT].bitcast(F32), ALU.subtract)\
                        .then_inc(*W.tell(fT_ready, (l, c)))
                post(l, "ffn", q_tts, o_ffn, (l + 1, "mix"))
    es.close()


def pieces_of(w, cols):
    w = np.asarray(w)
    cols = np.asarray(cols)
    block = np.where(cols >= 0, w[:, np.maximum(cols, 0)], np.zeros((), w.dtype))
    return block.reshape(-1, KP, P, COLS).transpose(0, 2, 1, 3).reshape(-1, P, KP * COLS)


def chunk_columns(name, c):
    r = np.arange
    if name == "w_in":
        first = [8, 9, 10, 11, 0, 1, 2, 3, 4, 5, 6, 7][c]
        return r(first * COLS, (first + 1) * COLS)
    if name == "w_in_2":
        mq, mk, mv, mo, mg = 0, BW, 2 * BW, 3 * BW, 4 * BW
        aq = mg + 16
        ak, av = aq + BW, aq + BW + P
        nq = av + P
        zg = nq + 3 * BW
        if c == 0:
            gates = np.full(256, -1)
            for k, at in enumerate((0, 64, 32, 96)):
                gates[at:at + MH] = r(mg + k * MH, mg + (k + 1) * MH)
            return np.concatenate([r(ak, ak + P), r(av, av + P), gates])
        if c < 9:
            first = [None, aq, mq, mk, mv, mo, nq, nq + BW, nq + 2 * BW][c]
            return r(first, first + COLS)
        return r(zg + (c - 9) * COLS, zg + (c - 8) * COLS)
    if name == "w_up":
        a = r(2 * c * P, (2 * c + 2) * P)
        return np.concatenate([a, FF + a])
    return r(c * COLS, (c + 1) * COLS)


def weight_stream(x):
    out = []
    for name, l, c, _ in stream():
        if name in ("w_in", "w_out"):
            w = x[name]
        elif name == "w_mod":
            w = x["w_mod_2"][l]
        elif name == "w_branch":
            w = x["w_branch_2"][l][c // 2]
            c = c % 2
        else:
            w = x[name if name.endswith("_2") else name + "_2"][l]
        out.append(pieces_of(w, chunk_columns(name, c)))
    return np.concatenate(out)


def column_vectors(x):
    f = np.float32
    out = np.zeros((P, NV), f)

    def put(name, a):
        a = np.asarray(a)
        n = a.size // P
        out[:, VAT[name]:VAT[name] + n] = a.reshape(n, P).T

    put("norm_in_g", x["norm_in_g"])
    put("conv_w", x["conv_w"])
    put("conv_b", x["conv_b"])
    put("gate_a_b", x["gate_a_b"])
    put("gate_x_b", x["gate_x_b"])
    put("lambda", x["lru_lambda"])
    put("c", x["c_2"])
    put("c_ctx", x["c_ctx_2"])
    for l in range(LAYERS):
        put(f"b_mod{l}", x["b_mod_2"][l])
        for a, b in (("g_pre_mix", "g_pre_mix_2"), ("g_post_mix", "g_post_mix_2"), ("g_pre_ffn", "g_pre_ffn_2"),
                     ("g_post_ffn", "g_post_ffn_2"), ("g_ml", "g_ml_out_2"), ("ffn_w", "conv_w_2"), ("ffn_b", "conv_b_2")):
            put(f"{a}{l}", x[b][l])
        g = np.asarray(x["b_ml_gates_2"][l])
        out[0:MH, VAT[f"i_bias{l}"]], out[32:32 + MH, VAT[f"i_bias{l}"]] = g[0:4], g[8:12]
        out[0:MH, VAT[f"f_bias{l}"]], out[32:32 + MH, VAT[f"f_bias{l}"]] = g[4:8], g[12:16]
    return out


def shape_tables():
    t = np.zeros((P, NTAB), np.float64)
    i = np.arange(P)
    t[:, TAT["ident"]:TAT["ident"] + P] = np.eye(P)
    t[:, TAT["causal"]:TAT["causal"] + P] = np.where(i[:, None] <= i[None, :], 0, NEG)
    t[:, TAT["anticausal"]:TAT["anticausal"] + P] = np.where(i[:, None] >= i[None, :], 0, NEG)
    col = i % GRID
    c0 = np.clip(col - WIN // 2, 0, GRID - WIN)
    k = np.arange(GRID)[None, :]
    t[:, TAT["window"]:TAT["window"] + GRID] = np.where((k >= c0[:, None]) & (k < c0[:, None] + WIN), 0, NEG)
    half = HD // 2
    inv = (10000.0 ** (-np.arange(0, half, 2) / half)).astype(np.float32)
    sign = np.concatenate([-np.ones(16), np.ones(16)] * 2)
    for n in range(NT):
        tok = n * P + i
        r = ((tok // GRID).astype(np.float32)[:, None] * inv).astype(np.float64)
        c = ((tok % GRID).astype(np.float32)[:, None] * inv).astype(np.float64)
        ang = np.concatenate([r, r, c, c], axis=1)
        t[:, TAT["rope_cos"] + n * HD:TAT["rope_cos"] + (n + 1) * HD] = np.cos(ang)
        t[:, TAT["rope_sin"] + n * HD:TAT["rope_sin"] + (n + 1) * HD] = np.sin(ang) * sign
    s = TAT["mod_sel"]
    t[0, s] = t[2, s] = t[1, s + 1] = t[3, s + 1] = 1
    inv = (10000.0 ** (-np.arange(0, P, 2) / P)).astype(np.float32)
    ang = (inv[:, None] * np.arange(T, dtype=np.float32)[None, :]).astype(np.float64)
    rot = np.stack([np.concatenate([np.cos(ang)] * 2), np.concatenate([np.sin(ang), -np.sin(ang)])], axis=1)
    log_g = np.log1p(-np.exp2(-5.0 - np.arange(HEADS)))
    rel = np.arange(T)[None, :] - i[:, None]
    decay = np.where(rel[:, None, :] >= 0, np.exp(np.maximum(rel, 0)[:, None, :] * log_g[None, :, None]), 0) * P ** -0.5
    return t.astype(np.float32), rot.astype(np.float32), decay.astype(np.float32)


def window_bias(rpb):
    rpb = np.asarray(rpb)
    p = np.arange(P)
    dr = 5 - p // GRID
    dr = dr[:, None, None] + np.arange(6)[None, :, None]
    dc = np.arange(GRID)[None, None, :] - (p % GRID)[:, None, None] + WIN - 1
    inside = (dc >= 0) & (dc < 2 * WIN - 1)
    got = rpb[:, :, dr, np.clip(dc, 0, 2 * WIN - 2)]
    return np.where(inside, got, np.zeros((), rpb.dtype))


def kernel(**inputs):
    import concourse.bacc as bacc
    from concourse.bass_utils import run_bass_kernel_spmd

    x = {k: np.asarray(v) for k, v in inputs.items()}
    tab, rot, decay = shape_tables()
    f = np.ascontiguousarray
    rows = np.stack([np.stack([x["g_q_2"][l], x["g_k_2"][l]]) for l in range(LAYERS)])
    arrays = {
        "weights": weight_stream(x),
        "x": f(x["x"].reshape(NT, P, D).transpose(1, 0, 2)),
        "ctx": f(x["ctx_2"].reshape(NT, P, D).transpose(1, 0, 2)),
        "vectors": column_vectors(x),
        "tables": tab,
        "rotary": rot,
        "decay": decay,
        "gate_weights": f(np.stack([x["gate_a_w"], x["gate_x_w"]]).transpose(2, 0, 1, 3)),
        "head_gains": f(np.broadcast_to(rows[None], (P, *rows.shape))),
        "norm_out_rows": f(np.broadcast_to(x["norm_out_g"][None], (P, D))),
        "window_bias": f(window_bias(x["na_rpb_2"])),
    }

    def emit(plan, planning):
        nc = bacc.Bacc("TRN2", target_bir_lowering=False, num_devices=1)
        args = [nc.dram_tensor(f"in_{n}", a.shape, mybir.dt.from_np(a.dtype), kind="ExternalInput").ap()
                for n, a in arrays.items()]
        order = dict(zip(arrays, args))
        out = nc.dram_tensor("out_0", (P, NT, D), F32, kind="ExternalOutput").ap()
        build(nc, order["weights"], order["x"], order["ctx"], order["vectors"], order["tables"], order["rotary"],
              order["decay"], order["gate_weights"], order["head_gains"], order["norm_out_rows"], order["window_bias"],
              out, plan, planning)
        return nc

    plan = {}
    emit(plan, True)
    nc = emit(plan, False)
    r = run_bass_kernel_spmd(nc, [{f"in_{n}": a for n, a in arrays.items()}], core_ids=[0])
    got = r.results[0]["out_0"]
    return np.ascontiguousarray(got.transpose(1, 0, 2)).reshape(1, T, D)
```

```python
from contextlib import ExitStack

import numpy as np

import concourse.bass as bass
from concourse import mybir

F32 = mybir.dt.float32
F32R = mybir.dt.float32r
ACT = mybir.ActivationFunctionType
ALU = mybir.AluOpType
AX = mybir.AxisListType

P = 128
D = 1024
KD = D // P
T = 256
NT = T // P
TT = 2 * T
COLS = 512
KP = 2
RING = 4
GA_EVERY, ML_EVERY, NA_EVERY, NA_SKIP = 1, 1, 2, 8
MODS_IN = 4
MOD_CHUNKS = 6 * D // COLS
EPS = 1e-6
HEADS = 8
MH = 4
AH = 8
HD = 64
BW = 512
FF = 2816
FB = FF // P
GRID = 64
WIN = 16
LAYERS = 2
NEG = -1e30
GATE_ROWS = 36

_VEC = [("norm_in_g", 8), ("conv_w", 32), ("conv_b", 8), ("gate_a_b", 8), ("gate_x_b", 8), ("lambda", 8),
        ("c", 8), ("c_ctx", 8)]
for _l in range(LAYERS):
    _VEC += [(f"b_mod{_l}", 48), (f"g_pre_mix{_l}", 8), (f"g_post_mix{_l}", 8), (f"g_pre_ffn{_l}", 8),
             (f"g_post_ffn{_l}", 8), (f"g_ml{_l}", 4), (f"ffn_w{_l}", 3 * 2 * FB), (f"ffn_b{_l}", 2 * FB),
             (f"i_bias{_l}", 1), (f"f_bias{_l}", 1)]
VAT, NV = {}, 0
for _n, _w in _VEC:
    VAT[_n] = NV
    NV += _w

_TAB = [("ident", 128), ("causal", 128), ("anticausal", 128), ("window", 64), ("rope_cos", 2 * HD),
        ("rope_sin", 2 * HD), ("mod_sel", 2)]
TAT, NTAB = {}, 0
for _n, _w in _TAB:
    TAT[_n] = NTAB
    NTAB += _w


def mods_beside(h):
    n = MOD_CHUNKS - MODS_IN
    return range(MODS_IN + n * h // (HEADS + 2), MODS_IN + n * (h + 1) // (HEADS + 2))


def ml_ranges(d, s, first):
    tiles = [t for t in range(first, 4) if ml_allowed(d, s, t)]
    out = []
    for t in tiles:
        if out and out[-1][1] == t * P:
            out[-1] = (out[-1][0], (t + 1) * P)
        else:
            out.append((t * P, (t + 1) * P))
    return out


def ml_allowed(d, s, t):
    if d == 0:
        return t >= s
    return s < 2 <= t or (s // 2 == t // 2 and s >= t)


def chunk(name, l, first, end, tiles=KD):
    return [(name, l, c, k) for c in range(first, end) for k in range(0, tiles, KP)]


def stream():
    out = []
    for c in range(12):
        for k in range(0, KD, KP):
            out.append(("w_in", 0, c, k))
            n = (c * KD + k) // KP + 1
            if n % (12 // MODS_IN) == 0:
                m = n // (12 // MODS_IN) - 1
                out.append(("w_mod", 0, m * KP // KD, m * KP % KD))
    out += chunk("w_mod", 0, MODS_IN, MOD_CHUNKS)
    out += chunk("w_out", 0, 0, 2, 2 * KD)
    for l in range(LAYERS):
        out += chunk("w_in_2", l, 0, 9)
        for b in range(3):
            for half in range(2):
                out += chunk("w_in_2", l, 9 + 2 * b + half, 10 + 2 * b + half)
                out += chunk("w_branch", l, 2 * b + half, 2 * b + half + 1, BW // P)
        out += chunk("w_out_2", l, 0, 2)
        mods = chunk("w_mod", l + 1, 0, MOD_CHUNKS) if l + 1 < LAYERS else []
        for piece in chunk("w_up", l, 0, FB // 2):
            out += [piece] + mods[:1]
            mods = mods[1:]
        out += mods + chunk("w_down", l, 0, 2, FB)
    return out


NPIECES = len(stream())


def build(nc, wst, x_in, ctx_in, vec_in, tab_in, rot_in, decay_in, gatew_in, rowg_in, gout_in, bias_in, out, plan,
          planning):
    es = ExitStack()
    base = (nc.sbuf_base + 31) // 32 * 32
    KB = 1024

    def sb(name, shape, at, dt=F32):
        return nc.alloc_sbuf_tensor_at(name, shape, dt, offset=base + int(at))

    resid = [sb("resid_c", [P, NT, D], 0), sb("resid_x", [P, NT, D], 8 * KB)]
    hT_hi = sb("hT_hi", [P, KD, TT], 16 * KB, F32R)
    hT_lo = sb("hT_lo", [P, KD, TT], 32 * KB, F32R)
    w_raw = sb("w_raw", [P, RING, KP * COLS], 48 * KB)
    w_hi = sb("w_hi", [P, RING, KP, COLS], 64 * KB, F32R)
    w_lo = sb("w_lo", [P, RING, KP, COLS], 80 * KB, F32R)
    R = 96 * KB
    C = R + 88.0625 * KB
    decay = sb("decay", [P, HEADS, T], 0)
    xT_hi = sb("xT_hi", [P, KD, T], 16 * KB, F32R)
    xT_lo = sb("xT_lo", [P, KD, T], 24 * KB, F32R)
    gatew = sb("gatew", [P, 2, HEADS, P], 32 * KB)
    xc = sb("xc", [P, HEADS, T], 40 * KB)
    mix_hi = sb("mix_hi", [P, 2 * KD, T], R, F32R)
    mix_lo = sb("mix_lo", [P, 2 * KD, T], R + 16 * KB, F32R)
    lru_r = sb("lru_r", [P, HEADS, T], R)
    lru_i = sb("lru_i", [P, HEADS, T], R + 16 * KB)
    qT = sb("qT", [P, HEADS, T], R + 32 * KB)
    kT = sb("kT", [P, HEADS, T], R + 40 * KB)
    v1 = sb("v1", [P, NT, D], R + 48 * KB)
    sg = sb("sg", [P, NT, D], R + 56 * KB)
    xlT = sb("xlT", [P, HEADS, T + 3], R + 64 * KB)
    glT = sb("glT", [P, HEADS, T], R + 73 * KB)
    rot = sb("rot", [P, 2, T], R + 81 * KB)
    rot_tmp = sb("rot_tmp", [P, 2, T], R + 83 * KB)
    sT = sb("sT", [P, 2, 3 * P], R + 85 * KB)
    xn1 = sb("xn1", [P, NT, D], R + 32 * KB)
    xt_tmp = sb("xt_tmp", [P, KD, T], R + 48 * KB)
    onrm = sb("onrm", [P, 2, T], 40 * KB)
    gout_row = sb("gout_row", [P, D], R + 64 * KB)
    S = R
    xn = sb("xn", [P, 2 * NT, D], S)
    o_mix = sb("o_mix", [P, 2 * NT, D], S)
    merged = sb("merged", [P, KD, TT], S)
    aq = sb("aq", [P, 2 * NT, BW], S)
    ak = sb("ak", [P, 2 * NT, P], S + 8 * KB)
    kdup = sb("kdup", [P, 2 * NT, 2 * P], S + 10 * KB)
    ml_w = sb("ml_w", [P, 2, 2 * NT, TT], S)
    mqT = sb("mqT", [P, MH, TT], R + 16 * KB)
    mkT = sb("mkT", [P, MH, TT], R + 24 * KB)
    mv = sb("mv", [P, 2 * NT, MH, P + 1], R + 32 * KB)
    zo = sb("zo", [P, 2 * NT, BW], R + 40.0625 * KB)
    gprob = sb("gprob", [P, 4, TT], R + 48.0625 * KB)
    ptmp = sb("ptmp", [P, 4, TT], R + 48.0625 * KB)
    gqT = sb("gqT", [P, 4, TT], R + 56.0625 * KB)
    gkT = sb("gkT", [P, 2, TT], R + 64.0625 * KB)
    av = sb("av", [P, 2 * NT, P], R + 68.0625 * KB)
    nqT = sb("nqT", [P, 4, TT], R + 64.0625 * KB)
    nkT = sb("nkT", [P, 4, TT], R + 72.0625 * KB)
    nv = sb("nv", [P, 2 * NT, BW], R + 80.0625 * KB)
    yT_hi = sb("yT_hi", [P, 4, TT], R + 16 * KB, F32R)
    yT_lo = sb("yT_lo", [P, 4, TT], R + 24 * KB, F32R)
    nbias = sb("nbias", [P, 4, 6, GRID], R + 32 * KB)
    nprob = sb("nprob", [P, 4, TT], R + 40.0625 * KB)
    fT_hi = sb("fT_hi", [P, FB, TT], R, F32R)
    fT_lo = sb("fT_lo", [P, FB, TT], R + 44 * KB, F32R)
    o_ffn = sb("o_ffn", [P, 2 * NT, D], 16 * KB)
    at = [C]

    def small(name, shape, dt=F32):
        n = 4 * int(np.prod(shape[1:]))
        t = sb(name, shape, at[0], dt)
        at[0] += (n + 31) // 32 * 32
        return t

    vec = small("vec", [P, NV])
    tab = small("tab", [P, NTAB])
    rowg = small("rowg", [P, LAYERS, 2, HD])
    modT = small("modT", [P, LAYERS, 48, 2])
    probT = sb("probT", [P, 2, TT], at[0])
    mrow = small("mrow", [P, 2, COLS])
    mod_c = small("mod_c", [P, KD, 2])
    mod_st = small("mod_st", [P, 4 * KD + P], F32R)
    acol = small("acol", [P, 2 * NT, 2, GATE_ROWS])
    scol = small("scol", [P, KD, 2])
    gcol = small("gcol", [P, KD, 2])
    ones = small("ones", [P, 1])
    zero = small("zero", [P, 1])
    ss = small("ss", [P, 64])
    rs = small("rs", [P, 64])
    att = small("att", [P, 4, 4])
    lam = small("lam", [P, 4, HEADS])
    bnst = small("bnst", [P, 4, 8])
    eps = small("eps", [P, 1])
    rows_at = at[0]
    rows = small("rows", [P, 5, TT])
    gain_mix = sb("gain_mix", [P, 2, D], R + 56.0625 * KB)
    gain_ffn = sb("gain_ffn", [P, 2, D], rows_at)
    junk_mix = sb("junk_mix", [P, 4, COLS], R + 48.0625 * KB)
    junk_ffn = sb("junk_ffn", [P, 4, COLS], 32 * KB)
    conv = sb("conv", [P, 4, TT], rows_at)

    ident = tab[:, TAT["ident"]:TAT["ident"] + P]

    def mod_cols_of(j):
        return mod_st[:, 0:4 * KD].rearrange("p (k f) -> p k f", f=4)[:, :, j:j + 2]

    def V(name, i=0, n=1):
        return vec[:, VAT[name] + i:VAT[name] + i + n]

    bank = [es.enter_context(nc.psum_tensor(f"bank{b}", [P, 512], F32)) for b in range(8)]
    bank_filled = [es.enter_context(nc.semaphore(f"bank_filled{b}")) for b in range(8)]
    bank_drained = [es.enter_context(nc.semaphore(f"bank_drained{b}")) for b in range(8)]
    raw_loaded = [es.enter_context(nc.semaphore(f"raw_loaded{s}")) for s in range(RING)]
    hi_ready = es.enter_context(nc.semaphore("hi_ready"))
    lo_ready = es.enter_context(nc.semaphore("lo_ready"))
    piece_used = es.enter_context(nc.semaphore("piece_used"))
    small_loaded = es.enter_context(nc.semaphore("small_loaded"))
    x_loaded = es.enter_context(nc.semaphore("x_loaded"))
    ctx_loaded = es.enter_context(nc.semaphore("ctx_loaded"))
    gout_loaded = es.enter_context(nc.semaphore("gout_loaded"))
    bias_loaded = [es.enter_context(nc.semaphore(f"bias_loaded{s}")) for s in range(4)]
    out_stored = es.enter_context(nc.semaphore("out_stored"))

    class Counter:

        def __init__(self, name):
            self.name, self.sem, self.n = name, es.enter_context(nc.semaphore(name)), 0

        def next(self, key):
            self.n += 1
            plan[(self.name, key)] = (self.name, self.n)
            return self.sem, 1

        def at(self, key):
            assert planning or (self.name, key) in plan, (self.name, key)
            name, n = plan.get((self.name, key), (self.name, 1))
            return by_name[name], n

    acol_ready = Counter("acol_ready")
    ak_raw = Counter("ak_raw")
    ak_ready = Counter("ak_ready")
    aq_ready = Counter("aq_ready")
    bias_used = Counter("bias_used")
    conv_done = Counter("conv_done")
    conv_mid = Counter("conv_mid")
    conv_ready = Counter("conv_ready")
    exp_done = Counter("exp_done")
    fT_hi_ready = Counter("fT_hi_ready")
    fT_ready = Counter("fT_ready")
    ffn_prod = Counter("ffn_prod")
    ffn_silu = Counter("ffn_silu")
    floor_ready = Counter("floor_ready")
    gate_used = Counter("gate_used")
    h1_ready = Counter("h1_ready")
    hT_hi_ready = Counter("hT_hi_ready")
    hT_ready = Counter("hT_ready")
    hT_tmp_ready = Counter("hT_tmp_ready")
    k_ready = Counter("k_ready")
    lam_ready = Counter("lam_ready")
    lam_scaled = Counter("lam_scaled")
    log_ready = Counter("log_ready")
    lru_a = Counter("lru_a")
    lru_clamped = Counter("lru_clamped")
    lru_e2 = Counter("lru_e2")
    lru_gated = Counter("lru_gated")
    lru_hi = Counter("lru_hi")
    lru_ix = Counter("lru_ix")
    lru_mult = Counter("lru_mult")
    lru_y = Counter("lru_y")
    merged_hi = Counter("merged_hi")
    merged_ready = Counter("merged_ready")
    merged_sum = Counter("merged_sum")
    ml_e = Counter("ml_e")
    ml_exp = Counter("ml_exp")
    ml_root = Counter("ml_root")
    ml_ss = Counter("ml_ss")
    ml_w_ready = Counter("ml_w_ready")
    ml_y = Counter("ml_y")
    mod_c_ready = Counter("mod_c_ready")
    mod_hi_ready = Counter("mod_hi_ready")
    mod_st_ready = Counter("mod_st_ready")
    neg_max = Counter("neg_max")
    post_ms = Counter("post_ms")
    post_root = Counter("post_root")
    probT_used = Counter("probT_used")
    prob_ready = Counter("prob_ready")
    q_ready = Counter("q_ready")
    qk_root = Counter("qk_root")
    qk_ss = Counter("qk_ss")
    resid_ready = Counter("resid_ready")
    ret_hi = Counter("ret_hi")
    ret_root = Counter("ret_root")
    ret_var = Counter("ret_var")
    ret_y = Counter("ret_y")
    root_ready = Counter("root_ready")
    rows_ready = Counter("rows_ready")
    xT_hi_ready = Counter("xT_hi_ready")
    xT_ready = Counter("xT_ready")
    xn_ready = Counter("xn_ready")
    yT_hi_ready = Counter("yT_hi_ready")
    yT_ready = Counter("yT_ready")
    gcol_ready = Counter("gcol_ready")
    gain_ready = Counter("gain_ready")
    stat_ready = Counter("stat_ready")
    recip_ready = Counter("recip_ready")
    xn_odd_ready = Counter("xn_odd_ready")
    zo_ready = Counter("zo_ready")
    by_name = {c.name: c.sem for c in (acol_ready, ak_raw, ak_ready, aq_ready, bias_used, conv_done, conv_mid, conv_ready, exp_done, fT_hi_ready, fT_ready, ffn_prod, ffn_silu, floor_ready, gate_used, h1_ready, hT_hi_ready, hT_ready, hT_tmp_ready, k_ready, lam_ready, lam_scaled, log_ready, lru_a, lru_clamped, lru_e2, lru_gated, lru_hi, lru_ix, lru_mult, lru_y, merged_hi, merged_ready, merged_sum, ml_e, ml_exp, ml_root, ml_ss, ml_w_ready, ml_y, mod_c_ready, mod_hi_ready, mod_st_ready, neg_max, post_ms, post_root, probT_used, prob_ready, q_ready, qk_root, qk_ss, resid_ready, ret_hi, ret_root, ret_var, ret_y, root_ready, rows_ready, xT_hi_ready, xT_ready, xn_ready, yT_hi_ready, yT_ready, gcol_ready, gain_ready, stat_ready, recip_ready, xn_odd_ready, zo_ready)}
    by_name.update({f"bank_drained{b}": bank_drained[b] for b in range(8)})
    uses = [0] * 8
    turn = {"rot": 0, "acc": 0, "gemm": 0, "side": 0}
    pools = {"rot": [0, 1, 2, 3, 4, 5], "acc": [6, 7], "gemm": [0, 1, 2, 3], "side": [4, 5]}
    fills = [0] * 8
    pieces = [0]

    def take(pe, key, pool="rot"):
        b = pools[pool][turn[pool] % len(pools[pool])]
        turn[pool] += 1
        if uses[b]:
            pe.wait_ge(bank_drained[b], uses[b])
        uses[b] += 1
        plan[("bank", key)] = b, uses[b]
        return bank[b]

    def filled(key):
        b = plan[("bank", key)][0]
        fills[b] += 1
        plan[("filled", key)] = ("bank", b, fills[b], pieces[0])
        return bank_filled[b], 1

    def psum(key):
        return bank[plan.get(("bank", key), (0, 1))[0]]

    def filled_at(key):
        kind, b, n, _ = plan.get(("filled", key), ("bank", 0, 1, 0))
        return bank_filled[b] if kind == "bank" else piece_used, n

    def drained_at(key):
        b, n = plan.get(("bank", key), (0, 1))
        return bank_drained[b], n

    class Beside:

        def __init__(self, steps, every=1, skip=0):
            self.steps, self.every, self.n = steps, every, -skip

        def slot(self):
            self.n += 1
            if self.n > 0 and self.n % self.every == 0:
                next(self.steps, None)

        def finish(self):
            for _ in self.steps:
                pass

    class Steps:

        def __init__(self, name):
            self.chain = Counter(name)
            by_name[name] = self.chain.sem

        def next(self):
            return self.tell(self.chain, self.chain.n)

        def tell(self, counter, key):
            inc = counter.next(key)
            self.at = counter.name, counter.n
            return inc

        def drain(self, key):
            b, n = plan.get(("bank", key), (0, 1))
            self.at = f"bank_drained{b}", n
            return bank_drained[b], 1

        def last(self):
            return by_name[self.at[0]], self.at[1]

        def mark(self, counter, key):
            plan[(counter.name, key)] = self.at

    A, W = Steps("act_chain"), Steps("dve_chain")

    with nc.Block() as block:
        @block.sync
        def _(sp):
            sp.dma_start(vec[:], vec_in).then_inc(small_loaded, 16)
            sp.dma_start(tab[:], tab_in).then_inc(small_loaded, 16)
            sp.dma_start(rowg[:], rowg_in).then_inc(small_loaded, 16)
            sp.dma_start(rot[:], rot_in).then_inc(small_loaded, 16)
            sp.dma_start(gatew[:], gatew_in).then_inc(small_loaded, 16)
            sp.dma_start(decay[:], decay_in).then_inc(small_loaded, 16)
            for s in range(RING):
                sp.dma_start(w_raw[:, s, :], wst[s]).then_inc(raw_loaded[s], 16)
            with sp.Fori(1, NPIECES // RING) as i:
                for s in range(RING):
                    sp.wait_ge(lo_ready, (i - 1) * RING + s + 1)
                    sp.dma_start(w_raw[:, s, :], wst[bass.ds(i * RING + s, 1)].rearrange("a p n -> (a p) n"))\
                        .then_inc(raw_loaded[s], 16)

        @block.gpsimd
        def _(pool):
            def split_lo(i, s, first):
                pool.wait_ge(hi_ready, i * RING + s + 1)
                if not first:
                    pool.wait_ge(piece_used, (i - 1) * RING + s + 1)
                nc.gpsimd.tensor_tensor(w_lo[:, s].rearrange("p k n -> p (k n)"), w_raw[:, s, :],
                                        w_hi[:, s].rearrange("p k n -> p (k n)").bitcast(F32),
                                        ALU.subtract).then_inc(lo_ready, 1)
            for s in range(RING):
                split_lo(0, s, True)
            with pool.Fori(1, NPIECES // RING) as i:
                for s in range(RING):
                    split_lo(i, s, False)

        @block.tensor
        def _(pe):
            def gemm(banks, tiles, x_hi, x_lo, weights_stationary, beside=None, steps=None, inputs=None):
                pool = "gemm" if beside else "rot"
                held = {}
                for p in range(tiles // KP):
                    s = pieces[0] % RING
                    pe.wait_ge(hi_ready, pieces[0] + 1)
                    pe.wait_ge(lo_ready, pieces[0] + 1)
                    pieces[0] += 1
                    if inputs is not None:
                        pe.wait_ge(*inputs(p))
                    for key, subs in banks:
                        if p == 0:
                            held[key] = take(pe, key, pool)
                        for n, (oc, wc, xcols) in enumerate(subs):
                            for kk in range(KP):
                                k = p * KP + kk
                                for t, (w, x) in enumerate(((w_hi, x_hi), (w_hi, x_lo), (w_lo, x_hi))):
                                    wa, xa = w[:, s, kk, wc], x[:, k, xcols]
                                    st, mv_ = (wa, xa) if weights_stationary else (xa, wa)
                                    mm = pe.matmul(held[key][:, oc], st, mv_, start=(k == 0 and t == 0 and n == 0),
                                                   stop=(k == tiles - 1 and t == 2), skip_group_check=True)
                        if key == banks[-1][0]:
                            mm.then_inc(piece_used, 1)
                            if p == tiles // KP - 1:
                                plan[("filled", key)] = ("piece", 0, pieces[0], pieces[0])
                        elif p == tiles // KP - 1:
                            mm.then_inc(*filled(key))
                        if beside:
                            beside.slot()
                    if steps is not None:
                        next(steps, None)

            def blocks_T(key, n, x, xs):
                nt = xs.stop - xs.start
                per = 512 // nt
                return [((key, g), [(slice(j * nt, (j + 1) * nt), slice((g * per + j) * P, (g * per + j + 1) * P), xs)
                                    for j in range(per)]) for g in range(n // per)]

            def gemm_T(key, xs, x_hi, x_lo, n=4, tiles=KD, **more):
                gemm(blocks_T(key, n, None, xs), tiles, x_hi, x_lo, True, **more)

            def gemm_tok(key, tts, x_hi, x_lo, tiles=KD, cols=COLS, at=0, **more):
                per = 512 // cols
                banks = []
                for g in range(len(tts) // per):
                    banks.append(((key, g), [(slice(j * cols, (j + 1) * cols), slice(at, at + cols),
                                              slice(tts[g * per + j] * P, (tts[g * per + j] + 1) * P)) for j in range(per)]))
                gemm(banks, tiles, x_hi, x_lo, False, **more)

            def mod_chunk(l, c, idle=0):
                key = ("mod", l, c)
                for p in range(KD // KP):
                    for _ in range(idle):
                        yield
                    if p == 0:
                        ps = take(pe, key, "acc")
                    s = pieces[0] % RING
                    pe.wait_ge(hi_ready, pieces[0] + 1)
                    pe.wait_ge(lo_ready, pieces[0] + 1)
                    pieces[0] += 1
                    for kk in range(KP):
                        k = p * KP + kk
                        for w in (w_hi, w_lo):
                            mm = pe.matmul(ps[:], mod_st[:, 4 * k:4 * k + P], w[:, s, kk, :],
                                           start=(k == 0 and w is w_hi), stop=(k == KD - 1 and w is w_lo))
                    mm.then_inc(piece_used, 1)
                    if p == KD // KP - 1:
                        plan[("filled", key)] = ("piece", 0, pieces[0], pieces[0])
                    yield

            def mod_turn(l, c):
                pe.wait_ge(*drained_at(("mod", l, c)))
                ps = take(pe, ("modT", l, c), "acc")
                for j in range(4):
                    mm = pe.matmul(ps[:, 2 * j:2 * j + 2], mrow[0:4, c % 2, j * P:(j + 1) * P],
                                   tab[0:4, TAT["mod_sel"]:TAT["mod_sel"] + 2], start=True, stop=True)
                mm.then_inc(*filled(("modT", l, c)))

            pe.wait_ge(small_loaded, 96)
            for t in range(NT):
                pe.wait_ge(*xn_ready.at(("b1", t)))
            for g in range(KD // 2):
                ps = take(pe, ("xT", g))
                for j in range(2):
                    for t in range(NT):
                        mm = pe.transpose(ps[:, j * T + t * P:j * T + (t + 1) * P],
                                          xn1[:, t, (2 * g + j) * P:(2 * g + j + 1) * P], ident)
                mm.then_inc(*filled(("xT", g)))
            xs = slice(0, T)
            pe.wait_ge(*mod_st_ready.at(0))

            def gate(n):
                pe.wait_ge(*conv_ready.at(n))
                ps = take(pe, ("gate", n))
                pe.matmul(ps[:, 0:T], gatew[:, 0, n, :], xc[:, n, :], start=True, stop=True)
                mm = pe.matmul(ps[:, T:2 * T], gatew[:, 1, n, :], xc[:, n, :], start=True, stop=True)
                mm.then_inc(*filled(("gate", n)))

            def every_third():
                for c in range(MODS_IN):
                    for _ in mod_chunk(0, c, 12 // MODS_IN - 1):
                        yield

            mods = every_third()
            for c in range(12):
                if c == 0:
                    gemm_T(("in", c), xs, xT_hi, xT_lo, steps=mods, inputs=xT_ready.at)
                elif c < 8:
                    gemm_T(("in", c), xs, xT_hi, xT_lo, steps=mods)
                else:
                    gemm_tok(("in", c), [0, 1], xT_hi, xT_lo, steps=mods)
                if c % (12 // MODS_IN) == 0 and c:
                    mod_turn(0, c // (12 // MODS_IN) - 1)
                if 4 <= c < 8:
                    gate(2 * (c - 4))
                    gate(2 * (c - 4) + 1)

            def ret_scores(h):
                pe.wait_ge(*q_ready.at(h // 2))
                pe.wait_ge(*k_ready.at(h // 2))
                ps = take(pe, ("rs", h))
                pe.matmul(ps[:, 0:T], kT[:, h, 0:P], qT[:, h, :], start=True, stop=True)
                mm = pe.matmul(ps[:, T:T + P], kT[:, h, P:T], qT[:, h, P:T], start=True, stop=True)
                mm.then_inc(*filled(("rs", h)))

            def ret_out(h):
                pe.wait_ge(*drained_at(("rs", h)))
                ps = take(pe, ("ro", h))
                e = slice(h * P, (h + 1) * P)
                pe.matmul(ps[:, 0:P], sT[:, h % 2, 0:P], v1[:, 0, e], start=True, stop=True)
                pe.matmul(ps[:, P:T], sT[:, h % 2, P:2 * P], v1[:, 0, e], start=True, stop=False)
                mm = pe.matmul(ps[:, P:T], sT[:, h % 2, 2 * P:3 * P], v1[:, 1, e], start=False, stop=True)
                mm.then_inc(*filled(("ro", h)))

            def ret_turn(h):
                pe.wait_ge(*ret_y.at(h))
                ps = take(pe, ("ry", h))
                for t in range(NT):
                    mm = pe.transpose(ps[:, t * P:(t + 1) * P], onrm[:, h % 2, t * P:(t + 1) * P], ident)
                mm.then_inc(*filled(("ry", h)))

            pe.wait_ge(*drained_at((("in", 9), 1)))
            for h in range(HEADS + 2):
                if h < HEADS:
                    ret_scores(h)
                if 1 <= h <= HEADS:
                    ret_out(h - 1)
                if h >= 2:
                    ret_turn(h - 2)
                for c in mods_beside(h):
                    for _ in mod_chunk(0, c):
                        pass
                    mod_turn(0, c - 1)
            mod_turn(0, MOD_CHUNKS - 1)
            pe.wait_ge(*lru_y.at(HEADS - 1))
            pe.wait_ge(*drained_at(("ry", HEADS - 1)))
            for c in range(2):
                gemm_tok(("out", c), [0, 1], mix_hi, mix_lo, tiles=2 * KD)

            def next_mods(l):
                if l < LAYERS:
                    for c in range(MOD_CHUNKS):
                        yield from mod_chunk(l, c)

            def norm_T(l, which, tts):
                for t in tts:
                    pe.wait_ge(*(xn_odd_ready if t % 2 else xn_ready).at((l, which, t)))
                for k in range(KD):
                    ps = take(pe, ("nT", l, which, k))
                    for t in tts:
                        mm = pe.transpose(ps[:, t * P:(t + 1) * P], xn[:, t, k * P:(k + 1) * P], ident)
                    mm.then_inc(*filled(("nT", l, which, k)))

            def normed(l, which):
                return lambda p: hT_ready.at((l, which, KP * p + KP - 1))

            def spread(l, which, sets):
                pe.wait_ge(*gcol_ready.at((l, which)))
                for s in sets:
                    for half in range(2):
                        ps = take(pe, ("spread", l, which, s, half), "acc")
                        for j in range(4):
                            k = half * 4 + j
                            mm = pe.matmul(ps[:, j * P:(j + 1) * P], gcol[:, k, 1 - s:2 - s].to_broadcast([P, P]),
                                           ident, start=True, stop=True)
                        mm.then_inc(*filled(("spread", l, which, s, half)))

            for l in range(LAYERS):
                last = l == LAYERS - 1
                every = slice(0, TT)
                tts = list(range(4))
                q_tts = [2, 3] if last else tts
                qs = slice(T, TT) if last else every
                sets = [1] if last else [0, 1]
                q0 = q_tts[0] * P
                norm_T(l, "mix", tts)

                def turn_heads():
                    for t in q_tts:
                        pe.wait_ge(*aq_ready.at((l, t)))
                    for j in range(4):
                        ps = take(pe, ("gqT", l, j))
                        for t in q_tts:
                            mm = pe.transpose(ps[:, t * P:(t + 1) * P], aq[:, t, j * P:(j + 1) * P], ident)
                        mm.then_inc(*filled(("gqT", l, j)))
                    for t in tts:
                        pe.wait_ge(*ak_ready.at((l, t)))
                    for j in range(2):
                        ps = take(pe, ("gkT", l, j))
                        for t in tts:
                            mm = pe.transpose(ps[:, t * P:(t + 1) * P], kdup[:, t, j * P:(j + 1) * P], ident)
                        mm.then_inc(*filled(("gkT", l, j)))

                def attention(kind, q_, k_, v_, prob):
                    pe.wait_ge(*drained_at((("nv", l), 3) if kind == "na" else ("gkT", l, 1)))
                    units = [(h, t) for h in range(AH) for t in q_tts]

                    def keys(t):
                        return TT if t >= 2 else T

                    def a_scores(u):
                        h, t = units[u]
                        b0 = (h % 2) * HD
                        ps = take(pe, (kind, "s", l, h, t), "side")
                        kt_ = k_[b0:b0 + HD, h // 4 if kind == "ga" else h // 2, 0:keys(t)]
                        mm = pe.matmul(ps[:, 0:keys(t)], q_[b0:b0 + HD, h // 2, t * P:(t + 1) * P], kt_,
                                       start=True, stop=True)
                        mm.then_inc(*filled((kind, "s", l, h, t)))

                    def a_turn(u):
                        h, t = units[u]
                        pe.wait_ge(*prob_ready.at((kind, l, h, t)))
                        ps = take(pe, (kind, "t", l, h, t), "side")
                        for j in range(keys(t) // P):
                            mm = pe.transpose(ps[:, j * P:(j + 1) * P], prob[:, u % 4, j * P:(j + 1) * P], ident)
                        mm.then_inc(*filled((kind, "t", l, h, t)))

                    def a_out(u):
                        h, t = units[u]
                        pe.wait_ge(*drained_at((kind, "t", l, h, t)))
                        b0 = (h % 2) * HD
                        if h % 2 == 0 and t == q_tts[0]:
                            take(pe, (kind, "o", l, h // 2), "acc")
                        ps = psum((kind, "o", l, h // 2))
                        n = keys(t) // P
                        for j in range(n):
                            vv = v_[:, j, (h // 4) * HD:(h // 4 + 1) * HD] if kind == "ga" else v_[:, j, h * HD:(h + 1) * HD]
                            mm = pe.matmul(ps[b0:b0 + HD, t * P:(t + 1) * P], vv, probT[:, u % 2, j * P:(j + 1) * P],
                                           start=(j == 0), stop=(j == n - 1))
                        if h % 2 == 1 and t == q_tts[-1]:
                            mm.then_inc(*filled((kind, "o", l, h // 2)))
                        else:
                            mm.then_inc(*probT_used.next((kind, l, h, t)))

                    n = len(units)
                    for u in range(n + 3):
                        if u < n:
                            a_scores(u)
                        if 2 <= u < n + 2:
                            a_turn(u - 2)
                        if u >= 3:
                            a_out(u - 3)
                        yield

                banks = [((("kv", l), g), [(slice(j * T, (j + 1) * T), slice(0, T),
                                           slice((2 * g + j) * P, (2 * g + j + 1) * P)) for j in range(2)])
                         for g in range(2)]
                outs = [(key, take(pe, key), subs, False) for key, subs in banks]
                gkey = ("gates", l)
                outs.append((gkey, take(pe, gkey), [(every, slice(T, T + P), every)], True))
                for p in range(KD // KP):
                    s = pieces[0] % RING
                    pe.wait_ge(hi_ready, pieces[0] + 1)
                    pe.wait_ge(lo_ready, pieces[0] + 1)
                    pieces[0] += 1
                    pe.wait_ge(*normed(l, "mix")(p))
                    for key, ps, subs, stationary in outs:
                        for n, (oc, wc, xcols) in enumerate(subs):
                            for kk in range(KP):
                                k = p * KP + kk
                                for t, (w, x) in enumerate(((w_hi, hT_hi), (w_hi, hT_lo), (w_lo, hT_hi))):
                                    wa, xa = w[:, s, kk, wc], x[:, k, xcols]
                                    st, mv_ = (wa, xa) if stationary else (xa, wa)
                                    mm = pe.matmul(ps[:, oc], st, mv_, start=(k == 0 and t == 0 and n == 0),
                                                   stop=(k == KD - 1 and t == 2), skip_group_check=True)
                        if p == KD // KP - 1 and key != gkey:
                            mm.then_inc(*filled(key))
                    mm.then_inc(piece_used, 1)
                plan[("filled", gkey)] = ("piece", 0, pieces[0], pieces[0])
                gemm_tok(("aq", l), q_tts, hT_hi, hT_lo)
                gemm_T(("mq", l), qs, hT_hi, hT_lo)
                turn_heads()
                ga = Beside(attention("ga", gqT, gkT, av, gprob), GA_EVERY)
                gemm_T(("mk", l), every, hT_hi, hT_lo, beside=ga)
                gemm_tok(("mv", l), tts, hT_hi, hT_lo, beside=ga)
                gemm_tok(("mo", l), q_tts, hT_hi, hT_lo, beside=ga)
                ga.finish()
                pe.wait_ge(*rows_ready.at(l))
                ps = take(pe, ("acol", l), "side")
                for t in range(4):
                    for j, r in enumerate((0, 3)):
                        o = (t * 2 + j) * GATE_ROWS
                        mm = pe.transpose(ps[:, o:o + GATE_ROWS], rows[0:GATE_ROWS, r, t * P:(t + 1) * P],
                                          tab[0:GATE_ROWS, TAT["ident"]:TAT["ident"] + GATE_ROWS])
                mm.then_inc(*filled(("acol", l)))
                pe.wait_ge(*drained_at((("mv", l), 3)))
                pe.wait_ge(*drained_at(("acol", l)))
                pairs = [(h, d) for h in range(MH) for d in range(2)]

                def ml_scores(i):
                    h, d = pairs[i]
                    ps = take(pe, ("mb", l, h, d), "side")
                    r = 32 * d + h
                    mm = pe.matmul(ps[:, qs], tab[0:GATE_ROWS, TAT["ident"] + r:TAT["ident"] + r + 1].to_broadcast([GATE_ROWS, P]),
                                   rows[0:GATE_ROWS, 4, qs], start=True, stop=True)
                    mm.then_inc(*filled(("mb", l, h, d)))
                    for s in range(4):
                        ps = take(pe, ("ms", l, h, d, s), "side")
                        seen = slice(T, TT) if s >= 2 else qs
                        mm = pe.matmul(ps[:, seen], mkT[:, h, s * P:(s + 1) * P], mqT[:, h, seen], start=True, stop=True)
                        mm.then_inc(*filled(("ms", l, h, d, s)))
                        yield

                def ml_out(i):
                    h, d = pairs[i]
                    pe.wait_ge(*ml_w_ready.at((l, h, d)))
                    for g in range(len(q_tts) // 2):
                        ps = take(pe, ("mh", l, h, d, g), "acc")
                        for j in range(2):
                            t = q_tts[2 * g + j]
                            keys = [s for s in range(4) if ml_allowed(d, s, t)]
                            for s in keys:
                                mm = pe.matmul(ps[:, j * (P + 1):(j + 1) * (P + 1)], ml_w[:, i % 2, s, t * P:(t + 1) * P],
                                               mv[:, s, h, :], start=(s == keys[0]), stop=(s == keys[-1]))
                        mm.then_inc(*filled(("mh", l, h, d, g)))

                def mlstm():
                    for i in range(len(pairs) + 1):
                        if i < len(pairs):
                            yield from ml_scores(i)
                        if i:
                            ml_out(i - 1)
                            yield

                ml = Beside(mlstm(), ML_EVERY)
                gemm_T(("nq", l), qs, hT_hi, hT_lo, beside=ml)
                gemm_T(("nk", l), every, hT_hi, hT_lo, beside=ml)
                gemm_tok(("nv", l), tts, hT_hi, hT_lo, beside=ml)
                ml.finish()

                def merge(b, beside=None):
                    for half in range(2):
                        gemm_T(("zg", l, b, half), qs, hT_hi, hT_lo, beside=beside)
                        if half == 0:
                            if b == 0:
                                turn_mlstm()
                            pe.wait_ge(*yT_ready.at((l, b)))
                        gemm_T(("br", l, b, half), qs, yT_hi, yT_lo, tiles=BW // P, beside=beside)

                def turn_mlstm():
                    pe.wait_ge(*ml_y.at(l))
                    for h in range(MH):
                        ps = take(pe, ("my", l, h), "side")
                        for t in q_tts:
                            mm = pe.transpose(ps[:, t * P:(t + 1) * P], ptmp[:, t, h * P:(h + 1) * P], ident)
                        mm.then_inc(*filled(("my", l, h)))

                na = Beside(attention("na", nqT, nkT, nv, nprob), NA_EVERY, NA_SKIP if last else 2 * NA_SKIP)
                merge(0, na)
                merge(1, na)
                na.finish()
                merge(2)
                for c in range(2):
                    gemm_tok(("wo", l, c), q_tts, hT_hi, hT_lo,
                             inputs=None if c else lambda p, l=l: merged_ready.at((l, KP * p + KP - 1)))
                    if c == 0:
                        spread(l, "mix", sets)

                norm_T(l, "ffn", q_tts)
                mods = next_mods(l + 1)
                for c in range(FB // 2):
                    gemm_T(("up", l, c), qs, hT_hi, hT_lo, steps=mods, inputs=None if c else normed(l, "ffn"))
                    if not last and c:
                        mod_turn(l + 1, c - 1)
                if not last:
                    for _ in mods:
                        pass
                    mod_turn(l + 1, MOD_CHUNKS - 2)
                    mod_turn(l + 1, MOD_CHUNKS - 1)
                for c in range(2):
                    gemm_tok(("down", l, c), q_tts, fT_hi, fT_lo, tiles=FB,
                             inputs=None if c else lambda p, l=l: fT_ready.at((l, p)))
                    if c == 0:
                        spread(l, "ffn", sets)

        hi_done = [0]

        @block.scalar
        def _(act):
            a = nc.scalar

            def split_hi(upto):
                while hi_done[0] < min(upto, NPIECES):
                    p = hi_done[0]
                    act.wait_ge(raw_loaded[p % RING], 16 * (p // RING + 1))
                    if p >= RING:
                        act.wait_ge(piece_used, p - RING + 1)
                    a.activation(w_hi[:, p % RING].rearrange("p k n -> p (k n)"), w_raw[:, p % RING, :],
                                 ACT.Copy).then_inc(hi_ready, 1)
                    hi_done[0] += 1

            def ahead(key):
                split_hi(plan.get(("filled", key), (0, 0, 0, 0))[3] + RING - 1)

            def mod_rows(l, c):
                ahead(("mod", l, c))
                act.wait_ge(*filled_at(("mod", l, c)))
                if c >= 2:
                    act.wait_ge(*filled_at(("modT", l, c - 2)))
                a.activation(mrow[0:4, c % 2, :], psum(("mod", l, c))[0:4, :], ACT.Copy).then_inc(*A.drain(("mod", l, c)))

            act.dma_start(resid[1][:], x_in).then_inc(x_loaded, 16)
            act.wait_ge(x_loaded, 16)
            for t in range(NT):
                a.activation(xn1[:, t, :], resid[1][:, t, :], ACT.Square, accum_out=ss[:, t:t + 1]).then_inc(*A.next())
            act.wait_ge(*A.last())
            a.activation(ss[:, 2:4], ss[:, 0:2], ACT.Copy, scale=1.0 / D, bias=EPS).then_inc(*A.next())
            act.wait_ge(*A.last())
            a.activation(rs[:, 0:2], ss[:, 2:4], ACT.Sqrt).then_inc(*A.tell(root_ready, "b1"))
            act.wait_ge(small_loaded, 96)
            a.activation(mod_c[:, :, 0], V("c", 0, KD), ACT.Silu).then_inc(*A.tell(mod_c_ready, 0))
            a.activation(mod_c[:, :, 1], V("c_ctx", 0, KD), ACT.Silu).then_inc(*A.tell(mod_c_ready, 1))
            act.wait_ge(*A.last())
            a.activation(mod_cols_of(0), mod_c[:], ACT.Copy).then_inc(*A.tell(mod_hi_ready, 0))
            a.activation(lam[:, 0, :], V("lambda", 0, HEADS), ACT.Abs).then_inc(*A.next())
            act.wait_ge(*A.last())
            a.activation(lam[:, 1, :], lam[:, 0, :], ACT.Exp, scale=-1.0).then_inc(*A.next())
            act.wait_ge(*A.last())
            a.activation(lam[:, 2, :], lam[:, 1, :], ACT.Ln, bias=1.0).then_inc(*A.tell(lam_ready, 0))
            for g in range(KD // 2):
                ahead(("xT", g))
                act.wait_ge(*filled_at(("xT", g)))
                ps = psum(("xT", g))
                for j in range(2):
                    k = 2 * g + j
                    a.activation(xt_tmp[:, k, :], ps[:, j * T:(j + 1) * T], ACT.Copy, scale=V("norm_in_g", k))\
                        .then_inc(*(A.drain(("xT", g)) if j else A.next()))
                act.wait_ge(*A.last())
                a.activation(xT_hi[:, 2 * g:2 * g + 2, :], xt_tmp[:, 2 * g:2 * g + 2, :], ACT.Copy)\
                    .then_inc(*A.tell(xT_hi_ready, g))
            for c in range(12):
                for g in range(2):
                    key = (("in", c), g)
                    if c < 2:
                        ahead(key)
                        act.wait_ge(*filled_at(key))
                        b = 4 * c + 2 * g
                        a.activation(xlT[:, b:b + 2, 3:T + 3], psum(key)[:].rearrange("p (b t) -> p b t", b=2), ACT.Copy)\
                            .then_inc(*A.drain(key))
                    elif c < 4:
                        ahead(key)
                        act.wait_ge(*filled_at(key))
                        b = 4 * (c - 2) + 2 * g
                        a.activation(glT[:, b:b + 2, :], psum(key)[:].rearrange("p (b t) -> p b t", b=2), ACT.Silu)\
                            .then_inc(*A.drain(key))
                    elif c >= 8:
                        ahead(key)
                        act.wait_ge(*filled_at(key))
                        dst = v1 if c < 10 else sg
                        a.activation(dst[:, g, (c % 2) * COLS:(c % 2 + 1) * COLS], psum(key)[:],
                                     ACT.Copy if c < 10 else ACT.Silu).then_inc(*A.drain(key))
                if c % (12 // MODS_IN) == 12 // MODS_IN - 1:
                    mod_rows(0, c // (12 // MODS_IN))
                if 4 <= c < 8:
                    for n in (2 * (c - 4), 2 * (c - 4) + 1):
                        key = ("gate", n)
                        ahead(key)
                        act.wait_ge(*filled_at(key))
                        a.activation(lru_r[:, n, :], psum(key)[:, 0:T], ACT.Sigmoid, bias=V("gate_a_b", n))\
                            .then_inc(*A.next())
                        a.activation(lru_i[:, n, :], psum(key)[:, T:2 * T], ACT.Sigmoid, bias=V("gate_x_b", n))\
                            .then_inc(*A.drain(key))
            ahead((("in", 11), 1))
            act.wait_ge(*lam_scaled.at(0))
            for n in range(HEADS):
                act.wait_ge(*lru_ix.at(n))
                act.wait_ge(*A.last())
                a.activation(xc[:, n, :], lru_r[:, n, :], ACT.Exp, scale=lam[:, 1, n:n + 1]).then_inc(*A.tell(lru_e2, n))
            act.wait_ge(*A.last())
            for n in range(HEADS):
                a.activation(lru_r[:, n, :], lru_r[:, n, :], ACT.Exp, scale=lam[:, 0, n:n + 1]).then_inc(*A.tell(lru_a, n))
            act.wait_ge(*lru_clamped.at(0))
            a.activation(xc[:], xc[:], ACT.Sqrt, bias=1.0).then_inc(*A.tell(lru_mult, 0))
            for n in range(HEADS):
                act.wait_ge(*lru_gated.at(n))
                a.activation(mix_hi[:, HEADS + n, :], xc[:, n, :], ACT.Copy).then_inc(*A.tell(lru_hi, n))
            for h in range(HEADS + 2):
                for c in mods_beside(h):
                    mod_rows(0, c)
                if h == HEADS:
                    ahead(("ry", HEADS - 1))
                    act.wait_ge(*filled_at(("ry", HEADS - 1)))
                    a.activation(mix_hi[:, HEADS - 1, :], psum(("ry", HEADS - 1))[:, 0:T], ACT.Copy)\
                        .then_inc(*A.tell(ret_hi, HEADS - 1))
                if h >= HEADS:
                    continue
                ahead(("ro", h))
                act.wait_ge(*ret_var.at(h))
                a.activation(bnst[:, h % 2, 6:8], bnst[:, 2 + h % 2, 0:2], ACT.Sqrt).then_inc(*A.tell(ret_root, h))
                if h >= 1:
                    ahead(("ry", h - 1))
                    act.wait_ge(*filled_at(("ry", h - 1)))
                    a.activation(mix_hi[:, h - 1, :], psum(("ry", h - 1))[:, 0:T], ACT.Copy)\
                        .then_inc(*A.tell(ret_hi, h - 1))
            act.dma_start(gout_row[:], gout_in).then_inc(gout_loaded, 16)
            act.dma_start(resid[0][:], ctx_in).then_inc(ctx_loaded, 16)
            ahead((("out", 1), 1))
            for t in range(NT):
                act.wait_ge(*h1_ready.at(t))
                a.activation(v1[:, t, :], resid[1][:, t, :], ACT.Square, accum_out=ss[:, t:t + 1]).then_inc(*A.next())
            act.wait_ge(*A.last())
            a.activation(ss[:, 2:4], ss[:, 0:2], ACT.Copy, scale=1.0 / D, bias=EPS).then_inc(*A.next())
            act.wait_ge(*A.last())
            a.activation(rs[:, 0:2], ss[:, 2:4], ACT.Sqrt).then_inc(*A.tell(root_ready, "b1out"))

            def norm(l, which, tts):
                for t in tts:
                    if (l, which) == (0, "mix") and t < 2:
                        act.wait_ge(ctx_loaded, 16)
                    else:
                        act.wait_ge(*resid_ready.at((l, which, t)))
                    a.activation(xn[:, t, :], resid[t // 2][:, t % 2, :], ACT.Square, accum_out=ss[:, 56 + t:57 + t]).then_inc(*A.next())
                    if t % 2:
                        act.wait_ge(*A.last())
                        a.activation(rs[:, 55 + t:57 + t], ss[:, 55 + t:57 + t], ACT.Sqrt, scale=1.0 / D, bias=eps[:])\
                            .then_inc(*A.tell(root_ready, (l, which, t)))
                for t in tts:
                    if t % 2:
                        act.wait_ge(*recip_ready.at((l, which, t)))
                        a.activation(xn[:, t, :], resid[t // 2][:, t % 2, :], ACT.Copy, scale=ss[:, 4 + t:5 + t])\
                            .then_inc(*A.tell(xn_odd_ready, (l, which, t)))
                t0 = tts[0] * P
                for k in range(KD):
                    ahead(("nT", l, which, k))
                    act.wait_ge(*hT_tmp_ready.at((l, which, k)))
                    a.activation(hT_hi[:, k, t0:TT], ptmp[:, k % 4, t0:TT], ACT.Copy).then_inc(*A.tell(hT_hi_ready, (l, which, k)))

            def output(l, which, w, tts, o, junk, gains):
                for c in range(2):
                    for g, t in enumerate(tts):
                        key = ((w, l, c), g)
                        ahead(key)
                        act.wait_ge(*filled_at(key))
                        if c == 0:
                            if which == "mix" and g == 0:
                                act.wait_ge(*merged_ready.at((l, KD - 1)))
                            a.activation(o[:, t, 0:COLS], psum(key)[:], ACT.Copy).then_inc(*A.next())
                        act.wait_ge(*A.last())
                        a.activation(junk[:, t, :], psum(key)[:], ACT.Square, accum_out=ss[:, 8 + 2 * t + c:9 + 2 * t + c])\
                            .then_inc(*(A.tell(stat_ready, (l, which, t)) if c else A.drain(key)))
                        if c and t % 2:
                            act.wait_ge(*post_ms.at((l, which, t)))
                            a.activation(rs[:, 3 + t:5 + t], ss[:, 23 + t:25 + t], ACT.Sqrt, scale=1.0 / D, bias=eps[:])\
                                .then_inc(*A.tell(post_root, (l, which, t)))
                    if c == 0:
                        if which == "ffn":
                            act.wait_ge(*fT_ready.at((l, FB // 2 - 1)))
                        for s in sorted({t // 2 for t in tts}):
                            for half in range(2):
                                key = ("spread", l, which, s, half)
                                ahead(key)
                                act.wait_ge(*filled_at(key))
                                a.activation(gains[:, s, half * COLS:(half + 1) * COLS], psum(key)[:], ACT.Copy)\
                                    .then_inc(*A.drain(key))
                        A.mark(gain_ready, (l, which))

            for l in range(LAYERS):
                last = l == LAYERS - 1
                tts = list(range(4))
                q_tts = [2, 3] if last else tts
                t0 = q_tts[0] * P
                nq = TT - t0
                norm(l, "mix", tts)

                def slots(keys, evacuate, tiles=KD, beside=None):
                    for p in range(tiles // KP):
                        for g, key in enumerate(keys):
                            if p == tiles // KP - 1:
                                ahead(key)
                                act.wait_ge(*filled_at(key))
                                evacuate(g, key)
                            if beside:
                                beside.slot()

                def evac_T(key, dst, func=ACT.Copy, scale=1.0, nt=None, beside=None):
                    nt = nt or nq
                    per = 512 // nt

                    def evacuate(g, key):
                        a.activation(dst[:, g * per:(g + 1) * per, TT - nt:TT],
                                     psum(key)[:].rearrange("p (b t) -> p b t", b=per), func, scale=scale)\
                            .then_inc(*A.drain(key))
                    slots([(key, g) for g in range(4 // per)], evacuate, beside=beside)

                def evac_tok(key, ts, out_of, func=ACT.Copy, beside=None):
                    def evacuate(g, key):
                        dst, src = out_of(ts[g], psum(key))
                        a.activation(dst, src, func).then_inc(*A.drain(key))
                    slots([(key, g) for g in range(len(ts))], evacuate, beside=beside)

                def attention(kind, q_, prob):
                    units = [(h, t) for h in range(AH) for t in q_tts]
                    n = len(units)

                    def exponential(u):
                        h, t = units[u]
                        nk = TT if t >= 2 else T
                        ahead((kind, "s", l, h, t))
                        if kind == "na" and t == q_tts[0] and 1 <= h <= 4:
                            act.wait_ge(*bias_used.at((l, h - 1)))
                            load_bias(h + 3)
                        if u >= 4:
                            act.wait_ge(*filled_at((kind, "t", l, *units[u - 4])))
                        act.wait_ge(*neg_max.at((kind, l, h, t)))
                        a.activation(prob[:, u % 4, 0:nk], psum((kind, "s", l, h, t))[:, 0:nk], ACT.Exp,
                                     bias=att[:, u % 4, 0:1], accum_out=att[:, u % 4, 1:2])\
                            .then_inc(*A.drain((kind, "s", l, h, t)))
                        A.mark(exp_done, (kind, l, h, t))

                    def turned(u):
                        h, t = units[u]
                        if u >= 2:
                            hh, tt_ = units[u - 2]
                            if hh % 2 == 1 and tt_ == q_tts[-1]:
                                act.wait_ge(*filled_at((kind, "o", l, hh // 2)))
                            else:
                                act.wait_ge(*probT_used.at((kind, l, hh, tt_)))
                        nk = TT if t >= 2 else T
                        ahead((kind, "t", l, h, t))
                        act.wait_ge(*filled_at((kind, "t", l, h, t)))
                        a.activation(probT[:, u % 2, 0:nk], psum((kind, "t", l, h, t))[:, 0:nk], ACT.Copy)\
                            .then_inc(*A.drain((kind, "t", l, h, t)))

                    def output(u):
                        h, t = units[u]
                        if h % 2 == 1 and t == q_tts[-1]:
                            key = (kind, "o", l, h // 2)
                            ahead(key)
                            act.wait_ge(*filled_at(key))
                            a.activation(q_[:, h // 2, t0:TT], psum(key)[:, t0:TT], ACT.Copy).then_inc(*A.drain(key))

                    for u in range(n + 3):
                        if u < n:
                            exponential(u)
                        if 2 <= u < n + 2:
                            turned(u - 2)
                        if u >= 4:
                            output(u - 4)
                        yield
                    output(n - 1)

                def load_bias(h):
                    act.dma_start(nbias[:, h % 4, :, :], bias_in[l, h]).then_inc(bias_loaded[h % 4], 16)

                for g in range(2):
                    key = (("kv", l), g)
                    ahead(key)
                    act.wait_ge(*filled_at(key))
                    v_ = psum(key)[:].rearrange("p (t c) -> p t c", t=2)
                    a.activation(ak[:, 2 * g:2 * g + 2, :], v_[:, :, 0:P], ACT.Copy).then_inc(*A.tell(ak_raw, (l, g)))
                    a.activation(av[:, 2 * g:2 * g + 2, :], v_[:, :, P:T], ACT.Copy).then_inc(*A.drain(key))
                key = ("gates", l)
                ahead(key)
                act.wait_ge(*filled_at(key))
                G = GATE_ROWS
                a.activation(rows[0:G, 0, :], psum(key)[0:G, :], ACT.Identity, bias=V(f"i_bias{l}")[0:G])\
                    .then_inc(*A.next())
                a.activation(rows[0:G, 1, :], psum(key)[64:64 + G, :], ACT.Identity, bias=V(f"f_bias{l}")[0:G])\
                    .then_inc(*A.drain(key))
                act.wait_ge(*A.last())
                a.activation(rows[0:G, 2, :], rows[0:G, 1, :], ACT.Abs).then_inc(*A.next())
                act.wait_ge(*A.last())
                a.activation(rows[0:G, 3, :], rows[0:G, 2, :], ACT.Exp, scale=-1.0).then_inc(*A.next())
                act.wait_ge(*A.last())
                a.activation(rows[0:G, 2, :], rows[0:G, 3, :], ACT.Ln, bias=1.0).then_inc(*A.tell(log_ready, l))
                for g, t in enumerate(q_tts):
                    key = (("aq", l), g)
                    ahead(key)
                    act.wait_ge(*filled_at(key))
                    a.activation(aq[:, t, :], psum(key)[:], ACT.Copy).then_inc(*A.drain(key))
                act.wait_ge(*qk_ss.at(l))
                a.activation(rs[:, 8:48], ss[:, 8:48], ACT.Sqrt).then_inc(*A.tell(qk_root, l))
                evac_T(("mq", l), mqT)
                for j in range(4):
                    key = ("gqT", l, j)
                    ahead(key)
                    act.wait_ge(*filled_at(key))
                    a.activation(gqT[:, j, t0:TT], psum(key)[:, t0:TT], ACT.Copy).then_inc(*A.drain(key))
                for j in range(2):
                    key = ("gkT", l, j)
                    ahead(key)
                    act.wait_ge(*filled_at(key))
                    a.activation(gkT[:, j, :], psum(key)[:], ACT.Copy).then_inc(*A.drain(key))
                ga = Beside(attention("ga", gqT, gprob), GA_EVERY)
                evac_T(("mk", l), mkT, scale=float(P) ** -0.5, nt=TT, beside=ga)
                evac_tok(("mv", l), tts, lambda t, ps: (mv[:, t, :, 0:P], ps[:].rearrange("p (h e) -> p h e", h=MH)),
                         beside=ga)
                evac_tok(("mo", l), q_tts, lambda t, ps: (zo[:, t, :], ps[:]), beside=ga)
                ga.finish()
                act.wait_ge(*A.last())
                a.activation(zo[:, q_tts[0]:, :], zo[:, q_tts[0]:, :], ACT.Sigmoid).then_inc(*A.tell(zo_ready, l))
                act.wait_ge(*acol_ready.at(l))
                a.activation(acol[:, :, 1, :], acol[:, :, 1, :], ACT.Exp).then_inc(*A.tell(floor_ready, l))
                def mlstm():
                    for i in range(2 * MH):
                        h, d = i // 2, i % 2
                        for s in range(4):
                            rng = ml_ranges(d, s, t0 // P)
                            ahead(("ms", l, h, d, s))
                            act.wait_ge(*ml_e.at((l, h, d, s)))
                            for n, (u0, u1) in enumerate(rng):
                                a.activation(ml_w[:, i % 2, s, u0:u1], ml_w[:, i % 2, s, u0:u1], ACT.Exp)\
                                    .then_inc(*(A.tell(ml_exp, (l, h, d, s)) if n == len(rng) - 1 else A.next()))
                            yield
                        if i:
                            yield

                ml = Beside(mlstm(), ML_EVERY)
                evac_T(("nq", l), nqT, scale=float(HD) ** -0.5, beside=ml)
                evac_T(("nk", l), nkT, nt=TT, beside=ml)
                evac_tok(("nv", l), tts, lambda t, ps: (nv[:, t, :], ps[:]), beside=ml)
                ml.finish()
                act.wait_ge(*ml_ss.at(l))
                a.activation(rs[:, 8:24], ss[:, 8:24], ACT.Sqrt).then_inc(*A.tell(ml_root, l))
                for h in range(MH):
                    key = ("my", l, h)
                    ahead(key)
                    act.wait_ge(*filled_at(key))
                    a.activation(yT_hi[:, h, t0:TT], psum(key)[:, t0:TT], ACT.Copy, scale=V(f"g_ml{l}", h))\
                        .then_inc(*A.tell(yT_hi_ready, (l, 0, h)))
                for h in range(4):
                    load_bias(h)

                def merge(b, beside=None):
                    per = 512 // nq
                    for half in range(2):
                        def gate(g, key):
                            if half:
                                act.wait_ge(*gate_used.at((l, b, 0, g)))
                            elif b:
                                act.wait_ge(*gate_used.at((l, b - 1, 1, g)))
                            a.activation(ptmp[:, g * per:(g + 1) * per, t0:TT],
                                         psum(key)[:].rearrange("p (b t) -> p b t", b=per), ACT.Sigmoid)\
                                .then_inc(*A.drain(key))
                        slots([(("zg", l, b, half), g) for g in range(4 // per)], gate, beside=beside)
                        for _ in range(BW // P // KP * (4 // per)):
                            if beside:
                                beside.slot()
                        if half == 1 and b < 2:
                            if b == 1:
                                beside.finish()
                            ahead((("br", l, b, 1), 4 // per - 1))
                            act.wait_ge(*filled_at((("br", l, b, 1), 4 // per - 1)))
                            act.wait_ge(*A.last())
                            for j in range(4):
                                a.activation(yT_hi[:, j, t0:TT], (gqT, nqT)[b][:, j, t0:TT], ACT.Copy)\
                                    .then_inc(*A.tell(yT_hi_ready, (l, b + 1, j)))

                na = Beside(attention("na", nqT, nprob), NA_EVERY, NA_SKIP if last else 2 * NA_SKIP)
                merge(0, na)
                merge(1, na)
                merge(2)
                for k in range(KD):
                    ahead((("br", l, 2, 1), 4 // (512 // nq) - 1))
                    act.wait_ge(*merged_sum.at((l, k // 4)))
                    a.activation(hT_hi[:, k, t0:TT], merged[:, k, t0:TT], ACT.Copy).then_inc(*A.tell(merged_hi, (l, k)))
                output(l, "mix", "wo", q_tts, o_mix, junk_mix, gain_mix)
                norm(l, "ffn", q_tts)
                per = 512 // nq
                for c in range(FB // 2):
                    for g in range(4 // per):
                        key = (("up", l, c), g)
                        ahead(key)
                        act.wait_ge(*filled_at(key))
                        if c and g == 0:
                            act.wait_ge(*fT_ready.at((l, c - 1)))
                        for j in range(per):
                            q = g * per + j
                            blk = 2 * c + q % 2 + (FB if q >= 2 else 0)
                            a.activation(conv[:, q, t0:TT], psum(key)[:, j * nq:(j + 1) * nq], ACT.Identity,
                                         scale=V(f"ffn_w{l}", 2 * FB + blk), bias=V(f"ffn_b{l}", blk))\
                                .then_inc(*(A.tell(conv_mid, (l, c, g)) if j == per - 1 else A.next()))
                    if not last:
                        mod_rows(l + 1, c)
                        if c == FB // 2 - 1:
                            mod_rows(l + 1, MOD_CHUNKS - 1)
                    act.wait_ge(*conv_done.at((l, c)))
                    a.activation(conv[:, 2:4, t0:TT], conv[:, 2:4, t0:TT], ACT.Silu).then_inc(*A.tell(ffn_silu, (l, c)))
                    act.wait_ge(*ffn_prod.at((l, c)))
                    a.activation(fT_hi[:, 2 * c:2 * c + 2, t0:TT], conv[:, 0:2, t0:TT], ACT.Copy)\
                        .then_inc(*A.tell(fT_hi_ready, (l, c)))
                output(l, "ffn", "down", q_tts, o_ffn, junk_ffn, gain_ffn)
            for t in range(2, 4):
                act.wait_ge(*resid_ready.at((LAYERS, "mix", t)))
            act.dma_start(out, resid[1][:]).then_inc(out_stored, 16)
            act.wait_ge(out_stored, 16)

        @block.vector
        def _(dve):
            v = nc.vector

            v.memset(ones[:], 1.0).then_inc(*W.next())
            v.memset(zero[:], 0.0).then_inc(*W.next())
            v.memset(eps[:], EPS).then_inc(*W.next())
            v.memset(mod_st[:, 4 * KD:].bitcast(F32), 0.0).then_inc(*W.next())
            v.memset(xlT[:, :, 0:3], 0.0).then_inc(*W.next())
            dve.wait_ge(*root_ready.at("b1"))
            v.reciprocal(rs[:, 2:4], rs[:, 0:2]).then_inc(*W.next())
            dve.wait_ge(*W.last())
            for t in range(NT):
                v.tensor_scalar(xn1[:, t, :], resid[1][:, t, :], rs[:, 2 + t:3 + t], None, ALU.mult)\
                    .then_inc(*W.tell(xn_ready, ("b1", t)))
            dve.wait_ge(*mod_hi_ready.at(0))
            v.tensor_tensor(mod_cols_of(2), mod_c[:], mod_cols_of(0).bitcast(F32), ALU.subtract)\
                .then_inc(*W.tell(mod_st_ready, 0))
            dve.wait_ge(*lam_ready.at(0))
            v.tensor_scalar(lam[:, 3, :], V("lambda", 0, HEADS), -1.0, 0.0, ALU.mult, ALU.max).then_inc(*W.next())
            dve.wait_ge(*W.last())
            v.tensor_tensor(lam[:, 2, :], lam[:, 2, :], lam[:, 3, :], ALU.add).then_inc(*W.next())
            dve.wait_ge(*W.last())
            v.tensor_scalar(lam[:, 0, :], lam[:, 2, :], -8.0, None, ALU.mult).then_inc(*W.next())
            v.tensor_scalar(lam[:, 1, :], lam[:, 2, :], -16.0, None, ALU.mult).then_inc(*W.tell(lam_scaled, 0))
            for g in range(KD // 2):
                dve.wait_ge(*xT_hi_ready.at(g))
                v.tensor_tensor(xT_lo[:, 2 * g:2 * g + 2, :], xt_tmp[:, 2 * g:2 * g + 2, :],
                                xT_hi[:, 2 * g:2 * g + 2, :].bitcast(F32), ALU.subtract).then_inc(*W.tell(xT_ready, g))

            def mod_cols(l, c):
                key = ("modT", l, c)
                dve.wait_ge(*filled_at(key))
                b = V(f"b_mod{l}", 4 * c, 4).unsqueeze(2).to_broadcast([P, 4, 2])
                v.tensor_tensor(modT[:, l, 4 * c:4 * c + 4, :], psum(key)[:, 0:8].rearrange("p (j s) -> p j s", s=2), b,
                                ALU.add).then_inc(*W.drain(key))

            def rotate(key, dst, b, rotated, tk):
                dve.wait_ge(*filled_at(key))
                ps = psum(key)[:].rearrange("p (b t) -> p b t", b=2)
                for half in (slice(0, HD), slice(HD, P)):
                    src = slice(HD, P) if half.start == 0 else slice(0, HD)
                    v.tensor_tensor(rot_tmp[half, :, :], ps[src, :, :], rot[src, 1, :].unsqueeze(1).to_broadcast([HD, 2, T]), ALU.mult)\
                        .then_inc(*W.next())
                v.tensor_tensor(dst[:, b:b + 2, :], ps, rot[:, 0, :].unsqueeze(1).to_broadcast([P, 2, T]), ALU.mult)\
                    .then_inc(*W.drain(key))
                dve.wait_ge(*W.last())
                v.tensor_tensor(dst[:, b:b + 2, :], dst[:, b:b + 2, :], rot_tmp[:], ALU.add).then_inc(*W.tell(rotated, tk))
                dve.wait_ge(*W.last())

            def conv_block(n):
                dve.wait_ge(*drained_at((("in", n // 4), n % 4 // 2)))
                v.tensor_scalar(xc[:, n, :], xlT[:, n, 0:T], V("conv_w", n), V("conv_b", n), ALU.mult, ALU.add)\
                    .then_inc(*W.next())
                for j in range(1, 4):
                    dve.wait_ge(*W.last())
                    v.scalar_tensor_tensor(xc[:, n, :], xlT[:, n, j:j + T], V("conv_w", 8 * j + n), xc[:, n, :],
                                           ALU.mult, ALU.add).then_inc(*(W.tell(conv_ready, n) if j == 3 else W.next()))

            for c in range(12):
                if c in (1, 2):
                    for n in range(4 * (c - 1), 4 * c):
                        conv_block(n)
                if 4 <= c < 8:
                    for g in range(2):
                        i = (c - 4) * 2 + g
                        if c < 6:
                            rotate((("in", c), g), qT, 2 * i, q_ready, i)
                        else:
                            rotate((("in", c), g), kT, 2 * (i - 4), k_ready, i - 4)
                if c % (12 // MODS_IN) == 0 and c:
                    mod_cols(0, c // (12 // MODS_IN) - 1)
                if 4 <= c < 8:
                    for n in (2 * (c - 4), 2 * (c - 4) + 1):
                        dve.wait_ge(*drained_at(("gate", n)))
                        v.tensor_tensor(lru_i[:, n, :], lru_i[:, n, :], xc[:, n, :], ALU.mult).then_inc(*W.tell(lru_ix, n))
            dve.wait_ge(*lru_e2.at(HEADS - 1))
            v.tensor_scalar(xc[:], xc[:], 1.0, -1.0, ALU.min, ALU.mult).then_inc(*W.tell(lru_clamped, 0))
            dve.wait_ge(*lru_a.at(HEADS - 1))
            dve.wait_ge(*lru_mult.at(0))
            v.tensor_tensor(lru_i[:], lru_i[:], xc[:], ALU.mult).then_inc(*W.next())
            dve.wait_ge(*W.last())
            for n in range(HEADS):
                v.tensor_tensor_scan(xc[:, n, :], lru_r[:, n, :], lru_i[:, n, :], 0.0, ALU.mult, ALU.add)\
                    .then_inc(*W.next())
            dve.wait_ge(*W.last())
            for n in range(HEADS):
                v.tensor_tensor(xc[:, n, :], xc[:, n, :], glT[:, n, :], ALU.mult).then_inc(*W.tell(lru_gated, n))
            for n in range(HEADS):
                dve.wait_ge(*lru_hi.at(n))
                v.tensor_tensor(mix_lo[:, HEADS + n, :], xc[:, n, :], mix_hi[:, HEADS + n, :].bitcast(F32), ALU.subtract)\
                    .then_inc(*W.tell(lru_y, n))

            def ret_decay(h):
                key = ("rs", h)
                dve.wait_ge(*filled_at(key))
                ps = psum(key)
                if h >= 2:
                    dve.wait_ge(*filled_at(("ro", h - 2)))
                v.tensor_tensor(sT[:, h % 2, 0:T], ps[:, 0:T], decay[:, h, :], ALU.mult).then_inc(*W.next())
                v.tensor_tensor(sT[:, h % 2, T:T + P], ps[:, T:T + P], decay[:, h, 0:P], ALU.mult).then_inc(*W.drain(key))

            def ret_stats(h):
                key = ("ro", h)
                dve.wait_ge(*filled_at(key))
                ps = psum(key)
                for t in range(NT):
                    v.bn_stats(bnst[:, t, 0:6], ps[:, t * P:(t + 1) * P]).then_inc(*W.next())
                    dve.wait_ge(*W.last())
                    v.bn_aggr(att[:, 2 * (h % 2) + t, 0:2], bnst[:, t, 0:6]).then_inc(*W.next())
                dve.wait_ge(*W.last())
                return key

            def ret_norm(h):
                key = ret_stats(h)
                ps = psum(key)
                mu = att[:, 2 * (h % 2):2 * (h % 2) + 2, 0]
                v.tensor_scalar(bnst[:, 2 + h % 2, 0:2], att[:, 2 * (h % 2):2 * (h % 2) + 2, 1], EPS, None, ALU.add)\
                    .then_inc(*W.tell(ret_var, h))
                dve.wait_ge(*ret_root.at(h))
                v.reciprocal(bnst[:, 2 + h % 2, 2:4], bnst[:, h % 2, 6:8]).then_inc(*W.next())
                dve.wait_ge(*W.last())
                if h >= 2:
                    dve.wait_ge(*filled_at(("ry", h - 2)))
                for t in range(NT):
                    v.tensor_scalar(onrm[:, h % 2, t * P:(t + 1) * P], ps[:, t * P:(t + 1) * P], mu[:, t:t + 1],
                                    bnst[:, 2 + h % 2, 2 + t:3 + t], ALU.subtract, ALU.mult)\
                        .then_inc(*(W.drain(key) if t == NT - 1 else W.next()))
                dve.wait_ge(*W.last())
                o = onrm[:, h % 2, :].rearrange("p (t c) -> p t c", t=NT)
                v.tensor_tensor(o, o, sg[:, :, h * P:(h + 1) * P], ALU.mult).then_inc(*W.tell(ret_y, h))

            def ret_lo(h):
                dve.wait_ge(*ret_hi.at(h))
                v.tensor_tensor(mix_lo[:, h, :], psum(("ry", h))[:, 0:T], mix_hi[:, h, :].bitcast(F32), ALU.subtract)\
                    .then_inc(*W.drain(("ry", h)))

            for c in (10, 11):
                for g in range(2):
                    dve.wait_ge(*drained_at((("in", c), g)))
            ret_decay(0)
            for h in range(HEADS):
                for c in mods_beside(h):
                    mod_cols(0, c - 1)
                if h + 1 < HEADS:
                    ret_decay(h + 1)
                ret_norm(h)
                if h >= 1:
                    ret_lo(h - 1)
            ret_lo(HEADS - 1)
            for h in range(HEADS, HEADS + 2):
                for c in mods_beside(h):
                    mod_cols(0, c - 1)
            mod_cols(0, MOD_CHUNKS - 1)
            for c in range(2):
                for t in range(NT):
                    key = (("out", c), t)
                    dve.wait_ge(*filled_at(key))
                    r = resid[1][:, t, c * COLS:(c + 1) * COLS]
                    v.tensor_tensor(r, psum(key)[:], r, ALU.add).then_inc(*W.drain(key))
            dve.wait_ge(*W.last())
            for t in range(NT):
                W.mark(h1_ready, t)
            dve.wait_ge(*root_ready.at("b1out"))
            v.reciprocal(rs[:, 2:4], rs[:, 0:2]).then_inc(*W.next())
            dve.wait_ge(*W.last())
            dve.wait_ge(gout_loaded, 16)
            dve.wait_ge(ctx_loaded, 16)
            for t in range(NT):
                v.scalar_tensor_tensor(resid[1][:, t, :], resid[1][:, t, :], rs[:, 2 + t:3 + t], gout_row[:],
                                       ALU.mult, ALU.mult).then_inc(*W.tell(resid_ready, (0, "mix", 2 + t)))

            def norm(l, which, tts):
                o = 0 if which == "mix" else 3
                pre = V(f"g_pre_{which}{l}", 0, KD)
                dve.wait_ge(*W.last())
                v.tensor_scalar(scol[:], modT[:, l, 8 * (o + 1):8 * (o + 2), :], 1.0, None, ALU.add).then_inc(*W.next())
                dve.wait_ge(*W.last())
                v.tensor_tensor(scol[:], scol[:], pre.unsqueeze(2).to_broadcast([P, KD, 2]), ALU.mult).then_inc(*W.next())
                g_post = V(f"g_post_{which}{l}", 0, KD)
                v.tensor_tensor(gcol[:], modT[:, l, 8 * (o + 2):8 * (o + 3), :], g_post.unsqueeze(2).to_broadcast([P, KD, 2]),
                                ALU.mult).then_inc(*W.tell(gcol_ready, (l, which)))
                for t in tts[1::2]:
                    dve.wait_ge(*root_ready.at((l, which, t)))
                    v.reciprocal(ss[:, 3 + t:5 + t], rs[:, 55 + t:57 + t]).then_inc(*W.tell(recip_ready, (l, which, t)))
                    dve.wait_ge(*W.last())
                    v.tensor_scalar(xn[:, t - 1, :], resid[t // 2][:, 0, :], ss[:, 3 + t:4 + t], None, ALU.mult)\
                        .then_inc(*W.tell(xn_ready, (l, which, t - 1)))
                t0 = tts[0] * P
                for k in range(KD):
                    key = ("nT", l, which, k)
                    dve.wait_ge(*filled_at(key))
                    if k >= 4:
                        dve.wait_ge(*hT_hi_ready.at((l, which, k - 4)))
                    parts = [(1, T, TT)] if t0 else [(0, 0, T), (1, T, TT)]
                    for n, (s, u0, u1) in enumerate(parts):
                        v.tensor_scalar(ptmp[:, k % 4, u0:u1], psum(key)[:, u0:u1], scol[:, k, 1 - s:2 - s],
                                        modT[:, l, 8 * o + k, 1 - s:2 - s], ALU.mult, ALU.add)\
                            .then_inc(*(W.drain(key) if n == len(parts) - 1 else W.next()))
                    W.mark(hT_tmp_ready, (l, which, k))
                    if k:
                        norm_lo(l, which, k - 1, t0)
                norm_lo(l, which, KD - 1, t0)

            def norm_lo(l, which, k, t0):
                dve.wait_ge(*hT_hi_ready.at((l, which, k)))
                v.tensor_tensor(hT_lo[:, k, t0:TT], ptmp[:, k % 4, t0:TT], hT_hi[:, k, t0:TT].bitcast(F32), ALU.subtract)\
                    .then_inc(*W.tell(hT_ready, (l, which, k)))

            def post(l, which, w, tts, o, gains, nxt):
                dve.wait_ge(*gain_ready.at((l, which)))
                for g, t in enumerate(tts):
                    dve.wait_ge(*drained_at(((w, l, 0), g)))
                    v.tensor_tensor(o[:, t, 0:COLS], o[:, t, 0:COLS], gains[:, t // 2, 0:COLS], ALU.mult).then_inc(*W.next())
                for g, t in enumerate(tts):
                    key = ((w, l, 1), g)
                    dve.wait_ge(*stat_ready.at((l, which, t)))
                    v.tensor_tensor(o[:, t, COLS:D], psum(key)[:], gains[:, t // 2, COLS:D], ALU.mult).then_inc(*W.drain(key))
                    if t % 2 == 0:
                        continue
                    sums = ss[:, 6 + 2 * t:10 + 2 * t].rearrange("p (t h) -> p t h", h=2)
                    v.tensor_tensor(ss[:, 23 + t:25 + t], sums[:, :, 0], sums[:, :, 1], ALU.add)\
                        .then_inc(*W.tell(post_ms, (l, which, t)))
                    dve.wait_ge(*post_root.at((l, which, t)))
                    v.reciprocal(ss[:, 27 + t:29 + t], rs[:, 3 + t:5 + t]).then_inc(*W.next())
                    dve.wait_ge(*W.last())
                    for j in range(NT):
                        r = resid[t // 2][:, j, :]
                        v.scalar_tensor_tensor(r, o[:, t - 1 + j, :], ss[:, 27 + t + j:28 + t + j], r, ALU.mult, ALU.add)\
                            .then_inc(*W.tell(resid_ready, (*nxt, t - 1 + j)))

            for l in range(LAYERS):
                last = l == LAYERS - 1
                tts = list(range(4))
                q_tts = [2, 3] if last else tts
                t0 = q_tts[0] * P
                nq = TT - t0
                sets = [1] if last else [0, 1]
                G = GATE_ROWS
                norm(l, "mix", tts)

                sq = probT[:, 0, :]
                if last:
                    v.memset(ss[:, 8:24], 1.0).then_inc(*W.next())
                for g, t in enumerate(q_tts):
                    dve.wait_ge(*drained_at((("aq", l), g)))
                    dve.wait_ge(*W.last())
                    v.tensor_tensor(sq, aq[:, t, :], aq[:, t, :], ALU.mult).then_inc(*W.next())
                    dve.wait_ge(*W.last())
                    v.tensor_reduce(ss[:, 8 + 8 * t:16 + 8 * t], sq.rearrange("p (h d) -> p h d", h=AH), AX.X, ALU.add)\
                        .then_inc(*W.next())
                sq = probT[:, 1, :]
                dve.wait_ge(*ak_raw.at((l, 1)))
                v.tensor_tensor(sq, ak[:].rearrange("p t c -> p (t c)"), ak[:].rearrange("p t c -> p (t c)"), ALU.mult)\
                    .then_inc(*W.next())
                dve.wait_ge(*W.last())
                v.tensor_reduce(ss[:, 40:48], sq.rearrange("p (h d) -> p h d", h=AH), AX.X, ALU.add).then_inc(*W.next())
                dve.wait_ge(*W.last())
                v.tensor_scalar(ss[:, 8:48], ss[:, 8:48], 1.0 / HD, EPS, ALU.mult, ALU.add).then_inc(*W.tell(qk_ss, l))
                dve.wait_ge(*qk_root.at(l))
                v.reciprocal(ss[:, 8:48], rs[:, 8:48]).then_inc(*W.next())
                dve.wait_ge(*W.last())
                v.tensor_scalar(ss[:, 8:40], ss[:, 8:40], float(HD) ** -0.5, None, ALU.mult).then_inc(*W.next())
                dve.wait_ge(*W.last())

                def heads(a_, n, ts, col, which):
                    t1 = ts[-1] + 1
                    heads_of = a_[:, ts[0]:t1, :].rearrange("p t (h d) -> p (t h) d", h=n)
                    m = n * len(ts)
                    v.tensor_tensor(heads_of, heads_of,
                                    ss[:, col + n * ts[0]:col + n * t1].unsqueeze(2).to_broadcast([P, m, HD]), ALU.mult)\
                        .then_inc(*W.next())
                    dve.wait_ge(*W.last())
                    v.tensor_tensor(heads_of, heads_of, rowg[:, l, which, :].unsqueeze(1).to_broadcast([P, m, HD]), ALU.mult)\
                        .then_inc(*W.next())
                    dve.wait_ge(*W.last())
                    for t in (2, 3):
                        s_ = tab[:, TAT["rope_sin"] + (t - 2) * HD:TAT["rope_sin"] + (t - 1) * HD]
                        q5 = a_[:, t, :].rearrange("p (h a b i) -> p h a b i", h=n, a=2, b=2)
                        t5 = probT[:, t - 2, 0:n * HD].rearrange("p (h a b i) -> p h a b i", h=n, a=2, b=2)
                        s5 = s_.rearrange("p (a b i) -> p a b i", a=2, b=2)
                        for b in range(2):
                            v.tensor_tensor(t5[:, :, :, b, :], q5[:, :, :, 1 - b, :],
                                            s5[:, :, b, :].unsqueeze(1).to_broadcast([P, n, 2, 16]), ALU.mult)\
                                .then_inc(*W.next())
                    dve.wait_ge(*W.last())
                    image = a_[:, 2:4, :].rearrange("p t (h d) -> p t h d", h=n)
                    cos = tab[:, TAT["rope_cos"]:TAT["rope_cos"] + 2 * HD].rearrange("p (t d) -> p t d", t=2)
                    v.tensor_tensor(image, image, cos.unsqueeze(2).to_broadcast([P, 2, n, HD]), ALU.mult).then_inc(*W.next())
                    dve.wait_ge(*W.last())
                    v.tensor_tensor(a_[:, 2:4, :], a_[:, 2:4, :], probT[:, 0:2, 0:n * HD], ALU.add).then_inc(*W.next())
                    dve.wait_ge(*W.last())

                def load_bias(h):
                    s = h % 4
                    dve.wait_ge(bias_loaded[s], 16 * (2 * l + h // 4 + 1))
                    b_ = nbias[:, s, :, :]
                    v.tensor_tensor(b_, b_, tab[:, TAT["window"]:TAT["window"] + GRID].unsqueeze(1).to_broadcast([P, 6, GRID]),
                                    ALU.add).then_inc(*W.next())

                def attention(kind, prob):
                    units = [(h, t) for h in range(AH) for t in q_tts]
                    n_ = len(units)
                    if kind == "na":
                        for h in range(AH // 2):
                            load_bias(h)
                        dve.wait_ge(*W.last())

                    def maxes(u):
                        h, t = units[u]
                        nk = TT if t >= 2 else T
                        key = (kind, "s", l, h, t)
                        ps = psum(key)
                        dve.wait_ge(*filled_at(key))
                        if kind == "na" and t >= 2:
                            if h >= 4 and t == 2:
                                load_bias(h)
                                dve.wait_ge(*W.last())
                            j0 = 2 if t == 2 else 0
                            sc = ps[:, T:TT].rearrange("p (r c) -> p r c", c=GRID)
                            v.tensor_tensor(sc, sc, nbias[:, h % 4, j0:j0 + 4, :], ALU.add)\
                                .then_inc(*(W.tell(bias_used, (l, h)) if t == 3 else W.next()))
                            dve.wait_ge(*W.last())
                        v.tensor_reduce(att[:, u % 4, 0:1], ps[:, 0:nk], AX.X, ALU.max, negate=True)\
                            .then_inc(*W.tell(neg_max, (kind, l, h, t)))

                    def normalise(u):
                        h, t = units[u]
                        nk = TT if t >= 2 else T
                        dve.wait_ge(*exp_done.at((kind, l, h, t)))
                        v.reciprocal(att[:, u % 4, 3:4], att[:, u % 4, 1:2]).then_inc(*W.next())
                        dve.wait_ge(*W.last())
                        v.tensor_scalar(prob[:, u % 4, 0:nk], prob[:, u % 4, 0:nk], att[:, u % 4, 3:4], None, ALU.mult)\
                            .then_inc(*W.tell(prob_ready, (kind, l, h, t)))

                    for u in range(n_ + 3):
                        if u < n_:
                            maxes(u)
                        if 1 <= u <= n_:
                            normalise(u - 1)
                        yield

                heads(aq, AH, q_tts, 8, 0)
                for t in q_tts:
                    W.mark(aq_ready, (l, t))
                heads(ak, 2, tts, 40, 1)
                kd = kdup[:].rearrange("p t (h r d) -> p (t h) r d", h=2, r=2)
                src = ak[:].rearrange("p t (h d) -> p (t h) d", h=2)
                v.tensor_copy(kd[:, :, 0, :], src).then_inc(*W.next())
                v.tensor_copy(kd[:, :, 1, :], src).then_inc(*W.next())
                for t in tts:
                    W.mark(ak_ready, (l, t))
                def zeros(p, n):
                    return zero[p, 0:1].to_broadcast([MH, n])

                def gate_rows():
                    dve.wait_ge(*log_ready.at(l))
                    fwd, bwd = slice(0, MH), slice(32, 32 + MH)
                    v.scalar_tensor_tensor(rows[0:G, 2, :], rows[0:G, 1, :], 0.0, rows[0:G, 2, :], ALU.min, ALU.subtract)\
                        .then_inc(*W.next())
                    v.memset(rows[0:G, 3, :], 0.0).then_inc(*W.next())
                    v.memset(rows[0:G, 4, :], 0.0).then_inc(*W.next())
                    yield
                    dve.wait_ge(*W.last())
                    v.tensor_tensor_scan(rows[fwd, 3, :], rows[fwd, 2, :], zeros(fwd, TT), 0.0, ALU.add, ALU.add)\
                        .then_inc(*W.next())
                    v.tensor_tensor_scan(rows[bwd, 3, 0:T][:, ::-1], rows[bwd, 2, 0:T][:, ::-1], zeros(bwd, T), 0.0, ALU.add, ALU.add)\
                        .then_inc(*W.next())
                    yield
                    dve.wait_ge(*W.last())
                    v.tensor_tensor_scan(rows[bwd, 3, T:TT][:, ::-1], rows[bwd, 2, T:TT][:, ::-1], zeros(bwd, T),
                                         rows[bwd, 3, 0:1], ALU.add, ALU.add).then_inc(*W.next())
                    yield
                    dve.wait_ge(*W.last())
                    v.tensor_tensor(rows[0:G, 0, :], rows[0:G, 0, :], rows[0:G, 3, :], ALU.subtract).then_inc(*W.next())
                    yield
                    dve.wait_ge(*W.last())
                    v.tensor_tensor_scan(rows[fwd, 4, :], rows[fwd, 0, :], rows[fwd, 0, :], 0.0, ALU.max, ALU.max)\
                        .then_inc(*W.next())
                    v.tensor_tensor_scan(rows[bwd, 4, 0:T][:, ::-1], rows[bwd, 0, 0:T][:, ::-1], rows[bwd, 0, 0:T][:, ::-1], 0.0,
                                         ALU.max, ALU.max).then_inc(*W.next())
                    yield
                    dve.wait_ge(*W.last())
                    v.tensor_tensor_scan(rows[bwd, 4, T:TT][:, ::-1], rows[bwd, 0, T:TT][:, ::-1], rows[bwd, 0, T:TT][:, ::-1],
                                         rows[bwd, 4, 0:1], ALU.max, ALU.max).then_inc(*W.next())
                    yield
                    dve.wait_ge(*W.last())
                    v.scalar_tensor_tensor(rows[0:G, 3, :], rows[0:G, 3, :], -1.0, rows[0:G, 4, :], ALU.mult, ALU.subtract)\
                        .then_inc(*W.next())
                    yield
                    dve.wait_ge(*W.last())
                    v.tensor_scalar(rows[0:G, 4, :], rows[0:G, 4, :], -1.0, None, ALU.mult).then_inc(*W.tell(rows_ready, l))

                rows_steps = gate_rows()
                for _ in attention("ga", gprob):
                    next(rows_steps, None)
                for _ in rows_steps:
                    pass
                key = ("acol", l)
                dve.wait_ge(*filled_at(key))
                v.tensor_copy(acol[:].rearrange("p t j g -> p (t j g)"), psum(key)[:, 0:8 * G]).then_inc(*W.drain(key))
                W.mark(acol_ready, l)
                v.memset(mv[:, :, :, P:P + 1], 1.0).then_inc(*W.next())

                dve.wait_ge(*floor_ready.at(l))
                dve.wait_ge(*drained_at(("gkT", l, 1)))
                pairs = [(h, d) for h in range(MH) for d in range(2)]

                def ml_exponents(i):
                    h, d = pairs[i]
                    mask = tab[:, TAT["causal"]:TAT["causal"] + P] if d == 0 else tab[:, TAT["anticausal"]:TAT["anticausal"] + P]
                    key = ("mb", l, h, d)
                    dve.wait_ge(*filled_at(key))
                    if i >= 2:
                        hh, dd = pairs[i - 2]
                        dve.wait_ge(*filled_at(("mh", l, hh, dd, len(q_tts) // 2 - 1)))
                    for s in range(4):
                        ac = acol[:, s, 0, 32 * d + h:32 * d + h + 1]
                        ops = []
                        for u0, u1 in ml_ranges(d, s, t0 // P):
                            if u0 <= s * P < u1:
                                ops += [(u0, s * P, 0), (s * P, (s + 1) * P, 1), ((s + 1) * P, u1, 0)]
                            else:
                                ops.append((u0, u1, 0))
                        ops = [o for o in ops if o[1] > o[0]]
                        for n, (u0, u1, masked) in enumerate(ops):
                            fin = n == len(ops) - 1
                            src, dst = psum(key)[:, u0:u1], ml_w[:, i % 2, s, u0:u1]
                            ins = (v.scalar_tensor_tensor(dst, src, ac, mask, ALU.add, ALU.min) if masked
                                   else v.tensor_scalar(dst, src, ac, 0.0, ALU.add, ALU.min))
                            ins.then_inc(*(W.drain(key) if fin and s == 3 else W.next()))
                        W.mark(ml_e, (l, h, d, s))

                def ml_weights(i):
                    h, d = pairs[i]
                    for s in range(4):
                        key = ("ms", l, h, d, s)
                        dve.wait_ge(*filled_at(key))
                        dve.wait_ge(*ml_exp.at((l, h, d, s)))
                        rng = ml_ranges(d, s, t0 // P)
                        for n, (u0, u1) in enumerate(rng):
                            w_ = ml_w[:, i % 2, s, u0:u1]
                            v.tensor_tensor(w_, psum(key)[:, u0:u1], w_, ALU.mult)\
                                .then_inc(*(W.drain(key) if n == len(rng) - 1 else W.next()))
                    W.mark(ml_w_ready, (l, h, d))

                def ml_norm(i):
                    h, d = pairs[i]
                    for g in range(len(q_tts) // 2):
                        key = ("mh", l, h, d, g)
                        dve.wait_ge(*filled_at(key))
                        ps = psum(key)[:, 0:2 * (P + 1)].rearrange("p (t e) -> p t e", t=2)
                        ta = q_tts[2 * g]
                        v.tensor_copy(rs[:, 48:50], ps[:, :, P]).then_inc(*W.next())
                        dve.wait_ge(*W.last())
                        v.scalar_tensor_tensor(rs[:, 52:54], rs[:, 48:50], -1.0, rs[:, 48:50], ALU.mult, ALU.max)\
                            .then_inc(*W.next())
                        dve.wait_ge(*W.last())
                        v.tensor_tensor(rs[:, 52:54], rs[:, 52:54], acol[:, ta:ta + 2, 1, 32 * d + h], ALU.max)\
                            .then_inc(*W.next())
                        dve.wait_ge(*W.last())
                        v.reciprocal(rs[:, 50:52], rs[:, 52:54]).then_inc(*W.next())
                        dve.wait_ge(*W.last())
                        for j in range(2):
                            dst = ptmp[:, ta + j, h * P:(h + 1) * P]
                            if d == 0:
                                v.tensor_scalar(dst, ps[:, j, 0:P], rs[:, 50 + j:51 + j], None, ALU.mult)\
                                    .then_inc(*(W.drain(key) if j == 1 else W.next()))
                            else:
                                v.scalar_tensor_tensor(dst, ps[:, j, 0:P], rs[:, 50 + j:51 + j], dst, ALU.mult, ALU.add)\
                                    .then_inc(*(W.drain(key) if j == 1 else W.next()))
                        dve.wait_ge(*W.last())

                for i in range(len(pairs) + 1):
                    if i < len(pairs):
                        ml_exponents(i)
                        ml_weights(i)
                    if i:
                        ml_norm(i - 1)
                dve.wait_ge(*zo_ready.at(l))
                if last:
                    v.memset(ss[:, 8:16], 1.0).then_inc(*W.next())
                for t in q_tts:
                    for h in range(MH):
                        y = ptmp[:, t, h * P:(h + 1) * P]
                        v.tensor_tensor(ml_w[:, 0, 0, h * P:(h + 1) * P], y, y, ALU.mult).then_inc(*W.next())
                    dve.wait_ge(*W.last())
                    v.tensor_reduce(ss[:, 8 + 4 * t:12 + 4 * t], ml_w[:, 0, 0, :].rearrange("p (h e) -> p h e", h=MH),
                                    AX.X, ALU.add).then_inc(*W.next())
                    dve.wait_ge(*W.last())
                v.tensor_scalar(ss[:, 8:24], ss[:, 8:24], 1.0 / P, EPS, ALU.mult, ALU.add).then_inc(*W.tell(ml_ss, l))
                dve.wait_ge(*ml_root.at(l))
                v.reciprocal(ss[:, 8:24], rs[:, 8:24]).then_inc(*W.next())
                dve.wait_ge(*W.last())
                for t in q_tts:
                    for h in range(MH):
                        y = ptmp[:, t, h * P:(h + 1) * P]
                        v.scalar_tensor_tensor(y, y, ss[:, 8 + 4 * t + h:9 + 4 * t + h], zo[:, t, h * P:(h + 1) * P],
                                               ALU.mult, ALU.mult).then_inc(*W.next())
                W.mark(ml_y, l)
                for h in range(MH):
                    key = ("my", l, h)
                    dve.wait_ge(*yT_hi_ready.at((l, 0, h)))
                    v.scalar_tensor_tensor(yT_lo[:, h, t0:TT], psum(key)[:, t0:TT], V(f"g_ml{l}", h),
                                           yT_hi[:, h, t0:TT].bitcast(F32), ALU.mult, ALU.subtract).then_inc(*W.drain(key))
                W.mark(yT_ready, (l, 0))

                def merge(b, beside=None):
                    per = 512 // nq
                    banks = 4 // per
                    for half in range(2):
                        for _ in range(KD // KP * banks):
                            if beside:
                                beside.slot()
                        for p in range(BW // P // KP):
                            for g in range(banks):
                                if p == BW // P // KP - 1:
                                    branch(b, half, g, per)
                                if beside:
                                    beside.slot()
                        if b == 2:
                            W.mark(merged_sum, (l, half))
                    if b < 2:
                        if b == 1:
                            beside.finish()
                        for j in range(4):
                            dve.wait_ge(*yT_hi_ready.at((l, b + 1, j)))
                            v.tensor_tensor(yT_lo[:, j, t0:TT], (gqT, nqT)[b][:, j, t0:TT], yT_hi[:, j, t0:TT].bitcast(F32),
                                            ALU.subtract).then_inc(*W.next())
                        W.mark(yT_ready, (l, b + 1))

                def branch(b, half, g, per):
                    key = (("br", l, b, half), g)
                    dve.wait_ge(*filled_at(key))
                    dve.wait_ge(*drained_at((("zg", l, b, half), g)))
                    gate = ptmp[:, g * per:(g + 1) * per, t0:TT]
                    ps = psum(key)[:].rearrange("p (b t) -> p b t", b=per)
                    m = merged[:, 4 * half + g * per:4 * half + (g + 1) * per, t0:TT]
                    if b == 0:
                        v.tensor_tensor(m, ps, gate, ALU.mult).then_inc(*W.drain(key))
                        W.mark(gate_used, (l, b, half, g))
                    else:
                        v.tensor_tensor(gate, ps, gate, ALU.mult).then_inc(*W.drain(key))
                        dve.wait_ge(*W.last())
                        v.tensor_tensor(m, m, gate, ALU.add).then_inc(*W.tell(gate_used, (l, b, half, g)))

                na = Beside(attention("na", nprob), NA_EVERY, NA_SKIP if last else 2 * NA_SKIP)
                merge(0, na)
                merge(1, na)
                merge(2)
                for k in range(KD):
                    dve.wait_ge(*merged_hi.at((l, k)))
                    v.tensor_tensor(hT_lo[:, k, t0:TT], merged[:, k, t0:TT], hT_hi[:, k, t0:TT].bitcast(F32), ALU.subtract)\
                        .then_inc(*W.tell(merged_ready, (l, k)))
                post(l, "mix", "wo", q_tts, o_mix, gain_mix, (l, "ffn"))
                norm(l, "ffn", q_tts)
                per = 512 // nq
                for c in range(FB // 2):
                    for g in range(4 // per):
                        key = (("up", l, c), g)
                        dve.wait_ge(*conv_mid.at((l, c, g)))
                        for tap in (0, 2):
                            if tap == 2:
                                dve.wait_ge(*W.last())
                            for j in range(per):
                                q = g * per + j
                                blk = 2 * c + q % 2 + (FB if q >= 2 else 0)
                                ps = psum(key)[:, j * nq:(j + 1) * nq].rearrange("p (s t) -> p s t", t=T)
                                cv = conv[:, q, t0:TT].rearrange("p (s t) -> p s t", t=T)
                                src, dst = (ps[:, :, 0:T - 1], cv[:, :, 1:T]) if tap == 0 else (ps[:, :, 1:T], cv[:, :, 0:T - 1])
                                v.scalar_tensor_tensor(dst, src, V(f"ffn_w{l}", tap * 2 * FB + blk), dst, ALU.mult, ALU.add)\
                                    .then_inc(*(W.drain(key) if tap == 2 and j == per - 1 else W.next()))
                            W.mark(conv_done, (l, c))
                    dve.wait_ge(*ffn_silu.at((l, c)))
                    v.tensor_tensor(conv[:, 0:2, t0:TT], conv[:, 0:2, t0:TT], conv[:, 2:4, t0:TT], ALU.mult)\
                        .then_inc(*W.tell(ffn_prod, (l, c)))
                    if not last and c:
                        mod_cols(l + 1, c - 1)
                    dve.wait_ge(*fT_hi_ready.at((l, c)))
                    v.tensor_tensor(fT_lo[:, 2 * c:2 * c + 2, t0:TT], conv[:, 0:2, t0:TT],
                                    fT_hi[:, 2 * c:2 * c + 2, t0:TT].bitcast(F32), ALU.subtract)\
                        .then_inc(*W.tell(fT_ready, (l, c)))
                if not last:
                    mod_cols(l + 1, MOD_CHUNKS - 2)
                    mod_cols(l + 1, MOD_CHUNKS - 1)
                post(l, "ffn", "down", q_tts, o_ffn, gain_ffn, (l + 1, "mix"))
    es.close()


def pieces_of(w, cols):
    w = np.asarray(w)
    cols = np.asarray(cols)
    block = np.where(cols >= 0, w[:, np.maximum(cols, 0)], np.zeros((), w.dtype))
    return block.reshape(-1, KP, P, COLS).transpose(0, 2, 1, 3).reshape(-1, P, KP * COLS)


def chunk_columns(name, c):
    r = np.arange
    if name == "w_in":
        first = [8, 9, 10, 11, 0, 1, 2, 3, 4, 5, 6, 7][c]
        return r(first * COLS, (first + 1) * COLS)
    if name == "w_in_2":
        mq, mk, mv, mo, mg = 0, BW, 2 * BW, 3 * BW, 4 * BW
        aq = mg + 16
        ak, av = aq + BW, aq + BW + P
        nq = av + P
        zg = nq + 3 * BW
        if c == 0:
            gates = np.full(256, -1)
            for k, at in enumerate((0, 64, 32, 96)):
                gates[at:at + MH] = r(mg + k * MH, mg + (k + 1) * MH)
            return np.concatenate([r(ak, ak + P), r(av, av + P), gates])
        if c < 9:
            first = [None, aq, mq, mk, mv, mo, nq, nq + BW, nq + 2 * BW][c]
            return r(first, first + COLS)
        return r(zg + (c - 9) * COLS, zg + (c - 8) * COLS)
    if name == "w_up":
        a = r(2 * c * P, (2 * c + 2) * P)
        return np.concatenate([a, FF + a])
    return r(c * COLS, (c + 1) * COLS)


def weight_stream(x):
    chunks, out = {}, []
    for name, l, c, k in stream():
        if (name, l, c) not in chunks:
            if name in ("w_in", "w_out"):
                w, at = x[name], c
            elif name == "w_branch":
                w, at = x["w_branch_2"][l][c // 2], c % 2
            else:
                w, at = x[name if name.endswith("_2") else name + "_2"][l], c
            chunks[name, l, c] = pieces_of(w, chunk_columns(name, at))
        out.append(chunks[name, l, c][k // KP])
    return np.stack(out)


def column_vectors(x):
    f = np.float32
    out = np.zeros((P, NV), f)

    def put(name, a):
        a = np.asarray(a)
        n = a.size // P
        out[:, VAT[name]:VAT[name] + n] = a.reshape(n, P).T

    put("norm_in_g", x["norm_in_g"])
    put("conv_w", x["conv_w"])
    put("conv_b", x["conv_b"])
    put("gate_a_b", x["gate_a_b"])
    put("gate_x_b", x["gate_x_b"])
    put("lambda", x["lru_lambda"])
    put("c", x["c_2"])
    put("c_ctx", x["c_ctx_2"])
    for l in range(LAYERS):
        put(f"b_mod{l}", x["b_mod_2"][l])
        for a, b in (("g_pre_mix", "g_pre_mix_2"), ("g_post_mix", "g_post_mix_2"), ("g_pre_ffn", "g_pre_ffn_2"),
                     ("g_post_ffn", "g_post_ffn_2"), ("g_ml", "g_ml_out_2"), ("ffn_w", "conv_w_2"), ("ffn_b", "conv_b_2")):
            put(f"{a}{l}", x[b][l])
        g = np.asarray(x["b_ml_gates_2"][l])
        out[0:MH, VAT[f"i_bias{l}"]], out[32:32 + MH, VAT[f"i_bias{l}"]] = g[0:4], g[8:12]
        out[0:MH, VAT[f"f_bias{l}"]], out[32:32 + MH, VAT[f"f_bias{l}"]] = g[4:8], g[12:16]
    return out


def shape_tables():
    t = np.zeros((P, NTAB), np.float64)
    i = np.arange(P)
    t[:, TAT["ident"]:TAT["ident"] + P] = np.eye(P)
    t[:, TAT["causal"]:TAT["causal"] + P] = np.where(i[:, None] <= i[None, :], 0, NEG)
    t[:, TAT["anticausal"]:TAT["anticausal"] + P] = np.where(i[:, None] >= i[None, :], 0, NEG)
    col = i % GRID
    c0 = np.clip(col - WIN // 2, 0, GRID - WIN)
    k = np.arange(GRID)[None, :]
    t[:, TAT["window"]:TAT["window"] + GRID] = np.where((k >= c0[:, None]) & (k < c0[:, None] + WIN), 0, NEG)
    half = HD // 2
    inv = (10000.0 ** (-np.arange(0, half, 2) / half)).astype(np.float32)
    sign = np.concatenate([-np.ones(16), np.ones(16)] * 2)
    for n in range(NT):
        tok = n * P + i
        r = ((tok // GRID).astype(np.float32)[:, None] * inv).astype(np.float64)
        c = ((tok % GRID).astype(np.float32)[:, None] * inv).astype(np.float64)
        ang = np.concatenate([r, r, c, c], axis=1)
        t[:, TAT["rope_cos"] + n * HD:TAT["rope_cos"] + (n + 1) * HD] = np.cos(ang)
        t[:, TAT["rope_sin"] + n * HD:TAT["rope_sin"] + (n + 1) * HD] = np.sin(ang) * sign
    s = TAT["mod_sel"]
    t[0, s] = t[2, s] = t[1, s + 1] = t[3, s + 1] = 1
    inv = (10000.0 ** (-np.arange(0, P, 2) / P)).astype(np.float32)
    ang = (inv[:, None] * np.arange(T, dtype=np.float32)[None, :]).astype(np.float64)
    rot = np.stack([np.concatenate([np.cos(ang)] * 2), np.concatenate([np.sin(ang), -np.sin(ang)])], axis=1)
    log_g = np.log1p(-np.exp2(-5.0 - np.arange(HEADS)))
    rel = np.arange(T)[None, :] - i[:, None]
    decay = np.where(rel[:, None, :] >= 0, np.exp(np.maximum(rel, 0)[:, None, :] * log_g[None, :, None]), 0) * P ** -0.5
    return t.astype(np.float32), rot.astype(np.float32), decay.astype(np.float32)


def window_bias(rpb):
    rpb = np.asarray(rpb)
    p = np.arange(P)
    dr = 5 - p // GRID
    dr = dr[:, None, None] + np.arange(6)[None, :, None]
    dc = np.arange(GRID)[None, None, :] - (p % GRID)[:, None, None] + WIN - 1
    inside = (dc >= 0) & (dc < 2 * WIN - 1)
    got = rpb[:, :, dr, np.clip(dc, 0, 2 * WIN - 2)]
    return np.where(inside, got, np.zeros((), rpb.dtype))


def kernel(**inputs):
    import concourse.bacc as bacc
    from concourse.bass_utils import run_bass_kernel_spmd

    x = {k: np.asarray(v) for k, v in inputs.items()}
    tab, rot, decay = shape_tables()
    f = np.ascontiguousarray
    rows = np.stack([np.stack([x["g_q_2"][l], x["g_k_2"][l]]) for l in range(LAYERS)])
    arrays = {
        "weights": weight_stream(x),
        "x": f(x["x"].reshape(NT, P, D).transpose(1, 0, 2)),
        "ctx": f(x["ctx_2"].reshape(NT, P, D).transpose(1, 0, 2)),
        "vectors": column_vectors(x),
        "tables": tab,
        "rotary": rot,
        "decay": decay,
        "gate_weights": f(np.stack([x["gate_a_w"], x["gate_x_w"]]).transpose(2, 0, 1, 3)),
        "head_gains": f(np.broadcast_to(rows[None], (P, *rows.shape))),
        "norm_out_rows": f(np.broadcast_to(x["norm_out_g"][None], (P, D))),
        "window_bias": f(window_bias(x["na_rpb_2"])),
    }

    def emit(plan, planning):
        nc = bacc.Bacc("TRN2", target_bir_lowering=False, num_devices=1)
        args = [nc.dram_tensor(f"in_{n}", a.shape, mybir.dt.from_np(a.dtype), kind="ExternalInput").ap()
                for n, a in arrays.items()]
        order = dict(zip(arrays, args))
        out = nc.dram_tensor("out_0", (P, NT, D), F32, kind="ExternalOutput").ap()
        build(nc, order["weights"], order["x"], order["ctx"], order["vectors"], order["tables"], order["rotary"],
              order["decay"], order["gate_weights"], order["head_gains"], order["norm_out_rows"], order["window_bias"],
              out, plan, planning)
        return nc

    plan = {}
    emit(plan, True)
    nc = emit(plan, False)
    r = run_bass_kernel_spmd(nc, [{f"in_{n}": a for n, a in arrays.items()}], core_ids=[0])
    got = r.results[0]["out_0"]
    return np.ascontiguousarray(got.transpose(1, 0, 2)).reshape(1, T, D)
```
